# Optimizing a Trainium2 kernel written in Bass

```python
import jax, jax.numpy as jnp
from jax import lax
import numpy as np
import math

D_MODEL = 1024
BATCH = 1
SEQ = 256
DEPTH = 2

N_EVEN = (DEPTH + 1) // 2
N_ODD = DEPTH // 2

A_WIDTH = D_MODEL // 2
A_HEADS = 4
A_HEAD_DIM = A_WIDTH // A_HEADS
MLSTM_CHUNK = 128
CONV_WIDTH = 5

B_WIDTH = D_MODEL - A_WIDTH
B_GROUPS = 4
B_GROUP_DIM = B_WIDTH // B_GROUPS
SGU_CHUNK = 128

AB_IN = 4 * A_WIDTH + 4 * A_HEADS + 2 * B_WIDTH

C_HEADS = 16
C_NOPE = 64
C_ROPE = 32
C_V = 64
Q_LORA = 384
KV_LORA = 256
C_IN = Q_LORA + KV_LORA + C_ROPE
ROPE_BASE = 10000.0
Q_BLOCK = 128

D_FF = 4 * D_MODEL

EPS = 1e-6


def rms_norm(x, g):
    xf = x.astype(jnp.float32)
    y = xf * lax.rsqrt(jnp.mean(xf * xf, axis=-1, keepdims=True) + EPS)
    return (y * g.astype(jnp.float32)).astype(x.dtype)

def centred_dwconv(x, w):
    pad = (w.shape[0] - 1) // 2
    return lax.conv_general_dilated(
        x, w[:, None, :].astype(x.dtype), window_strides=(1,),
        padding=[(pad, pad)], dimension_numbers=("NWC", "WIO", "NWC"),
        feature_group_count=x.shape[-1])

def mlstm_scan(q, k, v, log_i, log_f):
    bsz, nh, seq, dh = q.shape
    L = MLSTM_CHUNK
    nc = seq // L

    def to_chunks(t):
        return jnp.moveaxis(t.reshape(bsz, nh, nc, L, *t.shape[3:]), 2, 0)

    lower = jnp.tril(jnp.ones((L, L), dtype=bool))

    def step(carry, xs):
        C, n, m = carry
        qc, kc, vc, li, lf = xs
        b = jnp.cumsum(lf, axis=-1)
        dmat = jnp.where(lower, b[..., :, None] - b[..., None, :] + li[..., None, :], -jnp.inf)
        m_t = jnp.maximum(b + m[..., None], jnp.max(dmat, axis=-1))
        inter = jnp.exp(b + m[..., None] - m_t)
        s = jnp.einsum("bhtd,bhsd->bhts", qc, kc) * jnp.exp(dmat - m_t[..., None])
        num = (jnp.einsum("bhts,bhse->bhte", s, vc)
               + inter[..., None] * jnp.einsum("bhtd,bhde->bhte", qc, C))
        den = jnp.sum(s, axis=-1) + inter * jnp.einsum("bhtd,bhd->bht", qc, n)
        h = num / jnp.maximum(jnp.abs(den), jnp.exp(-m_t))[..., None]
        g = b[..., -1]
        w_log = g[..., None] - b + li
        m_new = jnp.maximum(g + m, jnp.max(w_log, axis=-1))
        decay = jnp.exp(g + m - m_new)
        w = jnp.exp(w_log - m_new[..., None])
        C_new = decay[..., None, None] * C + jnp.einsum("bhs,bhsd,bhse->bhde", w, kc, vc)
        n_new = decay[..., None] * n + jnp.einsum("bhs,bhsd->bhd", w, kc)
        return (C_new, n_new, m_new), h

    init = (jnp.zeros((bsz, nh, dh, dh), jnp.float32),
            jnp.zeros((bsz, nh, dh), jnp.float32),
            jnp.zeros((bsz, nh), jnp.float32))
    _, h = lax.scan(step, init, (to_chunks(q), to_chunks(k), to_chunks(v),
                                 to_chunks(log_i), to_chunks(log_f)))
    return jnp.moveaxis(h, 0, 2).reshape(bsz, nh, seq, dh)

def ab_mixer(h, w_in, conv_w, gate_b, head_g, v_g, ws, bs, w_out):
    bsz, seq, _ = h.shape
    p = h @ w_in
    qk, va, oa, gates, uv = jnp.split(
        p, [2 * A_WIDTH, 3 * A_WIDTH, 4 * A_WIDTH, 4 * A_WIDTH + 4 * A_HEADS], axis=-1)

    qk = jax.nn.silu(centred_dwconv(qk, conv_w))

    def heads(t):
        return t.reshape(bsz, seq, A_HEADS, A_HEAD_DIM).transpose(0, 2, 1, 3).astype(jnp.float32)

    q = heads(qk[..., :A_WIDTH]) * (A_HEAD_DIM ** -0.5)
    k = heads(qk[..., A_WIDTH:])
    v = heads(va)
    g = (gates + gate_b).astype(jnp.float32).reshape(bsz, seq, 4, A_HEADS).transpose(2, 0, 3, 1)
    li_f, lf_f = g[0], jax.nn.log_sigmoid(g[1])
    li_b, lf_b = g[2], jax.nn.log_sigmoid(g[3])
    h_fwd = mlstm_scan(q, k, v, li_f, lf_f)
    fl = lambda t: jnp.flip(t, axis=2)
    h_bwd = fl(mlstm_scan(fl(q), fl(k), fl(v), jnp.flip(li_b, -1), jnp.flip(lf_b, -1)))
    ha = rms_norm(h_fwd + h_bwd, head_g.reshape(A_HEADS, 1, A_HEAD_DIM))
    ha = ha.transpose(0, 2, 1, 3).reshape(bsz, seq, A_WIDTH).astype(h.dtype) * jax.nn.sigmoid(oa)

    u, vb = jnp.split(jax.nn.gelu(uv), 2, axis=-1)
    vb = rms_norm(vb.reshape(bsz, seq, B_GROUPS, B_GROUP_DIM), v_g.reshape(B_GROUPS, B_GROUP_DIM))
    vb = vb.reshape(bsz, seq // SGU_CHUNK, SGU_CHUNK, B_GROUPS, B_GROUP_DIM)
    sp = jnp.einsum("gts,bnsgc->bntgc", ws, vb) + bs.T[:, :, None]
    hb = u * sp.reshape(bsz, seq, B_WIDTH)

    return jnp.concatenate([ha, hb], axis=-1) @ w_out

def apply_rope(x, cos, sin):
    half = x.shape[-1] // 2
    x1, x2 = x[..., :half], x[..., half:]
    return jnp.concatenate([x1 * cos - x2 * sin, x1 * sin + x2 * cos], axis=-1).astype(x.dtype)

def mla_mixer(h, positions, w_in, q_g, kv_g, w_uq, w_ukv, w_out):
    bsz, seq, _ = h.shape
    cq, ckv, kr = jnp.split(h @ w_in, [Q_LORA, Q_LORA + KV_LORA], axis=-1)
    q = (rms_norm(cq, q_g) @ w_uq).reshape(bsz, seq, C_HEADS, C_NOPE + C_ROPE)
    kv = (rms_norm(ckv, kv_g) @ w_ukv).reshape(bsz, seq, C_HEADS, C_NOPE + C_V)

    half = C_ROPE // 2
    freq = ROPE_BASE ** (-jnp.arange(half, dtype=jnp.float32) / half)
    ang = positions.astype(jnp.float32)[..., None] * freq
    cos = jnp.cos(ang)[:, :, None, :]
    sin = jnp.sin(ang)[:, :, None, :]
    q_rope = apply_rope(q[..., C_NOPE:], cos, sin)
    k_rope = apply_rope(kr[:, :, None, :], cos, sin)
    qf = jnp.concatenate([q[..., :C_NOPE], q_rope], axis=-1)
    kf = jnp.concatenate([kv[..., :C_NOPE],
                          jnp.broadcast_to(k_rope, (bsz, seq, C_HEADS, C_ROPE))], axis=-1)
    v = kv[..., C_NOPE:]
    scale = (C_NOPE + C_ROPE) ** -0.5

    qb = jnp.moveaxis(qf.reshape(bsz, seq // Q_BLOCK, Q_BLOCK, C_HEADS, C_NOPE + C_ROPE), 1, 0)

    def attend(qblk):
        s = jnp.einsum("bqhd,bkhd->bhqk", qblk, kf, preferred_element_type=jnp.float32) * scale
        pr = jax.nn.softmax(s, axis=-1)
        return jnp.einsum("bhqk,bkhd->bqhd", pr.astype(v.dtype), v)

    o = lax.map(attend, qb)
    o = jnp.moveaxis(o, 0, 1).reshape(bsz, seq, C_HEADS * C_V)
    return o @ w_out

def first_inputs(seed: int = 0) -> dict:
    key = jax.random.key(seed)
    ks = iter(jax.random.split(key, 40))
    f32 = jnp.float32

    def nrm(shape, scale):
        return jax.random.normal(next(ks), shape, f32) * scale

    def gain(shape):
        return 1.0 + 0.02 * jax.random.normal(next(ks), shape, f32)

    x = jax.random.normal(next(ks), (BATCH, SEQ, D_MODEL), f32)
    offsets = jax.random.randint(next(ks), (BATCH, 1), 0, 1024, dtype=jnp.int32)
    positions = offsets + jnp.arange(SEQ, dtype=jnp.int32)[None, :]

    forget_b = jnp.linspace(3.0, 6.0, A_HEADS, dtype=f32)
    gate_b = jnp.concatenate([
        nrm((N_EVEN, A_HEADS), 0.1),
        forget_b + nrm((N_EVEN, A_HEADS), 0.1),
        nrm((N_EVEN, A_HEADS), 0.1),
        forget_b + nrm((N_EVEN, A_HEADS), 0.1)], axis=-1)

    return {
        "x": x,
        "positions": positions,
        "ab_norm": gain((N_EVEN, D_MODEL)),
        "ab_w_in": nrm((N_EVEN, D_MODEL, AB_IN), D_MODEL ** -0.5),
        "ab_conv": nrm((N_EVEN, CONV_WIDTH, 2 * A_WIDTH), CONV_WIDTH ** -0.5),
        "ab_gate_b": gate_b,
        "ab_head_g": gain((N_EVEN, A_WIDTH)),
        "ab_v_g": gain((N_EVEN, B_WIDTH)),
        "ab_ws": nrm((N_EVEN, B_GROUPS, SGU_CHUNK, SGU_CHUNK), SGU_CHUNK ** -0.5),
        "ab_bs": gain((N_EVEN, B_GROUPS, SGU_CHUNK)),
        "ab_w_out": nrm((N_EVEN, A_WIDTH + B_WIDTH, D_MODEL), (A_WIDTH + B_WIDTH) ** -0.5),
        "c_norm": gain((N_ODD, D_MODEL)),
        "c_w_in": nrm((N_ODD, D_MODEL, C_IN), D_MODEL ** -0.5),
        "c_q_g": gain((N_ODD, Q_LORA)),
        "c_kv_g": gain((N_ODD, KV_LORA)),
        "c_w_uq": nrm((N_ODD, Q_LORA, C_HEADS * (C_NOPE + C_ROPE)), Q_LORA ** -0.5),
        "c_w_ukv": nrm((N_ODD, KV_LORA, C_HEADS * (C_NOPE + C_V)), KV_LORA ** -0.5),
        "c_w_out": nrm((N_ODD, C_HEADS * C_V, D_MODEL), (C_HEADS * C_V) ** -0.5),
        "ffn_norm": gain((DEPTH, D_MODEL)),
        "ffn_w1": nrm((DEPTH, D_MODEL, D_FF), D_MODEL ** -0.5),
        "ffn_w2": nrm((DEPTH, D_FF, D_MODEL), D_FF ** -0.5),
        "final_norm": gain((D_MODEL,)),
    }

def first_block(x, positions, ab_norm, ab_w_in, ab_conv, ab_gate_b, ab_head_g, ab_v_g,
              ab_ws, ab_bs, ab_w_out, c_norm, c_w_in, c_q_g, c_kv_g, c_w_uq, c_w_ukv,
              c_w_out, ffn_norm, ffn_w1, ffn_w2, final_norm):
    for layer in range(DEPTH):
        j = layer // 2
        if layer % 2 == 0:
            x = x + ab_mixer(rms_norm(x, ab_norm[j]), ab_w_in[j], ab_conv[j], ab_gate_b[j],
                             ab_head_g[j], ab_v_g[j], ab_ws[j], ab_bs[j], ab_w_out[j])
        else:
            x = x + mla_mixer(rms_norm(x, c_norm[j]), positions, c_w_in[j], c_q_g[j],
                              c_kv_g[j], c_w_uq[j], c_w_ukv[j], c_w_out[j])
        hf = rms_norm(x, ffn_norm[layer])
        x = x + jnp.square(jax.nn.relu(hf @ ffn_w1[layer])) @ ffn_w2[layer]
    return rms_norm(x, final_norm)


DEPTH_2 = 1

N_HEADS = 16
HEAD_DIM = D_MODEL // N_HEADS
N_MIXERS = 2
CHUNK = 64
LEFT_CHUNKS = 8
BAND = (LEFT_CHUNKS + 1) * CHUNK
REL_CLIP = 128
N_REL = (CHUNK - 1) + REL_CLIP + 1
D_FF_2 = int(math.ceil(D_MODEL * 8 / 3 / 256) * 256)
N_A_LAYERS = (DEPTH_2 + N_MIXERS - 1) // N_MIXERS
RMS_EPS = 1e-6


def rms_norm_2(x, g):
    xf = x.astype(jnp.float32)
    y = xf * lax.rsqrt(jnp.mean(xf * xf, axis=-1, keepdims=True) + RMS_EPS)
    return (y * g.astype(jnp.float32)).astype(x.dtype)

def split_heads(h, w_qkv):
    b, s, _ = h.shape
    qkv = (h @ w_qkv).reshape(b, s, 3, N_HEADS, HEAD_DIM)
    qkv = jnp.transpose(qkv, (2, 0, 3, 1, 4))
    return qkv[0], qkv[1], qkv[2]

def merge_heads(o):
    b, h, s, d = o.shape
    return jnp.transpose(o, (0, 2, 1, 3)).reshape(b, s, h * d)

def chunk_relpos_attention(h, w_qkv, w_o, rel_bias):
    b, s, _ = h.shape
    n_chunks = s // CHUNK
    q, k, v = split_heads(h, w_qkv)
    i_idx = np.arange(CHUNK)[:, None]
    j_idx = np.arange(BAND)[None, :]
    rel = np.clip(LEFT_CHUNKS * CHUNK + i_idx - j_idx, -(CHUNK - 1), REL_CLIP) + (CHUNK - 1)
    bias = jnp.take(rel_bias, jnp.asarray(rel, dtype=jnp.int32), axis=1).astype(jnp.float32)
    scale = 1.0 / math.sqrt(HEAD_DIM)
    outs = []
    for c in range(n_chunks):
        k0 = max(0, (c - LEFT_CHUNKS) * CHUNK)
        k1 = (c + 1) * CHUNK
        n_keys = k1 - k0
        q_blk = q[:, :, c * CHUNK:(c + 1) * CHUNK]
        sc = jnp.einsum('bhqd,bhkd->bhqk', q_blk, k[:, :, k0:k1]).astype(jnp.float32) * scale
        sc = sc + bias[None, :, :, BAND - n_keys:]
        p = jax.nn.softmax(sc, axis=-1).astype(v.dtype)
        outs.append(jnp.einsum('bhqk,bhkd->bhqd', p, v[:, :, k0:k1]))
    o = jnp.concatenate(outs, axis=2)
    return merge_heads(o) @ w_o

def stick_breaking_attention(h, w_qkv, w_o):
    b, s, _ = h.shape
    q, k, v = split_heads(h, w_qkv)
    scale = 1.0 / math.sqrt(HEAD_DIM)
    outs = []
    for qb in range(s // Q_BLOCK):
        n_keys = (qb + 1) * Q_BLOCK
        q_blk = q[:, :, qb * Q_BLOCK:(qb + 1) * Q_BLOCK]
        z = jnp.einsum('bhqd,bhkd->bhqk', q_blk, k[:, :, :n_keys]).astype(jnp.float32) * scale
        t_pos = qb * Q_BLOCK + np.arange(Q_BLOCK)
        causal = jnp.asarray((np.arange(n_keys)[None, :] < t_pos[:, None])[None, None])
        log_keep = jnp.where(causal, jax.nn.log_sigmoid(-z), 0.0)
        suffix = lax.cumsum(log_keep, axis=3, reverse=True) - log_keep
        a = jnp.where(causal, jnp.exp(jax.nn.log_sigmoid(z) + suffix), 0.0).astype(v.dtype)
        outs.append(jnp.einsum('bhqk,bhkd->bhqd', a, v[:, :, :n_keys]))
    o = jnp.concatenate(outs, axis=2)
    return merge_heads(o) @ w_o

def swiglu(h, w_gate, w_up, w_down):
    return (jax.nn.silu(h @ w_gate) * (h @ w_up)) @ w_down

def second_inputs(seed: int = 0) -> dict:
    key = jax.random.key(seed)
    ks = jax.random.split(key, 12)
    d, f = D_MODEL, D_FF_2
    nrm = lambda k, shape, fan: jax.random.normal(k, shape, jnp.float32) * (fan ** -0.5)
    gain = lambda k: 1.0 + 0.02 * jax.random.normal(k, (DEPTH_2, d), jnp.float32)
    return {
        "x": jax.random.normal(ks[0], (BATCH, SEQ, d), jnp.float32),
        "g_pre_mix": gain(ks[1]),
        "g_post_mix": gain(ks[2]),
        "w_qkv": nrm(ks[3], (DEPTH_2, d, 3 * d), d),
        "w_o": nrm(ks[4], (DEPTH_2, d, d), d),
        "rel_bias": 0.5 * jax.random.normal(ks[5], (N_A_LAYERS, N_HEADS, N_REL), jnp.float32),
        "g_pre_ffn": gain(ks[6]),
        "g_post_ffn": gain(ks[7]),
        "w_gate": nrm(ks[8], (DEPTH_2, d, f), d),
        "w_up": nrm(ks[9], (DEPTH_2, d, f), d),
        "w_down": nrm(ks[10], (DEPTH_2, f, d), f),
    }

def second_block(x, g_pre_mix, g_post_mix, w_qkv, w_o, rel_bias, g_pre_ffn, g_post_ffn, w_gate, w_up, w_down):
    for i in range(DEPTH_2):
        h = rms_norm_2(x, g_pre_mix[i])
        if i % N_MIXERS == 0:
            m = chunk_relpos_attention(h, w_qkv[i], w_o[i], rel_bias[i // N_MIXERS])
        else:
            m = stick_breaking_attention(h, w_qkv[i], w_o[i])
        x = x + rms_norm_2(m, g_post_mix[i])
        h = rms_norm_2(x, g_pre_ffn[i])
        x = x + rms_norm_2(swiglu(h, w_gate[i], w_up[i], w_down[i]), g_post_ffn[i])
    return x


def setup_inputs(seed=0):
    out = dict(first_inputs(seed))
    for name, value in second_inputs(seed + 1).items():
        if name != "x":
            out[name + "_2"] = value
    return out


def reference(
    x, positions, ab_norm, ab_w_in, ab_conv, ab_gate_b, ab_head_g, ab_v_g, ab_ws, ab_bs,
    ab_w_out, c_norm, c_w_in, c_q_g, c_kv_g, c_w_uq, c_w_ukv, c_w_out, ffn_norm, ffn_w1, ffn_w2,
    final_norm, g_pre_mix_2, g_post_mix_2, w_qkv_2, w_o_2, rel_bias_2, g_pre_ffn_2,
    g_post_ffn_2, w_gate_2, w_up_2, w_down_2,
):
    x = first_block(
        x, positions, ab_norm, ab_w_in, ab_conv, ab_gate_b, ab_head_g, ab_v_g, ab_ws, ab_bs,
        ab_w_out, c_norm, c_w_in, c_q_g, c_kv_g, c_w_uq, c_w_ukv, c_w_out, ffn_norm, ffn_w1,
        ffn_w2, final_norm,
    )
    return second_block(
        x, g_pre_mix_2, g_post_mix_2, w_qkv_2, w_o_2, rel_bias_2, g_pre_ffn_2, g_post_ffn_2,
        w_gate_2, w_up_2, w_down_2,
    )


_drawn_inputs = setup_inputs


def setup_inputs(seed=0):
    import zlib

    import numpy as np

    out = dict(_drawn_inputs(seed))
    spreads = {}
    factors = {'ab_norm': 2.903,
     'ab_head_g': 7.141,
     'ab_v_g': 7.022,
     'ab_bs': 7.614,
     'c_norm': 8.0,
     'c_q_g': 8.0,
     'c_kv_g': 8.0,
     'g_pre_mix_2': 3.263,
     'g_post_mix_2': 3.514,
     'g_pre_ffn_2': 3.67,
     'g_post_ffn_2': 4.847}
    for name, (base, spread) in spreads.items():
        noise = np.random.default_rng([zlib.crc32(name.encode()), seed]).standard_normal(out[name].shape)
        drawn = base * np.exp(spread * noise) if base else spread * noise
        out[name] = __import__('jax').numpy.asarray(drawn.astype(out[name].dtype))
    for name, factor in factors.items():
        out[name] = (out[name] * factor).astype(out[name].dtype)
    return out
```

```python
import math
from contextlib import ExitStack

import concourse.bass as bass
import numpy as np
from concourse import mybir

F32 = mybir.dt.float32
F32R = mybir.dt.float32r
I32 = mybir.dt.int32
ALU = mybir.AluOpType
ACT = mybir.ActivationFunctionType
AX = mybir.AxisListType

P = 128
D = 1024
KB = D // P
S = 256
TB = S // P
PIECE = 2048
RING = 3
EPS = 1e-6
NEG = -1.0e30

A_W, A_H, A_D, TAPS = 512, 4, 128, 5
PAD = (TAPS - 1) // 2
B_W, B_G = 512, 4
C_H, C_NOPE, C_ROPE, C_V = 16, 64, 32, 64
C_QK = C_NOPE + C_ROPE
HALF = C_ROPE // 2
Q_LORA, KV_LORA = 384, 256
C_IN = Q_LORA + KV_LORA + C_ROPE
CH = 256
D_FF = 4096
FC = D_FF // CH
H2, HD2, CHUNK = 16, 64, 64
REL_CLIP = 128
N_REL = CHUNK - 1 + REL_CLIP + 1
EXT = 384
D_FF2 = 2816
GC = D_FF2 // CH

P_QK, P_VA, P_OA, P_U, P_VB, P_AOUT = 0, 4, 6, 8, 10, 12
P_FFN0 = 16
P_CIN = P_FFN0 + 2 * FC
P_UKV = P_CIN + 3
P_UQ = P_UKV + 2
P_COUT = P_UQ + 3
P_FFN1 = P_COUT + 4
P_QK2 = P_FFN1 + 2 * FC
P_V2 = P_QK2 + 8
P_O2 = P_V2 + 4
P_GLU = P_O2 + 4
PIECES = P_GLU + 3 * GC

T_AB, T_AMIX, T_FFN0, T_C, T_LAT, T_CMIX, T_FFN1, T_2, T_2MIX, T_GLU = range(10)
T_BANKS = [4, 4, 4, 4, 3, 4, 4, 4, 4, 4]
T_BLOCKS = [8, 8, 8, 8, 5, 8, 8, 8, 8, 8]

VEC = {"ab_norm": 0, "ab_head_g": 8, "ab_bs": 12, "c_norm": 16, "c_q_g": 24, "c_kv_g": 27,
       "ffn_norm": 29, "g_pre_mix_2": 45, "g_pre_ffn_2": 53, "ab_conv": 61}
VECS = 61 + TAPS * KB

JOBS = {}
for _name, _n, _w in [("ab0", 1, D), ("ab1", 1, D), ("vb", 8, 128), ("ha", 8, 128), ("ffn00", 1, D), ("ffn01", 1, D),
                      ("c0", 1, D), ("c1", 1, D), ("cq", 2, Q_LORA), ("ckv", 2, KV_LORA), ("ffn10", 1, D),
                      ("ffn11", 1, D), ("fin0", 1, D), ("fin1", 1, D), ("pre0", 1, D), ("pre1", 1, D),
                      ("pm0", 1, D), ("pm1", 1, D), ("glu0", 1, D), ("glu1", 1, D), ("pf0", 1, D), ("pf1", 1, D)]:
    JOBS[_name] = (sum(v[1] for v in JOBS.values()), _n, _w)
JOB_AT = {name: i for i, name in enumerate(JOBS)}
SS_ACT = ["ab0", "ab1", "ffn00", "ffn01", "c0", "c1", "cq0", "cq", "ckv0", "ckv", "ffn10", "ffn11", "fin0", "fin1",
          "pre0", "pre1", "pm0", "pm1", "glu0", "glu1", "pf0", "pf1"]
SS_DVE = ["vb", "ha"]
X_AT = {"ffn0": 0, "c": 2, "ffn1": 4, "fin": 6, "pre": 8, "glu": 10, "out": 12}

TWO_PI = 2 * math.pi
PI_1 = 6.28125
PI_2 = float(np.float32(round((TWO_PI - PI_1) * 2 ** 20) / 2 ** 20))
PI_3 = TWO_PI - PI_1 - PI_2
ROUND = 1.5 * 2.0 ** 23
PI_IN = 3.1415925


def build(nc, d, out):
    ctx = ExitStack()
    with ctx:
        def sb(name, shape, dt=F32):
            return ctx.enter_context(nc.sbuf_tensor(name, shape, dt))

        def sem(name):
            return ctx.enter_context(nc.semaphore(name))

        psum = ctx.enter_context(nc.psum_tensor("psum", [P, 8, 512], F32))
        raw = sb("raw", [P, RING, PIECE])
        w_hi = sb("w_hi", [P, RING, PIECE], F32R)
        w_lo = sb("w_lo", [P, RING, PIECE], F32R)
        x = sb("x", [P, TB, D])
        xn = sb("xn", [P, TB, D])
        h_hi = sb("h_hi", [P, KB, S], F32R)
        h_lo = sb("h_lo", [P, KB, S], F32R)
        junk = sb("junk", [P, D])
        g_act = sb("g_act", [P, 3, 2 * S])
        g_mul = sb("g_mul", [P, 3, 2 * S])
        g_hi = sb("g_hi", [P, 3, 2 * S], F32R)
        g_lo = sb("g_lo", [P, 3, 2 * S], F32R)
        ident = sb("ident", [P, P])
        mask = sb("mask", [P, 2, P])
        vecs = sb("vecs", [VECS, P])
        cols = sb("cols", [P, VECS])
        mhalf = sb("mhalf", [P, 8])
        n_stat = sum(v[1] for v in JOBS.values())
        ssq = sb("ssq", [P, n_stat])
        msq = sb("msq", [P, n_stat])
        rstd = sb("rstd", [P, n_stat])
        pos_i = sb("pos_i", [P, TB], I32)
        pos_f = sb("pos_f", [P, TB])
        freq = sb("freq", [P, HALF])
        ang = sb("ang", [P, TB, HALF])
        turns = sb("turns", [P, TB, HALF])
        ang2 = sb("ang2", [P, 2, TB, HALF])
        trig = sb("trig", [P, 2, TB, HALF])
        rel_t = sb("rel_t", [H2, N_REL])
        rel_ext = sb("rel_ext", [H2, EXT])
        rel_dram = nc.dram_tensor("rel_scratch", (H2, P, EXT), F32, kind="Internal")

        ARENA = 16640
        arena = sb("arena", [P, ARENA])

        class Carve:
            def __init__(self):
                self.at = 0

            def __call__(self, *shape):
                n = int(np.prod(shape))
                assert self.at + n <= ARENA, (self.at, n)
                v = arena[:, self.at:self.at + n]
                self.at += n
                if len(shape) == 2:
                    v = v.rearrange("p (a b) -> p a b", a=shape[0])
                if len(shape) == 3:
                    v = v.rearrange("p (a b c) -> p a b c", a=shape[0], b=shape[1])
                return v

        ca = Carve()
        qk_pad = ca(8, S + 2 * PAD)
        qk_conv = ca(8, S)
        qkT = qk_conv
        v_ext = ca(TB, A_H, A_D + 1)
        oa = ca(TB, A_W)
        u_act = ca(TB, B_W)
        vb = ca(TB, B_W)
        sq_tmp = ca(TB, A_W)
        hsum = ca(TB, A_W)
        decay = g_act[:, 0:2, :].rearrange("p u (b t) -> p u b t", b=4)
        score = g_mul[:, 0:2, :].rearrange("p u (b t) -> p u b t", b=4)
        ws_raw = g_act[:, 2, :].rearrange("p (g t) -> p g t", g=B_G)
        wsT = ca(B_G, P)
        vg_row = ca(B_W)
        gw_raw = ca(KB, 16)
        gb_row = ca(16)
        gates = ca(4, 8)
        g_abs = ca(4, 4)
        g_exp = ca(4, 4)
        g_ln = ca(4, 4)
        cumf = ca(2, S)
        a_row = ca(2, S)
        m_row = ca(2, S)
        mt_row = ca(2, S)
        ones_row = ca(S)
        nsel = ca(A_H, P)
        a_col = ca(TB, 8)
        e_col = ca(TB, 8)
        dmax = ca(2)
        dinv = ca(2)
        gw_hi = sb("gw_hi", [P, KB, 16], F32R)
        gw_lo = sb("gw_lo", [P, KB, 16], F32R)

        cc = Carve()
        q_tok = cc(TB, C_H * C_QK)
        kfT = cc(C_H, S)
        qfT = cc(C_H, S)
        v_tok = cc(TB, D)
        prob = cc(2, 2 * S)
        probT = cc(2, 2 * S)
        krr = cc(TB, C_QK)
        krT = cc(S)
        nmax = cc(2, C_H)
        psm = cc(2, C_H)
        pinv = cc(2, C_H)
        rp = [xn[:, :, i * S:(i + 1) * S].rearrange("p t (h e) -> p t h e", h=C_H) for i in range(4)]
        rk = [junk[:, i * 32:(i + 1) * 32].rearrange("p (t e) -> p t e", t=TB) for i in range(4)]

        c2 = Carve()
        qT2 = c2(8, S)
        kT2 = c2(8, S)
        v2 = c2(TB, D)
        s2 = c2(2, 3 * P)
        prob2 = c2(2, 3 * P)
        probT2 = c2(2, 3 * P)
        nmax2 = c2(2, H2)
        psm2 = c2(2, H2)
        pinv2 = c2(2, H2)
        bias2 = c2(H2, S)
        fin_row = c2(D)
        pm_row = c2(D)
        pf_row = c2(D)

        arrived = [sem(f"arrived{i}") for i in range(RING)]
        hi_ready = sem("hi_ready")
        lo_ready = sem("lo_ready")
        piece_used = sem("piece_used")
        x_loaded = sem("x_loaded")
        vecs_loaded = sem("vecs_loaded")
        ws_loaded = sem("ws_loaded")
        ab_small = sem("ab_small")
        pos_loaded = sem("pos_loaded")
        rel_loaded = sem("rel_loaded")
        rel_stored = sem("rel_stored")
        rows2_loaded = sem("rows2_loaded")
        bias_loaded = sem("bias_loaded")
        x_stored = sem("x_stored")
        ident_ready = sem("ident_ready")
        consts_ready = sem("consts_ready")
        pool_step = sem("pool_step")
        dve_step = sem("dve_step")
        act_step = sem("act_step")
        vecs_turned = sem("vecs_turned")
        cols_ready = sem("cols_ready")
        gw_hi_ready = sem("gw_hi_ready")
        gw_ready = sem("gw_ready")
        ss_act = sem("ss_act")
        ss_dve = sem("ss_dve")
        rstd_ready = sem("rstd_ready")
        x_ready = sem("x_ready")
        xn_ready = sem("xn_ready")
        turned = sem("turned")
        h_hi_ready = sem("h_hi_ready")
        h_lo_ready = sem("h_lo_ready")
        acc_half = sem("acc_half")
        gates_done = sem("gates_done")
        gate_abs = sem("gate_abs")
        gate_ln = sem("gate_ln")
        gates_ready = sem("gates_ready")
        rows_turned = sem("rows_turned")
        rows_ready = sem("rows_ready")
        cols_turned = sem("cols_turned")
        gcols_ready = sem("gcols_ready")
        evac_qk = sem("evac_qk")
        conv_done = sem("conv_done")
        silu_done = sem("silu_done")
        evac_v = sem("evac_v")
        evac_oa = sem("evac_oa")
        evac_u = sem("evac_u")
        evac_vb = sem("evac_vb")
        vbn_ready = sem("vbn_ready")
        spread = sem("spread")
        w_ready = sem("w_ready")
        s_ready = sem("s_ready")
        g_ready = sem("g_ready")
        o_ready = sem("o_ready")
        unit_done = sem("unit_done")
        sgu_done = sem("sgu_done")
        rel_built = sem("rel_built")
        trig_in = sem("trig_in")
        trig_ready = sem("trig_ready")
        act_out = sem("act_out")
        mul_out = sem("mul_out")
        g_hi_ready = sem("g_hi_ready")
        g_lo_ready = sem("g_lo_ready")
        krr_ready = sem("krr_ready")
        krr_turned = sem("krr_turned")
        krT_ready = sem("krT_ready")
        kfT_rope = sem("kfT_rope")
        krr_zero = sem("krr_zero")
        evac_k = sem("evac_k")
        evac_k2 = sem("evac_k2")
        evac_vc = sem("evac_vc")
        evac_q = sem("evac_q")
        q_roped = sem("q_roped")
        qf_turned = sem("qf_turned")
        qf_ready = sem("qf_ready")
        at_s, at_max, at_exp, at_pt, at_ptsb, at_pv = [
            [sem(f"{n}{i}") for i in range(2)] for n in ("scores", "maxed", "exped", "pturned", "pcopied", "pv")]
        evac_qk2 = sem("evac_qk2")
        evac_v2 = sem("evac_v2")
        bias_ready = sem("bias_ready")

        w_in = d["ab_w_in"][0].rearrange("(k p) n -> p k n", p=P)
        w_uv0 = 4 * A_W + 4 * A_H

        def rows_of(w, k0, k1):
            return w.rearrange("(k p) n -> p k n", p=P)[:, k0:k1, :]

        def cols_of(w, k0, k1, c0, c1):
            return w.rearrange("(k p) n -> p k n", p=P)[:, k0:k1, c0:c1]

        ab_w, c_w, qkv = d["ab_w_in"][0], d["c_w_in"][0], d["w_qkv_2"][0]
        SRC = {}
        for j in range(4):
            SRC[P_QK + j] = cols_of(ab_w, 0, KB, j * CH, (j + 1) * CH)
        for first, c0 in ((P_VA, 1024), (P_OA, 1536), (P_U, w_uv0), (P_VB, w_uv0 + B_W)):
            for j in range(2):
                SRC[first + j] = cols_of(ab_w, 4 * j, 4 * j + 4, c0, c0 + 512)
        for first, w in ((P_AOUT, d["ab_w_out"][0]), (P_COUT, d["c_w_out"][0]), (P_O2, d["w_o_2"][0])):
            for j in range(4):
                SRC[first + j] = rows_of(w, 2 * j, 2 * j + 2)
        for j, (k0, k1) in enumerate(((0, 3), (3, 6), (6, 8))):
            SRC[P_CIN + j] = rows_of(c_w, k0, k1)
        for j in range(2):
            SRC[P_UKV + j] = cols_of(d["c_w_ukv"][0], 0, 2, j * 1024, (j + 1) * 1024)
        for j in range(3):
            SRC[P_UQ + j] = cols_of(d["c_w_uq"][0], 0, 3, j * 512, (j + 1) * 512)
        for j in range(8):
            SRC[P_QK2 + j] = cols_of(qkv, 0, KB, j * CH, (j + 1) * CH)
        for n in range(2):
            for j in range(2):
                SRC[P_V2 + 2 * n + j] = cols_of(qkv, 4 * j, 4 * j + 4, 2 * D + n * 512, 2 * D + (n + 1) * 512)

        def width(n):
            if n in SRC:
                return SRC[n].shape[1] * SRC[n].shape[2]
            return PIECE

        def part(t, n, a):
            w = width(n)
            return t[:, n % RING, 0:w].rearrange("p (a b) -> p a b", a=a)

        def views(n, t, is_raw):
            w = t[:, n % RING, 0:width(n)]
            if not P_UKV <= n < P_UKV + 2:
                return [w]
            if is_raw:
                w = w.rearrange("p (k h v e) -> p v k h e", k=2, h=8, v=2)
            else:
                w = w.rearrange("p (k v h e) -> p v k h e", k=2, h=8, v=2)
            return [w[:, 0], w[:, 1]]

        def t_base(t):
            return sum(T_BANKS[:t])

        def bank(b, n=1):
            return psum[:, b:b + n, :].rearrange("p b c -> p (b c)")

        def col(name, i):
            c = VEC[name] + i
            return cols[:, c:c + 1]

        def gain(t, k):
            if t == T_AB:
                return col("ab_norm", k)
            if t == T_AMIX:
                return col("ab_head_g", k) if k < 4 else None
            if t == T_FFN0:
                return col("ffn_norm", k)
            if t == T_C:
                return col("c_norm", k)
            if t == T_LAT:
                return col("c_q_g", k) if k < 3 else col("c_kv_g", k - 3)
            if t == T_FFN1:
                return col("ffn_norm", 8 + k)
            if t == T_2:
                return col("g_pre_mix_2", k)
            if t == T_GLU:
                return col("g_pre_ffn_2", k)
            return None

        block = ctx.enter_context(nc.Block())

        @block.sync
        def _(sp):
            def load(n, slot, src, wide=PIECE, a=None):
                if not (isinstance(n, int) and n < RING):
                    sp.wait_ge(lo_ready, n - RING + 1)
                dst = raw[:, slot, 0:wide].rearrange("p (a b) -> p a b", a=a)
                sp.dma_start(dst, src).then_inc(arrived[slot], 16)

            def load_static(n):
                load(n, n % RING, SRC[n], width(n), SRC[n].shape[1])

            def ffn(first, w1, w2):
                w1v = w1.rearrange("(k p) n -> p k n", p=P)
                w2v = w2.rearrange("(k p) n -> p k n", p=P)
                load(first, first % RING, w1v[:, :, 0:CH], a=KB)
                with sp.Fori(0, (FC - 1) // 3) as i:
                    for j in range(3):
                        n = first + 1 + 2 * j
                        load(n + 6 * i, n % RING, w1v[:, :, bass.ds((3 * i + j + 1) * CH, CH)], a=KB)
                        load(n + 1 + 6 * i, (n + 1) % RING, w2v[:, bass.ds((3 * i + j) * 2, 2), :], a=2)
                n = first + 2 * FC - 1
                load(n, n % RING, w2v[:, 2 * FC - 2:2 * FC, :], a=2)

            def glu(first):
                wg = d["w_gate_2"][0].rearrange("(k p) n -> p k n", p=P)
                wu = d["w_up_2"][0].rearrange("(k p) n -> p k n", p=P)
                wd = d["w_down_2"][0].rearrange("(k p) n -> p k n", p=P)
                load(first, first % RING, wg[:, :, 0:CH], a=KB)
                load(first + 1, (first + 1) % RING, wu[:, :, 0:CH], a=KB)
                with sp.Fori(0, GC - 1) as c:
                    n = first + 2
                    load(n + 3 * c, n % RING, wg[:, :, bass.ds((c + 1) * CH, CH)], a=KB)
                    load(n + 1 + 3 * c, (n + 1) % RING, wu[:, :, bass.ds((c + 1) * CH, CH)], a=KB)
                    load(n + 2 + 3 * c, (n + 2) % RING, wd[:, bass.ds(2 * c, 2), :], a=2)
                n = first + 3 * GC - 1
                load(n, n % RING, wd[:, 2 * GC - 2:2 * GC, :], a=2)

            for n in range(P_FFN0):
                load_static(n)
            ffn(P_FFN0, d["ffn_w1"][0], d["ffn_w2"][0])
            for n in range(P_CIN, P_FFN1):
                load_static(n)
            ffn(P_FFN1, d["ffn_w1"][1], d["ffn_w2"][1])
            for n in range(P_QK2, P_GLU):
                load_static(n)
            glu(P_GLU)
            out_v = out[0].rearrange("(t p) c -> p t c", p=P)
            for tb in range(TB):
                sp.wait_ge(x_ready, X_AT["out"] + tb + 1)
                sp.dma_start(out_v[:, tb, :], x[:, tb, :]).then_inc(x_stored, 16)
            sp.wait_ge(x_stored, 16 * TB)

        @block.gpsimd
        def _(pool):
            steps = [0]

            def step(ins):
                steps[0] += 1
                ins.then_inc(pool_step, 1)
                pool.wait_ge(pool_step, steps[0])

            step(pool.memset(ident[:, :], 0.0))
            pool.affine_select(out=ident[:, :], in_=ident[:, :], compare_op=ALU.not_equal, fill=1.0, base=0,
                               pattern=[[-1, P]], channel_multiplier=1).then_inc(ident_ready, 1)
            step(pool.memset(mhalf[:, :], -0.5))

            def rms(name):
                c0, n, w = JOBS[name]
                if name in SS_ACT:
                    pool.wait_ge(ss_act, SS_ACT.index(name) + 1)
                else:
                    pool.wait_ge(ss_dve, SS_DVE.index(name) + 1)
                step(pool.tensor_scalar(msq[:, c0:c0 + n], ssq[:, c0:c0 + n], 1.0 / w, EPS, ALU.mult, ALU.add))
                pool.tensor_tensor(rstd[:, c0:c0 + n], msq[:, c0:c0 + n], mhalf[:, 0:n], ALU.pow)\
                    .then_inc(rstd_ready, 1)

            rms("ab0")
            rms("ab1")
            step(pool.memset(mask[:, :, :], 0.0))
            pool.affine_select(out=mask[:, 0, :], in_=mask[:, 0, :], compare_op=ALU.is_ge, fill=NEG, base=0,
                               pattern=[[1, P]], channel_multiplier=-1).then_inc(consts_ready, 1)
            pool.affine_select(out=mask[:, 1, :], in_=mask[:, 1, :], compare_op=ALU.is_ge, fill=NEG, base=0,
                               pattern=[[-1, P]], channel_multiplier=1).then_inc(consts_ready, 1)
            for i in range(HALF):
                ins = pool.memset(freq[:, i:i + 1], float(np.float32(10000.0) ** np.float32(-i / HALF)))
            ins.then_inc(consts_ready, 1)
            pool.wait_ge(rel_built, 1)
            pool.dma_start(rel_dram.ap(), rel_ext[:, :].unsqueeze(1).to_broadcast([H2, P, EXT])).then_inc(rel_stored, 16)
            for name in ("vb", "ha", "ffn00", "ffn01", "c0", "c1", "cq", "ckv"):
                rms(name)
            pool.wait_ge(krT_ready, 1)
            pool.tensor_copy(kfT[C_NOPE:C_QK, 0:C_H, :],
                             krT[C_NOPE:C_QK, :].unsqueeze(1).to_broadcast([C_ROPE, C_H, S])).then_inc(kfT_rope, 1)
            for name in ("ffn10", "ffn11", "fin0", "fin1", "pre0", "pre1"):
                if name == "ffn10":
                    pool.wait_ge(turned, t_base(T_CMIX) + T_BANKS[T_CMIX])
                    pool.wait_ge(rel_stored, 16)
                    pool.dma_start(bias2[:, :, :], bass.AP(rel_dram, P - 1, [[EXT - 1, P], [P * EXT, H2], [1, S]]))\
                        .then_inc(bias_loaded, 16)
                    pool.dma_start(fin_row, d["final_norm"].partition_broadcast(P)).then_inc(rows2_loaded, 16)
                    pool.dma_start(pm_row, d["g_post_mix_2"][0].partition_broadcast(P)).then_inc(rows2_loaded, 16)
                    pool.dma_start(pf_row, d["g_post_ffn_2"][0].partition_broadcast(P)).then_inc(rows2_loaded, 16)
                    pool.wait_ge(bias_loaded, 16)
                    pool.memset(bias2[0:CHUNK, :, P + CHUNK:S], NEG).then_inc(bias_ready, 1)
                rms(name)
            for name in ("pm0", "pm1", "glu0", "glu1", "pf0", "pf1"):
                rms(name)

        @block.scalar
        def _(act):
            steps = [0]

            def step(ins):
                steps[0] += 1
                ins.then_inc(act_step, 1)
                act.wait_ge(act_step, steps[0])

            def hi(n):
                if n >= PIECES:
                    return
                act.wait_ge(arrived[n % RING], 16 * (n // RING + 1))
                if n >= RING:
                    act.wait_ge(piece_used, n - RING + 1)
                for dst, src in zip(views(n, w_hi, False), views(n, raw, True)):
                    ins = act.activation(dst, src, ACT.Copy)
                ins.then_inc(hi_ready, 1)

            def hi_loop(n0, i):
                slot = n0 % RING
                act.wait_ge(arrived[slot], 16 * (n0 // RING + 1) + 32 * i)
                act.wait_ge(piece_used, n0 - RING + 1 + 6 * i)
                act.activation(w_hi[:, slot, :], raw[:, slot, :], ACT.Copy).then_inc(hi_ready, 1)

            def turn(t):
                for q in range(T_BANKS[t]):
                    act.wait_ge(turned, t_base(t) + q + 1)
                    for k in range(2 * q, min(2 * q + 2, T_BLOCKS[t])):
                        g = gain(t, k)
                        ins = act.activation(h_hi[:, k, :], bank(4 + q)[:, (k % 2) * S:(k % 2 + 1) * S], ACT.Copy,
                                             scale=1.0 if g is None else g)
                    ins.then_inc(h_hi_ready, 1)

            sums = [0]

            def squares(src, c):
                if sums[0]:
                    act.wait_ge(ss_act, sums[0])
                sums[0] += 1
                act.activation(junk[:, 0:src.shape[-1]], src, ACT.Square,
                               accum_out=ssq[:, c:c + 1]).then_inc(ss_act, 1)

            def squares_x(jobs, x_at):
                for tb in range(TB):
                    act.wait_ge(x_ready, x_at + tb + 1)
                    squares(x[:, tb, :], JOBS[jobs[tb]][0])

            x_v = d["x"][0].rearrange("(t p) c -> p t c", p=P)
            act.dma_start(x[:, 0, :], x_v[:, 0, :]).then_inc(x_loaded, 16)
            act.dma_start(x[:, 1, :], x_v[:, 1, :]).then_inc(x_loaded, 16)
            for name, r0 in VEC.items():
                v = d[name]
                if name == "ab_conv":
                    v = v[0].rearrange("w (k p) -> (w k) p", p=P)
                elif name == "ab_bs":
                    v = v[0]
                else:
                    v = v.rearrange("l (k p) -> (l k) p", p=P)
                act.dma_start(vecs[r0:r0 + v.shape[0], :], v).then_inc(vecs_loaded, 16)
            act.dma_start(ws_raw[:, :, :], d["ab_ws"][0].rearrange("g t s -> t g s")).then_inc(ws_loaded, 16)
            act.dma_start(gw_raw[:, :, :], w_in[:, :, 4 * A_W:4 * A_W + 16]).then_inc(ab_small, 16)
            act.dma_start(gb_row, d["ab_gate_b"][0].partition_broadcast(P)).then_inc(ab_small, 16)
            act.dma_start(vg_row, d["ab_v_g"][0].partition_broadcast(P)).then_inc(ab_small, 16)
            act.dma_start(pos_i[:, :], d["positions"][0].rearrange("(t p) -> p t", p=P),
                          allow_slow_non_contiguous=True).then_inc(pos_loaded, 16)
            act.dma_start(rel_t[:, :], d["rel_bias_2"][0]).then_inc(rel_loaded, 16)
            act.wait_ge(x_loaded, 32)
            for tb in range(TB):
                squares(x[:, tb, :], JOBS["ab0"][0] + tb)
            act.wait_ge(vecs_turned, 1)
            act.activation(cols[:, :], bank(0)[:, 0:VECS], ACT.Copy).then_inc(cols_ready, 1)
            act.wait_ge(vecs_turned, 2)
            act.activation(wsT[:, :, :], bank(1).rearrange("p (g t) -> p g t", g=B_G), ACT.Copy).then_inc(cols_ready, 1)
            act.wait_ge(ab_small, 48)
            act.activation(gw_hi[:, :, :], gw_raw[:, :, :], ACT.Copy).then_inc(gw_hi_ready, 1)
            hi(0)
            act.wait_ge(cols_ready, 1)
            turn(T_AB)
            hi(1)
            hi(2)
            act.wait_ge(trig_in, 1)
            act.activation(trig[:, :, :, :], ang2[:, :, :, :], ACT.Sin).then_inc(trig_ready, 1)
            act.wait_ge(gate_abs, 1)
            step(act.activation(g_exp[:, :, :], g_abs[:, :, :], ACT.Exp, scale=-1.0))
            act.activation(g_ln[:, :, :], g_exp[:, :, :], ACT.Ln, bias=1.0).then_inc(gate_ln, 1)

            def qk_out(j):
                act.wait_ge(piece_used, P_QK + j + 1)
                act.activation(qk_pad[:, 2 * j:2 * j + 2, PAD:PAD + S],
                               bank(j).rearrange("p (b t) -> p b t", b=2), ACT.Copy).then_inc(evac_qk, 1)

            def silu(j):
                act.wait_ge(conv_done, j + 1)
                act.activation(qkT[:, 2 * j:2 * j + 2, :], qk_conv[:, 2 * j:2 * j + 2, :], ACT.Silu)\
                    .then_inc(silu_done, 1)

            for j in range(4):
                qk_out(j)
                hi(P_QK + j + RING)
                if j >= 2:
                    silu(j - 2)
            hi(P_VA + RING)
            silu(2)
            silu(3)
            act.wait_ge(piece_used, P_VA + 2)
            for tb in range(TB):
                act.activation(v_ext[:, tb, :, 0:A_D], bank(4 + tb).rearrange("p (h e) -> p h e", h=A_H), ACT.Copy)\
                    .then_inc(evac_v, 1)
            hi(P_VA + 1 + RING)
            hi(P_OA + RING)
            act.wait_ge(piece_used, P_OA + 2)
            for tb in range(TB):
                act.activation(oa[:, tb, :], bank(tb), ACT.Sigmoid).then_inc(evac_oa, 1)
            hi(P_OA + 1 + RING)
            hi(P_U + RING)
            act.wait_ge(piece_used, P_U + 2)
            for tb in range(TB):
                act.activation(u_act[:, tb, :], bank(2 + tb), ACT.Gelu_apprx_tanh).then_inc(evac_u, 1)
            hi(P_U + 1 + RING)
            hi(P_VB + RING)
            act.wait_ge(piece_used, P_VB + 2)
            for tb in range(TB):
                act.activation(vb[:, tb, :], bank(4 + tb), ACT.Gelu_apprx_tanh).then_inc(evac_vb, 1)
            hi(P_VB + 1 + RING)
            act.wait_ge(cols_turned, 1)
            tc = bank(6)[:, 0:32].rearrange("p (q t e) -> p q t e", q=2, t=TB)
            act.activation(a_col[:, :, :], tc[:, 0], ACT.Copy).then_inc(gcols_ready, 1)
            act.activation(e_col[:, :, :], tc[:, 1], ACT.Exp, scale=-1.0).then_inc(gcols_ready, 1)
            act.wait_ge(gcols_ready, 2)
            for u in range(2 * A_H):
                h, back = u // 2, u % 2
                act.wait_ge(spread, u + 1)
                if u >= 2:
                    act.wait_ge(g_ready, u - 1)
                b = bank(u % 2)
                dst = decay[:, u % 2, :, :].rearrange("p b t -> p (b t)")
                at = back * A_H + h
                for s0, (c0, c1) in enumerate([((0, 256), (384, 512)), ((0, 128), (256, 512))][back]):
                    ins = act.activation(dst[:, c0:c1], b[:, c0:c1], ACT.Exp, bias=a_col[:, s0, at:at + 1])
                ins.then_inc(w_ready, 1)
            turn(T_AMIX)
            for j in range(4):
                hi(P_AOUT + j + RING)

            def ffn(first, hb, t, jobs, x_at):
                squares_x(jobs, x_at)
                turn(t)

                def hidden(c, r, n_w1):
                    act.wait_ge(piece_used, n_w1 + 1)
                    if not (isinstance(c, int) and c < 3):
                        act.wait_ge(g_lo_ready, hb + c - 2)
                    act.activation(g_act[:, r, :], bank(4 + r), ACT.Relu).then_inc(act_out, 1)
                    act.wait_ge(act_out, hb + c + 1)
                    act.activation(g_hi[:, r, :], g_act[:, r, :], ACT.Square).then_inc(g_hi_ready, 1)

                hidden(0, 0, first)
                hi(first + RING)

                def chunk(c, j, i):
                    n = first + 1 + 2 * j
                    hidden(c + 1, (j + 1) % 3, n + 6 * i)
                    if isinstance(i, int):
                        hi(n + 6 * i + RING)
                        hi(n + 6 * i + 1 + RING)
                    else:
                        hi_loop(n + RING, i)
                        hi_loop(n + 1 + RING, i)

                for j in range(3):
                    chunk(j, j, 0)
                with act.Fori(1, (FC - 1) // 3) as i:
                    for j in range(3):
                        chunk(3 * i + j, j, i)
                hi(first + 2 * FC - 1 + RING)

            ffn(P_FFN0, 0, T_FFN0, ("ffn00", "ffn01"), X_AT["ffn0"])

            squares_x(("c0", "c1"), X_AT["c"])
            turn(T_C)
            for j in range(2):
                hi(P_CIN + j + RING)
            act.wait_ge(piece_used, P_CIN + 3)
            for name, c0, w in (("cq", 0, Q_LORA), ("ckv", Q_LORA, KV_LORA)):
                for tb in range(TB):
                    squares(bank(2 * tb, 2)[:, c0:c0 + w], JOBS[name][0] + tb)
            hi(P_CIN + 2 + RING)
            turn(T_LAT)
            act.wait_ge(krr_turned, 1)
            act.activation(krT[C_NOPE:C_QK, :], psum[C_NOPE:C_QK, 7, 0:S], ACT.Copy).then_inc(krT_ready, 1)
            for j in range(2):
                act.wait_ge(piece_used, P_UKV + j + 1)
                b0 = (4, 0)[j]
                act.activation(kfT[0:C_NOPE, 8 * j:8 * j + 8:2, :],
                               bank(b0, 2)[0:C_NOPE, :].rearrange("p (h t) -> p h t", h=4), ACT.Copy).then_inc(evac_k, 1)
                hi(P_UKV + j + RING)
            for j in range(3):
                act.wait_ge(piece_used, P_UQ + j + 1)
                b0 = (4, 6, 0)[j]
                for tb in range(TB):
                    ins = act.activation(q_tok[:, tb, j * 512:(j + 1) * 512], bank(b0 + tb), ACT.Copy,
                                         scale=float(C_QK) ** -0.5)
                ins.then_inc(evac_q, 1)
                hi(P_UQ + j + RING)
            for n in range(1, 8, 2):
                act.wait_ge(qf_turned, n + 1)
                act.activation(qfT[0:C_QK, 2 * n:2 * n + 2, :],
                               bank(4 + n % 4)[0:C_QK, :].rearrange("p (h t) -> p h t", h=2), ACT.Copy)\
                    .then_inc(qf_ready, 1)
            for h in range(C_H):
                act.wait_ge(at_max[0], h + 1)
                if h >= 2:
                    act.wait_ge(at_pt[0], h - 1)
                for qb in range(2):
                    ins = act.activation(prob[:, h % 2, qb * S:(qb + 1) * S], bank(4 + h % 2)[:, qb * S:(qb + 1) * S],
                                         ACT.Exp, bias=nmax[:, qb, h:h + 1], accum_out=psm[:, qb, h:h + 1])
                ins.then_inc(at_exp[0], 1)
            turn(T_CMIX)
            for j in range(4):
                hi(P_COUT + j + RING)
            ffn(P_FFN1, FC, T_FFN1, ("ffn10", "ffn11"), X_AT["ffn1"])

            squares_x(("fin0", "fin1"), X_AT["fin"])
            squares_x(("pre0", "pre1"), X_AT["pre"])
            turn(T_2)
            for j in range(8):
                act.wait_ge(piece_used, P_QK2 + j + 1)
                dst = (qT2 if j < 4 else kT2)[:, 2 * (j % 4):2 * (j % 4) + 2, :]
                act.activation(dst, bank(j).rearrange("p (b t) -> p b t", b=2), ACT.Copy,
                               scale=float(HD2) ** -0.5 if j < 4 else 1.0).then_inc(evac_qk2, 1)
                hi(P_QK2 + j + RING)
            for n in range(2):
                hi(P_V2 + 2 * n + RING)
                act.wait_ge(piece_used, P_V2 + 2 * n + 2)
                for tb in range(TB):
                    act.activation(v2[:, tb, n * 512:(n + 1) * 512], bank(2 * n + tb), ACT.Copy).then_inc(evac_v2, 1)
                hi(P_V2 + 2 * n + 1 + RING)

            def copy_pt(h):
                act.wait_ge(at_pt[1], h + 1)
                if h >= 2:
                    act.wait_ge(at_pv[1], h - 1)
                act.activation(probT2[:, h % 2, :], bank(6 + h % 2)[:, 0:3 * P], ACT.Copy).then_inc(at_ptsb[1], 1)

            for h in range(H2):
                act.wait_ge(at_max[1], h + 1)
                if h >= 2:
                    act.wait_ge(at_pt[1], h - 1)
                for qb, (c0, c1) in enumerate(((0, P), (P, 3 * P))):
                    ins = act.activation(prob2[:, h % 2, c0:c1], s2[:, h % 2, c0:c1], ACT.Exp, scale=-1.0,
                                         bias=nmax2[:, qb, h:h + 1], accum_out=psm2[:, qb, h:h + 1])
                ins.then_inc(at_exp[1], 1)
                if h >= 1:
                    copy_pt(h - 1)
            copy_pt(H2 - 1)
            turn(T_2MIX)
            for j in range(4):
                hi(P_O2 + j + RING)

            def squares_acc(stage, last, jobs):
                for tb in range(TB):
                    if tb == 0:
                        act.wait_ge(acc_half, stage + 1)
                    else:
                        act.wait_ge(piece_used, last + 1)
                    squares(bank(2 * tb, 2), JOBS[jobs[tb]][0])

            squares_acc(4, P_O2 + 3, ("pm0", "pm1"))
            squares_x(("glu0", "glu1"), X_AT["glu"])
            turn(T_GLU)
            hb, first = 2 * FC, P_GLU

            def silu_glu(c, r, n_gate):
                act.wait_ge(piece_used, n_gate + 1)
                if not (isinstance(c, int) and c < 2):
                    act.wait_ge(g_lo_ready, hb + c - 1)
                act.activation(g_act[:, r, :], bank(4 + 2 * r), ACT.Silu).then_inc(act_out, 1)

            def glu_hi(c, r):
                act.wait_ge(mul_out, hb + c + 1)
                act.activation(g_hi[:, r, :], g_mul[:, r, :], ACT.Copy).then_inc(g_hi_ready, 1)

            silu_glu(0, 0, first)
            hi(first + RING)
            glu_hi(0, 0)
            hi(first + 1 + RING)

            def glu_chunk(c, j, i):
                n = first + 2 + 3 * j
                silu_glu(c + 1, (j + 1) % 2, n + 6 * i)
                ahead = hi if isinstance(i, int) else hi_loop
                a = (lambda k: (n + 6 * i + k + RING,)) if isinstance(i, int) else (lambda k: (n + k + RING, i))
                ahead(*a(0))
                glu_hi(c + 1, (j + 1) % 2)
                ahead(*a(1))
                ahead(*a(2))

            for j in range(2):
                glu_chunk(j, j, 0)
            with act.Fori(1, (GC - 1) // 2 - 1) as i:
                for j in range(2):
                    glu_chunk(2 * i + j, j, i)
            i = (GC - 1) // 2 - 1
            for j in range(2):
                glu_chunk(2 * i + j, j, i)
            squares_acc(5, PIECES - 1, ("pf0", "pf1"))

        @block.vector
        def _(dve):
            steps = [0]

            def step(ins):
                steps[0] += 1
                ins.then_inc(dve_step, 1)
                dve.wait_ge(dve_step, steps[0])

            def lo(n):
                if n >= PIECES:
                    return
                dve.wait_ge(hi_ready, n + 1)
                for dst, src, high in zip(views(n, w_lo, False), views(n, raw, True), views(n, w_hi, False)):
                    ins = dve.tensor_tensor(dst, src, high, ALU.subtract)
                ins.then_inc(lo_ready, 1)

            def lo_loop(n0, i):
                slot = n0 % RING
                dve.wait_ge(hi_ready, n0 + 1 + 6 * i)
                dve.tensor_tensor(w_lo[:, slot, :], raw[:, slot, :], w_hi[:, slot, :], ALU.subtract)\
                    .then_inc(lo_ready, 1)

            def turn(t):
                for q in range(T_BANKS[t]):
                    dve.wait_ge(h_hi_ready, t_base(t) + q + 1)
                    for k in range(2 * q, min(2 * q + 2, T_BLOCKS[t])):
                        g = gain(t, k)
                        ins = dve.scalar_tensor_tensor(
                            out=h_lo[:, k, :], in0=bank(4 + q)[:, (k % 2) * S:(k % 2 + 1) * S],
                            scalar=1.0 if g is None else g, in1=h_hi[:, k, :], op0=ALU.mult, op1=ALU.subtract)
                    ins.then_inc(h_lo_ready, 1)

            def rs(name, i=0):
                c = JOBS[name][0] + i
                return rstd[:, c:c + 1]

            def rs_wait(name):
                dve.wait_ge(rstd_ready, JOB_AT[name] + 1)

            def scaled(jobs):
                for tb in range(TB):
                    rs_wait(jobs[tb])
                    dve.tensor_scalar(xn[:, tb, :], x[:, tb, :], rs(jobs[tb]), None, ALU.mult).then_inc(xn_ready, 1)

            def acc_wait(stage, last, tb):
                if tb == 0:
                    dve.wait_ge(acc_half, stage + 1)
                else:
                    dve.wait_ge(piece_used, last + 1)

            def residual(stage, last):
                for tb in range(TB):
                    acc_wait(stage, last, tb)
                    dve.tensor_tensor(x[:, tb, :], x[:, tb, :], bank(2 * tb, 2), ALU.add).then_inc(x_ready, 1)

            step(dve.memset(qk_pad[:, :, 0:PAD], 0.0))
            step(dve.memset(qk_pad[:, :, PAD + S:], 0.0))
            step(dve.memset(v_ext[:, :, :, A_D:A_D + 1], 1.0))
            step(dve.memset(ones_row[0:A_H, :], 1.0))
            dve.wait_ge(x_loaded, 32)
            scaled(("ab0", "ab1"))
            dve.wait_ge(gw_hi_ready, 1)
            dve.tensor_tensor(gw_lo[:, :, :], gw_raw[:, :, :], gw_hi[:, :, :], ALU.subtract).then_inc(gw_ready, 1)
            dve.wait_ge(ident_ready, 1)
            step(dve.tensor_scalar(nsel[0:A_H, :, :],
                                   ident[0:A_H, 0:A_H].unsqueeze(2).to_broadcast([A_H, A_H, P]), -1.0, None, ALU.mult))
            lo(0)
            dve.wait_ge(cols_ready, 1)
            turn(T_AB)
            dve.wait_ge(pos_loaded, 16)
            dve.wait_ge(consts_ready, 3)
            step(dve.tensor_copy(pos_f[:, :], pos_i[:, :]))
            for tb in range(TB):
                step(dve.tensor_scalar(ang[:, tb, :], freq[:, :], pos_f[:, tb:tb + 1], None, ALU.mult))
            step(dve.tensor_scalar(turns[:, :, :], ang[:, :, :], 1.0 / TWO_PI, ROUND, ALU.mult, ALU.add))
            step(dve.tensor_scalar(turns[:, :, :], turns[:, :, :], -ROUND, None, ALU.add))
            for c in (PI_1, PI_2, PI_3):
                step(dve.scalar_tensor_tensor(out=ang[:, :, :], in0=turns[:, :, :], scalar=-c, in1=ang[:, :, :],
                                              op0=ALU.mult, op1=ALU.add))
            step(dve.tensor_scalar(ang2[:, 1, :, :], ang[:, :, :], PI_IN, -PI_IN, ALU.min, ALU.max))
            step(dve.tensor_scalar(ang[:, :, :], ang[:, :, :], math.pi / 2, None, ALU.add))
            step(dve.tensor_scalar(turns[:, :, :], ang[:, :, :], math.pi, -TWO_PI, ALU.is_gt, ALU.mult))
            step(dve.tensor_tensor(ang[:, :, :], ang[:, :, :], turns[:, :, :], ALU.add))
            dve.tensor_scalar(ang2[:, 0, :, :], ang[:, :, :], PI_IN, -PI_IN, ALU.min, ALU.max).then_inc(trig_in, 1)
            lo(1)
            lo(2)
            dve.wait_ge(gates_done, 1)
            for tb in range(TB):
                step(dve.tensor_tensor(gates[:, 2 * tb:2 * tb + 2, :],
                                       bank(7)[:, 16 * tb:16 * tb + 16].rearrange("p (a b) -> p a b", a=2),
                                       gb_row.rearrange("p (a b) -> p a b", a=2), ALU.add))
            fg = gates[:, :, A_H:2 * A_H]
            dve.scalar_tensor_tensor(out=g_abs[:, :, :], in0=fg, scalar=-1.0, in1=fg, op0=ALU.mult, op1=ALU.max)\
                .then_inc(gate_abs, 1)

            def conv(j):
                dve.wait_ge(evac_qk, j + 1)
                for b in (2 * j, 2 * j + 1):
                    step(dve.tensor_scalar(qk_conv[:, b, :], qk_pad[:, b, 0:S], col("ab_conv", b), None, ALU.mult))
                    for t in range(1, TAPS):
                        ins = dve.scalar_tensor_tensor(out=qk_conv[:, b, :], in0=qk_pad[:, b, t:t + S],
                                                       scalar=col("ab_conv", 8 * t + b), in1=qk_conv[:, b, :],
                                                       op0=ALU.mult, op1=ALU.add)
                        if t < TAPS - 1 or b == 2 * j:
                            step(ins)
                ins.then_inc(conv_done, 1)

            lo(3)
            conv(0)
            dve.wait_ge(gate_ln, 1)
            dve.scalar_tensor_tensor(out=fg, in0=fg, scalar=0.0, in1=g_ln[:, :, :], op0=ALU.min, op1=ALU.subtract)\
                .then_inc(gates_ready, 1)
            lo(4)
            conv(1)
            lo(5)
            conv(2)
            lo(6)
            conv(3)
            lo(7)
            lo(8)
            dve.wait_ge(rows_turned, 1)
            rows = bank(6, 2)[0:A_H, :].rearrange("p (d q t) -> p d q t", d=2, q=2)
            one = ones_row[0:A_H, :]
            step(dve.tensor_tensor_scan(cumf[0:A_H, 0, :], one, rows[:, 0, 1, :], 0.0, ALU.mult, ALU.add))
            step(dve.tensor_tensor_scan(cumf[0:A_H, 1, ::-1], one, rows[:, 1, 1, ::-1], 0.0, ALU.mult, ALU.add))
            step(dve.tensor_tensor(a_row[0:A_H, :, :], rows[:, :, 0, :], cumf[0:A_H, :, :], ALU.subtract))
            step(dve.tensor_tensor_scan(m_row[0:A_H, 0, :], a_row[0:A_H, 0, :], a_row[0:A_H, 0, :], 0.0,
                                        ALU.max, ALU.max))
            step(dve.tensor_tensor_scan(m_row[0:A_H, 1, ::-1], a_row[0:A_H, 1, ::-1], a_row[0:A_H, 1, ::-1], 0.0,
                                        ALU.max, ALU.max))
            dve.tensor_tensor(mt_row[0:A_H, :, :], cumf[0:A_H, :, :], m_row[0:A_H, :, :], ALU.add)\
                .then_inc(rows_ready, 1)
            dve.wait_ge(rel_loaded, 16)
            n0 = P
            n1 = n0 + N_REL - 1
            step(dve.tensor_copy(rel_ext[:, 0:n0], rel_t[:, N_REL - 1:N_REL].to_broadcast([H2, n0])))
            step(dve.tensor_copy(rel_ext[:, n0:n1], rel_t[:, N_REL - 2::-1]))
            dve.tensor_copy(rel_ext[:, n1:EXT], rel_t[:, 0:1].to_broadcast([H2, EXT - n1])).then_inc(rel_built, 1)
            for n in range(9, 15):
                lo(n)
            dve.wait_ge(evac_vb, 2)
            groups = vb[:, :, :].rearrange("p t (g c) -> p (t g) c", g=B_G)
            sq_g = sq_tmp[:, :, :].rearrange("p t (g c) -> p (t g) c", g=B_G)
            step(dve.tensor_tensor(sq_g, groups, groups, ALU.mult))
            c0 = JOBS["vb"][0]
            dve.tensor_reduce(ssq[:, c0:c0 + 8], sq_g, AX.X, ALU.add).then_inc(ss_dve, 1)

            def weigh(u):
                h, back = u // 2, u % 2
                dve.wait_ge(w_ready, u + 1)
                dve.wait_ge(s_ready, h + 1)
                src = bank(2 + h % 2)
                w = decay[:, u % 2, :, :].rearrange("p b t -> p (b t)")
                dst = score[:, u % 2, :, :].rearrange("p b t -> p (b t)")
                for c0, c1 in [((0, 256), (384, 512)), ((0, 128), (256, 512))][back]:
                    ins = dve.scalar_tensor_tensor(out=dst[:, c0:c1], in0=src[:, c0:c1], scalar=float(A_D) ** -0.5,
                                                   in1=w[:, c0:c1], op0=ALU.mult, op1=ALU.mult)
                ins.then_inc(g_ready, 1)

            def unit_out(u):
                h, back = u // 2, u % 2
                dve.wait_ge(o_ready, u + 1)
                o = bank(4 + u % 2)[:, 0:2 * (A_D + 1)].rearrange("p (t e) -> p t e", t=TB)
                at = back * A_H + h
                den = o[:, :, A_D]
                step(dve.tensor_tensor(dmax, den, e_col[:, :, at], ALU.max))
                step(dve.scalar_tensor_tensor(out=dmax, in0=den, scalar=-1.0, in1=dmax, op0=ALU.mult, op1=ALU.max))
                step(dve.reciprocal(dinv, dmax))
                for tb in range(TB):
                    dst = hsum[:, tb, h * A_D:(h + 1) * A_D]
                    if back:
                        ins = dve.scalar_tensor_tensor(out=dst, in0=o[:, tb, 0:A_D], scalar=dinv[:, tb:tb + 1],
                                                       in1=dst, op0=ALU.mult, op1=ALU.add)
                    else:
                        ins = dve.tensor_scalar(dst, o[:, tb, 0:A_D], dinv[:, tb:tb + 1], None, ALU.mult)
                    if tb == 0:
                        step(ins)
                ins.then_inc(unit_done, 1)
                dve.wait_ge(unit_done, u + 1)

            dve.wait_ge(gcols_ready, 2)
            for u in range(2 * A_H):
                weigh(u)
                if u == 2:
                    rs_wait("vb")
                    step(dve.tensor_tensor(groups, groups,
                                           rstd[:, c0:c0 + 8].unsqueeze(2).to_broadcast([P, 8, 128]), ALU.mult))
                    dve.tensor_tensor(vb[:, :, :], vb[:, :, :], vg_row.unsqueeze(1).to_broadcast([P, TB, B_W]),
                                      ALU.mult).then_inc(vbn_ready, 1)
                if u >= 1:
                    unit_out(u - 1)
            unit_out(2 * A_H - 1)
            heads = hsum[:, :, :].rearrange("p t (g c) -> p (t g) c", g=A_H)
            step(dve.tensor_tensor(sq_g, heads, heads, ALU.mult))
            c1 = JOBS["ha"][0]
            dve.tensor_reduce(ssq[:, c1:c1 + 8], sq_g, AX.X, ALU.add).then_inc(ss_dve, 1)
            dve.wait_ge(sgu_done, 1)
            for g in range(B_G):
                step(dve.scalar_tensor_tensor(
                    out=xn[:, :, A_W + g * 128:A_W + (g + 1) * 128],
                    in0=bank(6, 2)[:, g * S:(g + 1) * S].rearrange("p (n c) -> p n c", n=TB),
                    scalar=col("ab_bs", g), in1=u_act[:, :, g * 128:(g + 1) * 128], op0=ALU.add, op1=ALU.mult))
            rs_wait("ha")
            step(dve.tensor_tensor(heads, heads, rstd[:, c1:c1 + 8].unsqueeze(2).to_broadcast([P, 8, 128]), ALU.mult))
            for tb in range(TB):
                dve.tensor_tensor(xn[:, tb, 0:A_W], hsum[:, tb, :], oa[:, tb, :], ALU.mult).then_inc(xn_ready, 1)
            turn(T_AMIX)
            for j in range(4):
                lo(P_AOUT + j + RING)
            residual(0, P_AOUT + 3)

            def ffn(first, hb, t, jobs, stage):
                scaled(jobs)
                turn(t)

                def hidden(c, r):
                    dve.wait_ge(act_out, hb + c + 1)
                    dve.tensor_tensor(g_mul[:, r, :], g_act[:, r, :], g_act[:, r, :], ALU.mult).then_inc(mul_out, 1)
                    dve.wait_ge(mul_out, hb + c + 1)
                    dve.wait_ge(g_hi_ready, hb + c + 1)
                    dve.tensor_tensor(g_lo[:, r, :], g_mul[:, r, :], g_hi[:, r, :], ALU.subtract)\
                        .then_inc(g_lo_ready, 1)

                hidden(0, 0)
                lo(first + RING)

                def chunk(c, j, i):
                    n = first + 1 + 2 * j
                    hidden(c + 1, (j + 1) % 3)
                    if isinstance(i, int):
                        lo(n + 6 * i + RING)
                        lo(n + 6 * i + 1 + RING)
                    else:
                        lo_loop(n + RING, i)
                        lo_loop(n + 1 + RING, i)

                for j in range(3):
                    chunk(j, j, 0)
                with dve.Fori(1, (FC - 1) // 3) as i:
                    for j in range(3):
                        chunk(3 * i + j, j, i)
                lo(first + 2 * FC - 1 + RING)
                residual(stage, first + 2 * FC - 1)

            ffn(P_FFN0, 0, T_FFN0, ("ffn00", "ffn01"), 1)

            dve.memset(krr[:, :, 0:C_NOPE], 0.0).then_inc(krr_zero, 1)
            scaled(("c0", "c1"))
            turn(T_C)
            for j in range(2):
                lo(P_CIN + j + RING)
            dve.wait_ge(piece_used, P_CIN + 3)

            def rope(lo_half, hi_half, out_lo, out_hi, cos, sin, t):
                step(dve.tensor_tensor(t[0], lo_half, cos, ALU.mult))
                step(dve.tensor_tensor(t[1], hi_half, sin, ALU.mult))
                step(dve.tensor_tensor(t[2], lo_half, sin, ALU.mult))
                step(dve.tensor_tensor(t[3], hi_half, cos, ALU.mult))
                step(dve.tensor_tensor(out_lo, t[0], t[1], ALU.subtract))
                return dve.tensor_tensor(out_hi, t[2], t[3], ALU.add)

            for name, c0, w in (("cq", 0, Q_LORA), ("ckv", Q_LORA, KV_LORA)):
                rs_wait(name)
                if name == "cq":
                    dve.wait_ge(ss_act, SS_ACT.index("ckv") + 1)
                for tb in range(TB):
                    ins = dve.tensor_scalar(xn[:, tb, c0:c0 + w], bank(2 * tb, 2)[:, c0:c0 + w], rs(name, tb), None,
                                            ALU.mult)
                    if name == "ckv":
                        ins.then_inc(xn_ready, 1)
            kr = psum[:, :, :].rearrange("p (t b) c -> p t (b c)", b=2)[:, 0:TB, Q_LORA + KV_LORA:C_IN]
            dve.wait_ge(trig_ready, 1)
            rope(kr[:, :, 0:HALF], kr[:, :, HALF:], krr[:, :, C_NOPE:C_NOPE + HALF], krr[:, :, C_NOPE + HALF:],
                 trig[:, 0], trig[:, 1], rk).then_inc(krr_ready, 1)
            lo(P_CIN + 2 + RING)
            turn(T_LAT)
            for j in range(2):
                dve.wait_ge(piece_used, P_UKV + j + 1)
                b0 = (6, 2)[j]
                for tb in range(TB):
                    ins = dve.tensor_copy(v_tok[:, tb, j * 512:(j + 1) * 512], bank(b0 + tb))
                ins.then_inc(evac_vc, 1)
                dve.wait_ge(evac_k, j + 1)
                dve.tensor_copy(kfT[0:C_NOPE, 8 * j + 1:8 * j + 8:2, :],
                                bank((4, 0)[j], 2)[C_NOPE:P, :].rearrange("p (h t) -> p h t", h=4)).then_inc(evac_k2, 1)
                lo(P_UKV + j + RING)
            for j in range(3):
                lo(P_UQ + j + RING)
            dve.wait_ge(evac_q, 3)
            dve.wait_ge(turned, t_base(T_LAT) + 3)
            qv = q_tok[:, :, :].rearrange("p t (h e) -> p t h e", h=C_H)
            cs = [trig[:, i].unsqueeze(2).to_broadcast([P, TB, C_H, HALF]) for i in range(2)]
            for tb in range(TB):
                ins = rope(qv[:, tb, :, C_NOPE:C_NOPE + HALF], qv[:, tb, :, C_NOPE + HALF:],
                           qv[:, tb, :, C_NOPE:C_NOPE + HALF], qv[:, tb, :, C_NOPE + HALF:],
                           cs[0][:, tb], cs[1][:, tb], [t[:, tb] for t in rp])
                ins.then_inc(q_roped, 1)
            for n in range(0, 8, 2):
                dve.wait_ge(qf_turned, n + 1)
                dve.tensor_copy(qfT[0:C_QK, 2 * n:2 * n + 2, :],
                                bank(4 + n % 4)[0:C_QK, :].rearrange("p (h t) -> p h t", h=2)).then_inc(evac_k2, 1)

            def pt_out(h):
                dve.wait_ge(at_pt[0], h + 1)
                if h >= 2:
                    dve.wait_ge(at_pv[0], h - 1)
                dve.tensor_copy(probT[:, h % 2, :], bank(6 + h % 2)).then_inc(at_ptsb[0], 1)

            def head_max(h):
                dve.wait_ge(at_s[0], h + 1)
                dve.tensor_reduce(nmax[:, :, h], bank(4 + h % 2).rearrange("p (q k) -> p q k", q=2), AX.X, ALU.max,
                                  negate=True).then_inc(at_max[0], 1)

            for h in range(C_H + 1):
                if h < C_H:
                    head_max(h)
                if h >= 1:
                    pt_out(h - 1)

            def mixed(n_heads, hd, sums, inv, exped, pv):
                dve.wait_ge(exped, n_heads)
                step(dve.reciprocal(inv, sums))
                dve.wait_ge(pv, n_heads)
                for qb in range(TB):
                    dve.tensor_tensor(xn[:, qb, :].rearrange("p (h e) -> p h e", h=n_heads),
                                      bank(2 * qb, 2).rearrange("p (h e) -> p h e", h=n_heads),
                                      inv[:, qb, :].unsqueeze(2).to_broadcast([P, n_heads, hd]), ALU.mult)\
                        .then_inc(xn_ready, 1)

            mixed(C_H, C_V, psm, pinv, at_exp[0], at_pv[0])
            turn(T_CMIX)
            for j in range(4):
                lo(P_COUT + j + RING)
            residual(2, P_COUT + 3)
            ffn(P_FFN1, FC, T_FFN1, ("ffn10", "ffn11"), 3)

            dve.wait_ge(rows2_loaded, 48)
            for tb in range(TB):
                job = f"fin{tb}"
                rs_wait(job)
                dve.scalar_tensor_tensor(out=x[:, tb, :], in0=x[:, tb, :], scalar=rs(job), in1=fin_row,
                                         op0=ALU.mult, op1=ALU.mult).then_inc(x_ready, 1)
            dve.wait_ge(x_ready, X_AT["pre"] + 2)
            scaled(("pre0", "pre1"))
            turn(T_2)
            for j in range(12):
                lo(P_QK2 + j + RING)
            dve.wait_ge(bias_ready, 1)

            def bias_max(h):
                dve.wait_ge(at_s[1], h + 1)
                if h >= 2:
                    dve.wait_ge(at_exp[1], h - 1)
                for qb, (c0, c1, k0) in enumerate(((0, P, P), (P, 3 * P, 0))):
                    ins = dve.tensor_tensor_reduce(s2[:, h % 2, c0:c1], bank(4 + h % 2)[:, c0:c1],
                                                   bias2[:, h, k0:S], -1.0, -NEG, ALU.add, ALU.min,
                                                   nmax2[:, qb, h:h + 1])
                ins.then_inc(at_max[1], 1)

            for h in range(H2):
                bias_max(h)
            mixed(H2, HD2, psm2, pinv2, at_exp[1], at_pv[1])
            turn(T_2MIX)
            for j in range(4):
                lo(P_O2 + j + RING)

            def post_norm(stage, last, jobs, row):
                for tb in range(TB):
                    rs_wait(jobs[tb])
                    step(dve.scalar_tensor_tensor(out=xn[:, tb, :], in0=bank(2 * tb, 2), scalar=rs(jobs[tb]),
                                                  in1=row, op0=ALU.mult, op1=ALU.mult))
                    dve.tensor_tensor(x[:, tb, :], x[:, tb, :], xn[:, tb, :], ALU.add).then_inc(x_ready, 1)

            post_norm(4, P_O2 + 3, ("pm0", "pm1"), pm_row)
            dve.wait_ge(x_ready, X_AT["glu"] + 2)
            scaled(("glu0", "glu1"))
            turn(T_GLU)
            hb, first = 2 * FC, P_GLU

            def glu_mul(c, r, n_up):
                dve.wait_ge(act_out, hb + c + 1)
                dve.wait_ge(piece_used, n_up + 1)
                dve.tensor_tensor(g_mul[:, r, :], g_act[:, r, :], bank(5 + 2 * r), ALU.mult).then_inc(mul_out, 1)

            def glu_lo(c, r):
                dve.wait_ge(g_hi_ready, hb + c + 1)
                dve.tensor_tensor(g_lo[:, r, :], g_mul[:, r, :], g_hi[:, r, :], ALU.subtract).then_inc(g_lo_ready, 1)

            lo(first + RING)
            glu_mul(0, 0, first + 1)
            glu_lo(0, 0)
            lo(first + 1 + RING)

            def glu_chunk(c, j, i):
                n = first + 2 + 3 * j
                r = (j + 1) % 2
                ahead = lo if isinstance(i, int) else lo_loop
                a = (lambda k: (n + 6 * i + k + RING,)) if isinstance(i, int) else (lambda k: (n + k + RING, i))
                ahead(*a(0))
                glu_mul(c + 1, r, n + 1 + 6 * i)
                glu_lo(c + 1, r)
                ahead(*a(1))
                ahead(*a(2))

            for j in range(2):
                glu_chunk(j, j, 0)
            with dve.Fori(1, (GC - 1) // 2 - 1) as i:
                for j in range(2):
                    glu_chunk(2 * i + j, j, i)
            i = (GC - 1) // 2 - 1
            for j in range(2):
                glu_chunk(2 * i + j, j, i)
            post_norm(5, PIECES - 1, ("pf0", "pf1"), pf_row)

        @block.tensor
        def _(pe):
            def product(dst, stat, mov, first, last):
                pe.matmul(dst, stat[0], mov[0], start=first, stop=False)
                pe.matmul(dst, stat[0], mov[1], start=False, stop=False)
                return pe.matmul(dst, stat[1], mov[0], start=False, stop=last)

            def h_block(k, tb=None):
                if tb is None:
                    return h_hi[:, k, :], h_lo[:, k, :]
                return h_hi[:, k, tb * P:(tb + 1) * P], h_lo[:, k, tb * P:(tb + 1) * P]

            def split(n):
                pe.wait_ge(lo_ready, n + 1)

            def turn(t, n_ready):
                for tb in range(TB):
                    pe.wait_ge(xn_ready, n_ready + tb + 1)
                    for k in range(T_BLOCKS[t]):
                        at = (k % 2) * S + tb * P
                        ins = pe.transpose(bank(4 + k // 2)[:, at:at + P], xn[:, tb, k * P:(k + 1) * P], ident[:, :])
                        if tb == TB - 1 and (k % 2 or k == T_BLOCKS[t] - 1):
                            ins.then_inc(turned, 1)

            def h_wait(t, k):
                pe.wait_ge(h_lo_ready, t_base(t) + k // 2 + 1)

            def stationary(n, t, b, first_use, slot=None, signal=True):
                s = n % RING if slot is None else slot
                wh = w_hi[:, s, :].rearrange("p (k c) -> p k c", k=KB)
                wl = w_lo[:, s, :].rearrange("p (k c) -> p k c", k=KB)
                for f in range(2):
                    for k in range(KB):
                        if first_use and f == 0 and k % 2 == 0:
                            h_wait(t, k)
                        ins = product(bank(b)[:, f * S:(f + 1) * S],
                                      (wh[:, k, f * P:(f + 1) * P], wl[:, k, f * P:(f + 1) * P]),
                                      h_block(k), k == 0, k == KB - 1)
                ins.then_inc(piece_used, 1)

            def moving(first, banks):
                for j in range(2):
                    split(first + j)
                    wh, wl = part(w_hi, first + j, 4), part(w_lo, first + j, 4)
                    for tb in range(TB):
                        for k in range(4):
                            ins = product(bank(banks[tb]), h_block(4 * j + k, tb), (wh[:, k, :], wl[:, k, :]),
                                          j == 0 and k == 0, j == 1 and k == 3)
                    ins.then_inc(piece_used, 1)

            def out_piece(act_of, n_slot, first, last):
                wh = w_hi[:, n_slot, :].rearrange("p (k c) -> p k c", k=2)
                wl = w_lo[:, n_slot, :].rearrange("p (k c) -> p k c", k=2)
                for tb in range(TB):
                    for k in range(2):
                        for h in range(2):
                            ins = product(bank(2 * tb + h), act_of(k, tb),
                                          (wh[:, k, h * 512:(h + 1) * 512], wl[:, k, h * 512:(h + 1) * 512]),
                                          first and k == 0, last and k == 1)
                    if last and tb == 0:
                        ins.then_inc(acc_half, 1)
                ins.then_inc(piece_used, 1)

            def out_product(first, t):
                for j in range(4):
                    split(first + j)
                    h_wait(t, 2 * j)
                    out_piece(lambda k, tb: h_block(2 * j + k, tb), (first + j) % RING, j == 0, j == 3)

            pe.wait_ge(ident_ready, 1)
            pe.wait_ge(vecs_loaded, 16 * len(VEC))
            pe.transpose(bank(0)[:, 0:VECS], vecs[:, :], ident[0:VECS, 0:VECS]).then_inc(vecs_turned, 1)
            pe.wait_ge(ws_loaded, 16)
            for g in range(B_G):
                ins = pe.transpose(bank(1)[:, g * P:(g + 1) * P], ws_raw[:, g, :], ident[:, :])
            ins.then_inc(vecs_turned, 1)
            turn(T_AB, 0)
            pe.wait_ge(gw_ready, 1)
            h_wait(T_AB, KB - 1)
            for tb in range(TB):
                for k in range(KB):
                    ins = product(bank(7)[:, 16 * tb:16 * tb + 16], h_block(k, tb), (gw_hi[:, k, :], gw_lo[:, k, :]),
                                  k == 0, k == KB - 1)
            ins.then_inc(gates_done, 1)
            pe.wait_ge(cols_ready, 2)
            for j in range(4):
                split(P_QK + j)
                stationary(P_QK + j, T_AB, j, False)
            moving(P_VA, (4, 5))
            pe.wait_ge(gates_ready, 1)
            for dq in range(4):
                for tb in range(TB):
                    at = dq * S + tb * P
                    src = gates[:, 2 * tb + dq // 2, (dq % 2) * A_H:(dq % 2 + 1) * A_H]
                    ins = pe.transpose(bank(6, 2)[0:A_H, at:at + P], src, ident[:, :])
            ins.then_inc(rows_turned, 1)
            pe.wait_ge(evac_qk, 2)
            moving(P_OA, (0, 1))
            pe.wait_ge(evac_qk, 4)
            moving(P_U, (2, 3))
            pe.wait_ge(rows_ready, 1)
            for q, rows in enumerate((a_row, mt_row)):
                for tb in range(TB):
                    for back in range(2):
                        at = 16 * q + 8 * tb + A_H * back
                        ins = pe.transpose(bank(6)[:, at:at + A_H], rows[0:A_H, back, tb * P:(tb + 1) * P],
                                           ident[0:A_H, 0:A_H])
            ins.then_inc(cols_turned, 1)
            pe.wait_ge(evac_v, 2)
            moving(P_VB, (4, 5))

            def spread_m(u):
                h, back = u // 2, u % 2
                if u == 0:
                    pe.wait_ge(evac_oa, 2)
                    pe.wait_ge(consts_ready, 3)
                if u >= 2:
                    pe.wait_ge(w_ready, u - 1)
                b = bank(u % 2)
                whole, half = (((0, 256), (384, 512)), ((256, 512), (0, 128)))[back]
                m = m_row[0:A_H, back, :]
                msk = mask[:, back, :]
                pe.matmul(b[:, whole[0]:whole[1]], nsel[0:A_H, h, :], m, start=True, stop=False)
                wd = whole[0] + (P if back else 0)
                pe.matmul(b[:, wd:wd + P], ident[:, :], msk, start=False, stop=True)
                pe.matmul(b[:, half[0]:half[1]], nsel[0:A_H, h, :], m[:, P:S] if not back else m[:, 0:P],
                          start=True, stop=False)
                pe.matmul(b[:, half[0]:half[1]], ident[:, :], msk, start=False, stop=True).then_inc(spread, 1)

            def head_scores(h):
                if h == 0:
                    pe.wait_ge(silu_done, 4)
                    pe.wait_ge(evac_u, 2)
                if h >= 2:
                    pe.wait_ge(g_ready, 2 * h - 2)
                for s0 in range(2):
                    ins = pe.matmul(bank(2 + h % 2)[:, s0 * S:(s0 + 1) * S], qkT[:, 4 + h, s0 * P:(s0 + 1) * P],
                                    qkT[:, h, :], start=True, stop=True)
                ins.then_inc(s_ready, 1)

            def unit_pv(u):
                h, back = u // 2, u % 2
                if u == 0:
                    pe.wait_ge(evac_vb, 2)
                pe.wait_ge(g_ready, u + 1)
                if u >= 2:
                    pe.wait_ge(unit_done, u - 1)
                for t0, sources in enumerate([((0,), (0, 1)), ((0, 1), (1,))][back]):
                    for s0 in sources:
                        ins = pe.matmul(bank(4 + u % 2)[:, t0 * (A_D + 1):(t0 + 1) * (A_D + 1)],
                                        score[:, u % 2, 2 * s0 + t0, :], v_ext[:, s0, h, :],
                                        start=s0 == sources[0], stop=s0 == sources[-1])
                ins.then_inc(o_ready, 1)

            spread_m(0)
            head_scores(0)
            spread_m(1)
            for u in range(2 * A_H):
                if u + 2 < 2 * A_H:
                    spread_m(u + 2)
                if u % 2 == 1 and u // 2 + 1 < A_H:
                    head_scores(u // 2 + 1)
                unit_pv(u)
                if u == 4:
                    pe.wait_ge(vbn_ready, 1)
                    pe.wait_ge(gcols_ready, 2)
                    for g in range(B_G):
                        ins = pe.matmul(bank(6, 2)[:, g * S:(g + 1) * S].rearrange("p (n c) -> p n c", n=TB),
                                        wsT[:, g, :], vb[:, :, g * 128:(g + 1) * 128], start=True, stop=True)
                    ins.then_inc(sgu_done, 1)
            turn(T_AMIX, 2)
            out_product(P_AOUT, T_AMIX)

            def ffn(first, hb, t, n_ready):
                turn(t, n_ready)
                split(first)
                stationary(first, t, 4, True)

                def chunk(c, j, i):
                    n = first + 1 + 2 * j
                    r1 = (j + 1) % 3
                    split(n + 6 * i)
                    if not (isinstance(c, int) and c < 2):
                        pe.wait_ge(act_out, hb + c - 1)
                    stationary(None, t, 4 + r1, False, slot=n % RING)
                    split(n + 1 + 6 * i)
                    pe.wait_ge(g_lo_ready, hb + c + 1)
                    down(j % 3, (n + 1) % RING, isinstance(c, int) and c == 0, False)

                def down(r, slot, start, stop):
                    out_piece(lambda k, tb: (g_hi[:, r, k * S + tb * P:k * S + (tb + 1) * P],
                                             g_lo[:, r, k * S + tb * P:k * S + (tb + 1) * P]), slot, start, stop)

                for j in range(3):
                    chunk(j, j, 0)
                with pe.Fori(1, (FC - 1) // 3) as i:
                    for j in range(3):
                        chunk(3 * i + j, j, i)
                n = first + 2 * FC - 1
                split(n)
                pe.wait_ge(g_lo_ready, hb + FC)
                down((FC - 1) % 3, n % RING, False, True)

            ffn(P_FFN0, 0, T_FFN0, 4)

            turn(T_C, 6)
            for j, (k0, k1) in enumerate(((0, 3), (3, 6), (6, 8))):
                n = P_CIN + j
                split(n)
                wh, wl = part(w_hi, n, k1 - k0), part(w_lo, n, k1 - k0)
                for tb in range(TB):
                    for k in range(k0, k1):
                        if tb == 0:
                            h_wait(T_C, k)
                        for c0, c1 in ((0, 512), (512, C_IN)):
                            ins = product(bank(2 * tb, 2)[:, c0:c1], h_block(k, tb),
                                          (wh[:, k - k0, c0:c1], wl[:, k - k0, c0:c1]), k == 0, k == KB - 1)
                ins.then_inc(piece_used, 1)
            turn(T_LAT, 8)
            pe.wait_ge(krr_ready, 1)
            pe.wait_ge(krr_zero, 1)
            pe.wait_ge(h_lo_ready, t_base(T_C) + 4)
            for tb in range(TB):
                ins = pe.transpose(psum[0:C_QK, 7, tb * P:(tb + 1) * P], krr[:, tb, :], ident[:, :])
            ins.then_inc(krr_turned, 1)
            h_wait(T_LAT, 4)
            for j in range(2):
                n = P_UKV + j
                split(n)
                if j == 0:
                    pe.wait_ge(krT_ready, 1)
                wh, wl = part(w_hi, n, 2), part(w_lo, n, 2)
                for pair in range(4):
                    hs = slice(pair * P, (pair + 1) * P)
                    for k in range(2):
                        product(bank((4, 0)[j], 2)[:, pair * S:(pair + 1) * S],
                                (wh[:, k, hs], wl[:, k, hs]), h_block(3 + k), k == 0, k == 1)
                for tb in range(TB):
                    for k in range(2):
                        ins = product(bank((6, 2)[j] + tb), h_block(3 + k, tb), (wh[:, k, 512:], wl[:, k, 512:]),
                                      k == 0, k == 1)
                ins.then_inc(piece_used, 1)
            for j in range(3):
                n = P_UQ + j
                split(n)
                pe.wait_ge(evac_k2, (1, 1, 2)[j])
                pe.wait_ge(evac_vc, (1, 1, 2)[j])
                wh, wl = part(w_hi, n, 3), part(w_lo, n, 3)
                for tb in range(TB):
                    for k in range(3):
                        ins = product(bank((4, 6, 0)[j] + tb), h_block(k, tb), (wh[:, k, :], wl[:, k, :]),
                                      k == 0, k == 2)
                ins.then_inc(piece_used, 1)
            pe.wait_ge(q_roped, 2)
            for n in range(8):
                if n >= 4:
                    if n % 2:
                        pe.wait_ge(qf_ready, (n - 4) // 2 + 1)
                    else:
                        pe.wait_ge(evac_k2, 2 + (n - 4) // 2 + 1)
                for i in range(2):
                    h = 2 * n + i
                    for tb in range(TB):
                        at = i * S + tb * P
                        ins = pe.transpose(bank(4 + n % 4)[0:C_QK, at:at + P],
                                           q_tok[:, tb, h * C_QK:(h + 1) * C_QK], ident[:, :])
                ins.then_inc(qf_turned, 1)
            pe.wait_ge(qf_ready, 4)
            pe.wait_ge(evac_k2, 6)
            pe.wait_ge(kfT_rope, 1)

            def c_scores(h):
                if h >= 2:
                    pe.wait_ge(at_exp[0], h - 1)
                for qb in range(2):
                    ins = pe.matmul(bank(4 + h % 2)[:, qb * S:(qb + 1) * S], qfT[0:C_QK, h, qb * P:(qb + 1) * P],
                                    kfT[0:C_QK, h, :], start=True, stop=True)
                ins.then_inc(at_s[0], 1)

            def c_turn(h):
                pe.wait_ge(at_exp[0], h + 1)
                if h >= 2:
                    pe.wait_ge(at_ptsb[0], h - 1)
                for kb in range(2):
                    for qb in range(2):
                        at = kb * S + qb * P
                        ins = pe.transpose(bank(6 + h % 2)[:, at:at + P],
                                           prob[:, h % 2, qb * S + kb * P:qb * S + (kb + 1) * P], ident[:, :])
                ins.then_inc(at_pt[0], 1)

            def c_pv(h):
                pe.wait_ge(at_ptsb[0], h + 1)
                for qb in range(2):
                    for kb in range(2):
                        ins = pe.matmul(bank(2 * qb, 2)[:, h * C_V:(h + 1) * C_V],
                                        probT[:, h % 2, kb * S + qb * P:kb * S + (qb + 1) * P],
                                        v_tok[:, kb, h * C_V:(h + 1) * C_V], start=kb == 0, stop=kb == 1)
                ins.then_inc(at_pv[0], 1)

            def pipeline(n, *stages):
                for i in range(n + len(stages) - 1):
                    for lag, stage in enumerate(stages):
                        if 0 <= i - lag < n:
                            stage(i - lag)

            pipeline(C_H, c_scores, c_turn, c_pv)
            turn(T_CMIX, 10)
            out_product(P_COUT, T_CMIX)
            ffn(P_FFN1, FC, T_FFN1, 12)

            turn(T_2, 14)
            for j in range(8):
                split(P_QK2 + j)
                if j == 0:
                    h_wait(T_2, KB - 1)
                stationary(P_QK2 + j, T_2, j, False)
            for n in range(2):
                pe.wait_ge(evac_qk2, 2 * n + 2)
                moving(P_V2 + 2 * n, (2 * n, 2 * n + 1))
            pe.wait_ge(evac_v2, 4)
            pe.wait_ge(evac_qk2, 8)

            def scores2(h):
                if h >= 2:
                    pe.wait_ge(at_max[1], h - 1)
                rows = slice(HD2 * (h % 2), HD2 * (h % 2 + 1))
                for qb, (c0, c1) in enumerate(((0, P), (P, 3 * P))):
                    ins = pe.matmul(bank(4 + h % 2)[:, c0:c1], qT2[rows, h // 2, qb * P:(qb + 1) * P],
                                    kT2[rows, h // 2, 0:c1 - c0], start=True, stop=True)
                ins.then_inc(at_s[1], 1)

            def turn2(h):
                pe.wait_ge(at_exp[1], h + 1)
                if h >= 2:
                    pe.wait_ge(at_ptsb[1], h - 1)
                for b in range(3):
                    ins = pe.transpose(bank(6 + h % 2)[:, b * P:(b + 1) * P], prob2[:, h % 2, b * P:(b + 1) * P],
                                       ident[:, :])
                ins.then_inc(at_pt[1], 1)

            def pv2(h):
                pe.wait_ge(at_ptsb[1], h + 1)
                for qb, blocks in enumerate((((0, 0),), ((1, 0), (2, 1)))):
                    for b, kb in blocks:
                        ins = pe.matmul(bank(2 * qb, 2)[:, h * HD2:(h + 1) * HD2], probT2[:, h % 2, b * P:(b + 1) * P],
                                        v2[:, kb, h * HD2:(h + 1) * HD2], start=kb == 0, stop=kb == qb)
                ins.then_inc(at_pv[1], 1)

            pipeline(H2, scores2, turn2, pv2)
            turn(T_2MIX, 16)
            out_product(P_O2, T_2MIX)

            turn(T_GLU, 18)
            hb, first = 2 * FC, P_GLU

            def gate_up(c, r, n0, i, first_use):
                split(n0 + 6 * i)
                if not (isinstance(c, int) and c < 2):
                    pe.wait_ge(act_out, hb + c - 1)
                stationary(None, T_GLU, 4 + 2 * r, first_use, slot=n0 % RING)
                split(n0 + 1 + 6 * i)
                if not (isinstance(c, int) and c < 2):
                    pe.wait_ge(mul_out, hb + c - 1)
                stationary(None, T_GLU, 5 + 2 * r, False, slot=(n0 + 1) % RING)

            def glu_down(c, r, n0, i, start, stop):
                split(n0 + 6 * i)
                pe.wait_ge(g_lo_ready, hb + c + 1)
                out_piece(lambda k, tb: (g_hi[:, r, k * S + tb * P:k * S + (tb + 1) * P],
                                         g_lo[:, r, k * S + tb * P:k * S + (tb + 1) * P]), n0 % RING, start, stop)

            gate_up(0, 0, first, 0, True)

            def glu_chunk(c, j, i):
                n = first + 2 + 3 * j
                gate_up(c + 1, (j + 1) % 2, n, i, False)
                glu_down(c, j % 2, n + 2, i, isinstance(c, int) and c == 0, False)

            for j in range(2):
                glu_chunk(j, j, 0)
            with pe.Fori(1, (GC - 1) // 2) as i:
                for j in range(2):
                    glu_chunk(2 * i + j, j, i)
            glu_down(GC - 1, (GC - 1) % 2, PIECES - 1, 0, False, True)


_INS = ["x", "positions", "ab_norm", "ab_w_in", "ab_conv", "ab_gate_b", "ab_head_g", "ab_v_g", "ab_ws", "ab_bs",
        "ab_w_out", "c_norm", "c_w_in", "c_q_g", "c_kv_g", "c_w_uq", "c_w_ukv", "c_w_out", "ffn_norm", "ffn_w1",
        "ffn_w2", "final_norm", "g_pre_mix_2", "g_post_mix_2", "w_qkv_2", "w_o_2", "rel_bias_2", "g_pre_ffn_2",
        "g_post_ffn_2", "w_gate_2", "w_up_2", "w_down_2"]


def kernel(**inputs):
    import numpy as _np
    import concourse.bacc as _bacc
    from concourse import mybir as _mybir
    from concourse.bass_utils import run_bass_kernel_spmd as _run

    nc = _bacc.Bacc("TRN2", target_bir_lowering=False, num_devices=1)
    arrays, d = {}, {}
    for name in _INS:
        a = _np.ascontiguousarray(inputs[name])
        arrays[f"in_{name}"] = a
        d[name] = nc.dram_tensor(f"in_{name}", a.shape, _mybir.dt.from_np(a.dtype), kind="ExternalInput").ap()
    out = nc.dram_tensor("out", (1, S, D), _mybir.dt.float32, kind="ExternalOutput").ap()
    build(nc, d, out)
    r = _run(nc, [arrays], core_ids=[0])
    return r.results[0]["out"]
```

```python
import math
from contextlib import ExitStack

import concourse.bass as bass
import numpy as np
from concourse import mybir

F32 = mybir.dt.float32
F32R = mybir.dt.float32r
I32 = mybir.dt.int32
ALU = mybir.AluOpType
ACT = mybir.ActivationFunctionType
AX = mybir.AxisListType

P = 128
D = 1024
KB = D // P
S = 256
TB = S // P
PIECE = 2048
RING = 3
EPS = 1e-6
NEG = -1.0e30

A_W, A_H, A_D, TAPS = 512, 4, 128, 5
PAD = (TAPS - 1) // 2
B_W, B_G = 512, 4
C_H, C_NOPE, C_ROPE, C_V = 16, 64, 32, 64
C_QK = C_NOPE + C_ROPE
HALF = C_ROPE // 2
Q_LORA, KV_LORA = 384, 256
C_IN = Q_LORA + KV_LORA + C_ROPE
CH = 256
D_FF = 4096
FC = D_FF // CH
H2, HD2, CHUNK = 16, 64, 64
REL_CLIP = 128
N_REL = CHUNK - 1 + REL_CLIP + 1
EXT = 384
D_FF2 = 2816
GC = D_FF2 // CH

P_QK, P_VA, P_VB, P_OA, P_U, P_AOUT = 0, 4, 6, 8, 10, 12
P_FFN0 = 16
P_CIN = P_FFN0 + 2 * FC
P_UQ = P_CIN + 3
P_UKV = P_UQ + 3
P_COUT = P_UKV + 2
P_FFN1 = P_COUT + 4
P_V2 = P_FFN1 + 2 * FC
P_QK2 = P_V2 + 4
P_O2 = P_QK2 + 8
P_GLU = P_O2 + 4
PIECES = P_GLU + 3 * GC

QK_ORDER = (0, 2, 1, 3)

T_AB, T_AMIX, T_FFN0, T_C, T_LAT, T_CMIX, T_FFN1, T_2, T_2MIX, T_GLU = range(10)
T_BANKS = [4, 4, 4, 4, 3, 4, 4, 4, 4, 4]
T_BLOCKS = [8, 8, 8, 8, 5, 8, 8, 8, 8, 8]

VEC = {"ab_norm": 0, "ab_head_g": 8, "ab_bs": 12, "c_norm": 16, "c_q_g": 24, "c_kv_g": 27,
       "ffn_norm": 29, "g_pre_mix_2": 45, "g_pre_ffn_2": 53, "final_norm": 61, "ab_conv": 69}
VECS = 69 + TAPS * KB

JOBS = {}
for _name, _n, _w in [("ab0", 1, D), ("ab1", 1, D), ("vb", 8, 128), ("ha", 8, 128), ("ffn00", 1, D), ("ffn01", 1, D),
                      ("c0", 1, D), ("c1", 1, D), ("cq", 2, Q_LORA), ("ckv", 2, KV_LORA), ("ffn10", 1, D),
                      ("ffn11", 1, D), ("fin0", 1, D), ("fin1", 1, D), ("pre0", 1, D), ("pre1", 1, D),
                      ("pm0", 1, D), ("pm1", 1, D), ("glu0", 1, D), ("glu1", 1, D), ("pf0", 1, D), ("pf1", 1, D)]:
    JOBS[_name] = (sum(v[1] for v in JOBS.values()), _n, _w)
JOB_AT = {name: i for i, name in enumerate(JOBS)}
SS_ACT = ["ab0", "ab1", "ffn00", "ffn01", "c0", "c1", "cq0", "cq", "ckv0", "ckv", "ffn10", "ffn11", "fin0", "fin1",
          "pre0", "pre1", "pm0", "pm1", "glu0", "glu1", "pf0", "pf1"]
SQUARED = ("ffn00", "ffn01", "ffn10", "ffn11")
SS_DVE = ["vb", "ha"]
X_AT = {"ffn0": 0, "c": 4, "ffn1": 8, "fin": 12, "pre": 16, "glu": 20, "out": 24}
XN_AT = {T_AB: 0, T_AMIX: 2, T_LAT: 4, T_CMIX: 6, T_2MIX: 10}

TWO_PI = 2 * math.pi
PI_1 = 6.28125
PI_2 = float(np.float32(round((TWO_PI - PI_1) * 2 ** 20) / 2 ** 20))
PI_3 = TWO_PI - PI_1 - PI_2
ROUND = 1.5 * 2.0 ** 23
PI_IN = 3.1415925


def build(nc, d, out):
    ctx = ExitStack()
    with ctx:
        def sb(name, shape, dt=F32):
            return ctx.enter_context(nc.sbuf_tensor(name, shape, dt))

        def sem(name):
            return ctx.enter_context(nc.semaphore(name))

        psum = ctx.enter_context(nc.psum_tensor("psum", [P, 8, 512], F32))
        raw = sb("raw", [P, RING, PIECE])
        w_hi = sb("w_hi", [P, RING, PIECE], F32R)
        w_lo = sb("w_lo", [P, RING, PIECE], F32R)
        x = sb("x", [P, TB, D])
        xn = sb("xn", [P, TB, D])
        h_hi = sb("h_hi", [P, KB, S], F32R)
        h_lo = sb("h_lo", [P, KB, S], F32R)
        junk = sb("junk", [P, D])
        g_act = sb("g_act", [P, 3, 2 * S])
        g_mul = sb("g_mul", [P, 3, 2 * S])
        g_hi = sb("g_hi", [P, 3, 2 * S], F32R)
        g_lo = sb("g_lo", [P, 3, 2 * S], F32R)
        ident = sb("ident", [P, P])
        mask = sb("mask", [P, 2, P])
        vecs = sb("vecs", [VECS, P])
        cols = sb("cols", [P, VECS])
        mhalf = sb("mhalf", [P, 8])
        mone = sb("mone", [P, 1])
        ones = sb("ones", [P, P])
        diag = sb("diag", [P, TB, P])
        r_row = sb("r_row", [P, S])
        gain2 = sb("gain2", [P, KB])
        r_both = sb("r_both", [P, TB])
        n_stat = sum(v[1] for v in JOBS.values())
        ssq = sb("ssq", [P, n_stat])
        msq = sb("msq", [P, n_stat])
        rstd = sb("rstd", [P, n_stat])
        pos_i = sb("pos_i", [P, TB], I32)
        pos_f = sb("pos_f", [P, TB])
        freq = sb("freq", [P, HALF])
        ang = sb("ang", [P, TB, HALF])
        turns = sb("turns", [P, TB, HALF])
        ang2 = sb("ang2", [P, 2, TB, HALF])
        trig = sb("trig", [P, 2, TB, HALF])
        rel_t = sb("rel_t", [H2, N_REL])
        rel_ext = sb("rel_ext", [H2, EXT])
        rel_dram = nc.dram_tensor("rel_scratch", (H2, P, EXT), F32, kind="Internal")

        ARENA = 16640
        arena = sb("arena", [P, ARENA])

        class Carve:
            def __init__(self):
                self.at = 0

            def __call__(self, *shape):
                n = int(np.prod(shape))
                assert self.at + n <= ARENA, (self.at, n)
                v = arena[:, self.at:self.at + n]
                self.at += n
                if len(shape) == 2:
                    v = v.rearrange("p (a b) -> p a b", a=shape[0])
                if len(shape) == 3:
                    v = v.rearrange("p (a b c) -> p a b c", a=shape[0], b=shape[1])
                return v

        ca = Carve()
        qk_pad = ca(8, S + 2 * PAD)
        qk_conv = ca(8, S)
        qkT = qk_conv
        v_ext = ca(TB, A_H, A_D + 1)
        oa = ca(TB, A_W)
        u_act = ca(TB, B_W)
        vb = ca(TB, B_W)
        sq_tmp = ca(TB, A_W)
        hsum = ca(TB, A_W)
        decay = g_act[:, 0:2, :].rearrange("p u (b t) -> p u b t", b=4)
        score = g_mul[:, 0:2, :].rearrange("p u (b t) -> p u b t", b=4)
        ws_raw = g_act[:, 2, :].rearrange("p (g t) -> p g t", g=B_G)
        wsT = ca(B_G, P)
        vg_row = ca(B_W)
        gw_raw = ca(KB, 16)
        gb_row = ca(16)
        gates = ca(4, 8)
        g_abs = ca(4, 4)
        g_exp = ca(4, 4)
        g_ln = ca(4, 4)
        cumf = ca(2, S)
        a_row = ca(2, S)
        m_row = ca(2, S)
        mt_row = ca(2, S)
        ones_row = ca(S)
        nsel = ca(A_H, P)
        a_col = ca(TB, 8)
        e_col = ca(TB, 8)
        dmax = ca(2)
        dinv = ca(2)
        gw_hi = sb("gw_hi", [P, KB, 16], F32R)
        gw_lo = sb("gw_lo", [P, KB, 16], F32R)

        cc = Carve()
        q_tok = cc(TB, C_H * C_QK)
        kfT = cc(C_H, S)
        qfT = cc(C_H, S)
        v_tok = cc(TB, D)
        prob = cc(2, 2 * S)
        probT = cc(2, 2 * S)
        krr = cc(TB, C_QK)
        krs = cc(TB, C_ROPE)
        krT = cc(S)
        nmax = cc(2, C_H)
        psm = cc(2, C_H)
        pinv = cc(2, C_H)
        rp = [xn[:, :, i * S:(i + 1) * S].rearrange("p t (h e) -> p t h e", h=C_H) for i in range(4)]
        rk = [junk[:, i * 32:(i + 1) * 32].rearrange("p (t e) -> p t e", t=TB) for i in range(4)]

        c2 = Carve()
        qT2 = c2(8, S)
        kT2 = c2(8, S)
        v2 = c2(TB, D)
        s2 = c2(2, 3 * P)
        prob2 = c2(2, 3 * P)
        probT2 = c2(2, 3 * P)
        nmax2 = c2(2, H2)
        psm2 = c2(2, H2)
        pinv2 = c2(2, H2)
        bias2 = c2(H2, S)
        fin_row = c2(D)
        pm_row = c2(D)
        pf_row = c2(D)

        arrived = [sem(f"arrived{i}") for i in range(RING)]
        hi_ready = sem("hi_ready")
        lo_ready = sem("lo_ready")
        piece_used = sem("piece_used")
        x_loaded = sem("x_loaded")
        vecs_loaded = sem("vecs_loaded")
        ws_loaded = sem("ws_loaded")
        ab_small = sem("ab_small")
        pos_loaded = sem("pos_loaded")
        rel_loaded = sem("rel_loaded")
        rel_stored = sem("rel_stored")
        rows2_loaded = sem("rows2_loaded")
        bias_loaded = sem("bias_loaded")
        x_stored = sem("x_stored")
        ident_ready = sem("ident_ready")
        consts_ready = sem("consts_ready")
        pool_step = sem("pool_step")
        dve_step = sem("dve_step")
        act_step = sem("act_step")
        vecs_turned = sem("vecs_turned")
        cols_ready = sem("cols_ready")
        gw_hi_ready = sem("gw_hi_ready")
        gw_ready = sem("gw_ready")
        ss_act = sem("ss_act")
        ss_dve = sem("ss_dve")
        rstd_ready = sem("rstd_ready")
        x_ready = sem("x_ready")
        xn_ready = sem("xn_ready")
        turned = sem("turned")
        h_hi_ready = sem("h_hi_ready")
        h_lo_ready = sem("h_lo_ready")
        acc_half = sem("acc_half")
        gates_done = sem("gates_done")
        gate_abs = sem("gate_abs")
        gate_ln = sem("gate_ln")
        gates_ready = sem("gates_ready")
        rows_turned = sem("rows_turned")
        rows_ready = sem("rows_ready")
        cols_turned = sem("cols_turned")
        gcols_ready = sem("gcols_ready")
        evac_qk = sem("evac_qk")
        conv_done = sem("conv_done")
        silu_done = sem("silu_done")
        diag_ready = sem("diag_ready")
        row_spread = sem("row_spread")
        row_ready = sem("row_ready")
        gate_scaled = sem("gate_scaled")
        r_both_ready = sem("r_both_ready")
        post_read = sem("post_read")
        evac_v = sem("evac_v")
        evac_oa = sem("evac_oa")
        evac_u = sem("evac_u")
        evac_vb = sem("evac_vb")
        vbn_ready = sem("vbn_ready")
        spread = sem("spread")
        w_ready = sem("w_ready")
        s_ready = sem("s_ready")
        g_ready = sem("g_ready")
        o_ready = sem("o_ready")
        unit_done = sem("unit_done")
        sgu_done = sem("sgu_done")
        rel_built = sem("rel_built")
        trig_in = sem("trig_in")
        trig_ready = sem("trig_ready")
        act_out = sem("act_out")
        mul_out = sem("mul_out")
        g_hi_ready = sem("g_hi_ready")
        g_lo_ready = sem("g_lo_ready")
        krr_ready = sem("krr_ready")
        krr_turned = sem("krr_turned")
        krT_ready = sem("krT_ready")
        kfT_rope = sem("kfT_rope")
        krr_zero = sem("krr_zero")
        evac_k = sem("evac_k")
        evac_k2 = sem("evac_k2")
        evac_vc = sem("evac_vc")
        evac_q = sem("evac_q")
        q_roped = sem("q_roped")
        qf_turned = sem("qf_turned")
        qf_ready = sem("qf_ready")
        at_s, at_max, at_exp, at_pt, at_ptsb, at_pv = [
            [sem(f"{n}{i}") for i in range(2)] for n in ("scores", "maxed", "exped", "pturned", "pcopied", "pv")]
        evac_qk2 = sem("evac_qk2")
        evac_v2 = sem("evac_v2")
        bias_ready = sem("bias_ready")

        w_in = d["ab_w_in"][0].rearrange("(k p) n -> p k n", p=P)
        w_uv0 = 4 * A_W + 4 * A_H

        def rows_of(w, k0, k1):
            return w.rearrange("(k p) n -> p k n", p=P)[:, k0:k1, :]

        def cols_of(w, k0, k1, c0, c1):
            return w.rearrange("(k p) n -> p k n", p=P)[:, k0:k1, c0:c1]

        ab_w, c_w, qkv = d["ab_w_in"][0], d["c_w_in"][0], d["w_qkv_2"][0]
        SRC = {}
        for j in range(4):
            SRC[P_QK + j] = cols_of(ab_w, 0, KB, QK_ORDER[j] * CH, (QK_ORDER[j] + 1) * CH)
        for first, c0 in ((P_VA, 1024), (P_OA, 1536), (P_U, w_uv0), (P_VB, w_uv0 + B_W)):
            for j in range(2):
                SRC[first + j] = cols_of(ab_w, 4 * j, 4 * j + 4, c0, c0 + 512)
        for first, w in ((P_AOUT, d["ab_w_out"][0]), (P_COUT, d["c_w_out"][0]), (P_O2, d["w_o_2"][0])):
            for j in range(4):
                SRC[first + j] = rows_of(w, 2 * j, 2 * j + 2)
        for j, (k0, k1) in enumerate(((0, 3), (3, 6), (6, 8))):
            SRC[P_CIN + j] = rows_of(c_w, k0, k1)
        for j in range(2):
            SRC[P_UKV + j] = cols_of(d["c_w_ukv"][0], 0, 2, j * 1024, (j + 1) * 1024)
        for j in range(3):
            SRC[P_UQ + j] = cols_of(d["c_w_uq"][0], 0, 3, j * 512, (j + 1) * 512)
        for j in range(8):
            c0 = (j % 2) * D + (j // 2) * CH
            SRC[P_QK2 + j] = cols_of(qkv, 0, KB, c0, c0 + CH)
        for n in range(2):
            for j in range(2):
                SRC[P_V2 + 2 * n + j] = cols_of(qkv, 4 * j, 4 * j + 4, 2 * D + n * 512, 2 * D + (n + 1) * 512)

        def width(n):
            if n in SRC:
                return SRC[n].shape[1] * SRC[n].shape[2]
            return PIECE

        def part(t, n, a):
            w = width(n)
            return t[:, n % RING, 0:w].rearrange("p (a b) -> p a b", a=a)

        def views(n, t, is_raw):
            w = t[:, n % RING, 0:width(n)]
            if not P_UKV <= n < P_UKV + 2:
                return [w]
            if is_raw:
                w = w.rearrange("p (k h v e) -> p v k h e", k=2, h=8, v=2)
            else:
                w = w.rearrange("p (k v h e) -> p v k h e", k=2, h=8, v=2)
            return [w[:, 0], w[:, 1]]

        def t_base(t):
            return sum(T_BANKS[:t])

        def bank(b, n=1):
            return psum[:, b:b + n, :].rearrange("p b c -> p (b c)")

        def col(name, i):
            c = VEC[name] + i
            return cols[:, c:c + 1]

        def gain(t, k):
            if t == T_AB:
                return col("ab_norm", k)
            if t == T_AMIX:
                return col("ab_head_g", k) if k < 4 else None
            if t == T_FFN0:
                return col("ffn_norm", k)
            if t == T_C:
                return col("c_norm", k)
            if t == T_LAT:
                return col("c_q_g", k) if k < 3 else col("c_kv_g", k - 3)
            if t == T_FFN1:
                return col("ffn_norm", 8 + k)
            if t == T_2:
                return gain2[:, k:k + 1]
            if t == T_GLU:
                return col("g_pre_ffn_2", k)
            return None

        block = ctx.enter_context(nc.Block())

        @block.sync
        def _(sp):
            def load(n, slot, src, wide=PIECE, a=None):
                if not (isinstance(n, int) and n < RING):
                    sp.wait_ge(lo_ready, n - RING + 1)
                dst = raw[:, slot, 0:wide].rearrange("p (a b) -> p a b", a=a)
                sp.dma_start(dst, src).then_inc(arrived[slot], 16)

            def load_static(n):
                load(n, n % RING, SRC[n], width(n), SRC[n].shape[1])

            def ffn(first, w1, w2):
                w1v = w1.rearrange("(k p) n -> p k n", p=P)
                w2v = w2.rearrange("(k p) n -> p k n", p=P)
                load(first, first % RING, w1v[:, :, 0:CH], a=KB)
                with sp.Fori(0, (FC - 1) // 3) as i:
                    for j in range(3):
                        n = first + 1 + 2 * j
                        load(n + 6 * i, n % RING, w1v[:, :, bass.ds((3 * i + j + 1) * CH, CH)], a=KB)
                        load(n + 1 + 6 * i, (n + 1) % RING, w2v[:, bass.ds((3 * i + j) * 2, 2), :], a=2)
                n = first + 2 * FC - 1
                load(n, n % RING, w2v[:, 2 * FC - 2:2 * FC, :], a=2)

            def glu(first):
                wg = d["w_gate_2"][0].rearrange("(k p) n -> p k n", p=P)
                wu = d["w_up_2"][0].rearrange("(k p) n -> p k n", p=P)
                wd = d["w_down_2"][0].rearrange("(k p) n -> p k n", p=P)
                load(first, first % RING, wg[:, :, 0:CH], a=KB)
                load(first + 1, (first + 1) % RING, wu[:, :, 0:CH], a=KB)
                with sp.Fori(0, GC - 1) as c:
                    n = first + 2
                    load(n + 3 * c, n % RING, wg[:, :, bass.ds((c + 1) * CH, CH)], a=KB)
                    load(n + 1 + 3 * c, (n + 1) % RING, wu[:, :, bass.ds((c + 1) * CH, CH)], a=KB)
                    load(n + 2 + 3 * c, (n + 2) % RING, wd[:, bass.ds(2 * c, 2), :], a=2)
                n = first + 3 * GC - 1
                load(n, n % RING, wd[:, 2 * GC - 2:2 * GC, :], a=2)

            x_v = d["x"][0].rearrange("(t p) c -> p t c", p=P)
            for tb in range(TB):
                sp.dma_start(x[:, tb, :], x_v[:, tb, :]).then_inc(x_loaded, 16)
            for n in range(P_FFN0):
                load_static(n)
            ffn(P_FFN0, d["ffn_w1"][0], d["ffn_w2"][0])
            for n in range(P_CIN, P_FFN1):
                load_static(n)
            ffn(P_FFN1, d["ffn_w1"][1], d["ffn_w2"][1])
            for n in range(P_V2, P_GLU):
                load_static(n)
            glu(P_GLU)
            out_v = out[0].rearrange("(t p) c -> p t c", p=P)
            for tb in range(TB):
                for half in range(2):
                    cs = slice(half * 512, (half + 1) * 512)
                    sp.wait_ge(x_ready, X_AT["out"] + 2 * tb + half + 1)
                    sp.dma_start(out_v[:, tb, cs], x[:, tb, cs]).then_inc(x_stored, 16)
            sp.wait_ge(x_stored, 16 * 2 * TB)

        @block.gpsimd
        def _(pool):
            steps = [0]

            def step(ins):
                steps[0] += 1
                ins.then_inc(pool_step, 1)
                pool.wait_ge(pool_step, steps[0])

            step(pool.memset(ident[:, :], 0.0))
            pool.affine_select(out=ident[:, :], in_=ident[:, :], compare_op=ALU.not_equal, fill=1.0, base=0,
                               pattern=[[-1, P]], channel_multiplier=1).then_inc(ident_ready, 1)
            step(pool.memset(mhalf[:, :], -0.5))
            step(pool.memset(mone[:, :], -1.0))

            def rms(name):
                c0, n, w = JOBS[name]
                if name in SS_ACT:
                    pool.wait_ge(ss_act, SS_ACT.index(name) + 1)
                else:
                    pool.wait_ge(ss_dve, SS_DVE.index(name) + 1)
                step(pool.tensor_scalar(msq[:, c0:c0 + n], ssq[:, c0:c0 + n], 1.0 / w, EPS, ALU.mult, ALU.add))
                power = mone[:, :] if name in SQUARED else mhalf[:, 0:n]
                pool.tensor_tensor(rstd[:, c0:c0 + n], msq[:, c0:c0 + n], power, ALU.pow)\
                    .then_inc(rstd_ready, 1)

            rms("ab0")
            rms("ab1")
            step(pool.memset(mask[:, :, :], 0.0))
            pool.affine_select(out=mask[:, 0, :], in_=mask[:, 0, :], compare_op=ALU.is_ge, fill=NEG, base=0,
                               pattern=[[1, P]], channel_multiplier=-1).then_inc(consts_ready, 1)
            pool.affine_select(out=mask[:, 1, :], in_=mask[:, 1, :], compare_op=ALU.is_ge, fill=NEG, base=0,
                               pattern=[[-1, P]], channel_multiplier=1).then_inc(consts_ready, 1)
            step(pool.memset(ones[:, :], 1.0))
            for i in range(HALF):
                ins = pool.memset(freq[:, i:i + 1], float(np.float32(10000.0) ** np.float32(-i / HALF)))
            ins.then_inc(consts_ready, 1)
            rms("vb")
            rms("ha")
            pool.wait_ge(rel_built, 1)
            pool.dma_start(rel_dram.ap(), rel_ext[:, :].unsqueeze(1).to_broadcast([H2, P, EXT])).then_inc(rel_stored, 16)
            for name in ("ffn00", "ffn01", "c0", "c1", "cq", "ckv"):
                rms(name)
            pool.wait_ge(krT_ready, 1)
            pool.tensor_copy(kfT[C_NOPE:C_QK, 0:C_H, :],
                             krT[C_NOPE:C_QK, :].unsqueeze(1).to_broadcast([C_ROPE, C_H, S])).then_inc(kfT_rope, 1)
            for name in ("ffn10", "ffn11", "fin0", "fin1", "pre0", "pre1"):
                if name == "ffn10":
                    pool.wait_ge(turned, t_base(T_CMIX) + T_BANKS[T_CMIX])
                    pool.wait_ge(rel_stored, 16)
                    pool.dma_start(bias2[:, :, :], bass.AP(rel_dram, P - 1, [[EXT - 1, P], [P * EXT, H2], [1, S]]))\
                        .then_inc(bias_loaded, 16)
                    pool.dma_start(fin_row, d["final_norm"].partition_broadcast(P)).then_inc(rows2_loaded, 16)
                    pool.dma_start(pm_row, d["g_post_mix_2"][0].partition_broadcast(P)).then_inc(rows2_loaded, 16)
                    pool.dma_start(pf_row, d["g_post_ffn_2"][0].partition_broadcast(P)).then_inc(rows2_loaded, 16)
                    pool.wait_ge(bias_loaded, 16)
                    pool.memset(bias2[0:CHUNK, :, P + CHUNK:S], NEG).then_inc(bias_ready, 1)
                rms(name)
            for name in ("pm0", "pm1", "glu0", "glu1", "pf0", "pf1"):
                rms(name)

        @block.scalar
        def _(act):
            steps = [0]

            def step(ins):
                steps[0] += 1
                ins.then_inc(act_step, 1)
                act.wait_ge(act_step, steps[0])

            def hi(n):
                if n >= PIECES:
                    return
                act.wait_ge(arrived[n % RING], 16 * (n // RING + 1))
                if n >= RING:
                    act.wait_ge(piece_used, n - RING + 1)
                for dst, src in zip(views(n, w_hi, False), views(n, raw, True)):
                    ins = act.activation(dst, src, ACT.Copy)
                ins.then_inc(hi_ready, 1)

            def hi_loop(n0, i):
                slot = n0 % RING
                act.wait_ge(arrived[slot], 16 * (n0 // RING + 1) + 32 * i)
                act.wait_ge(piece_used, n0 - RING + 1 + 6 * i)
                act.activation(w_hi[:, slot, :], raw[:, slot, :], ACT.Copy).then_inc(hi_ready, 1)

            def turn(t):
                for q in range(T_BANKS[t]):
                    act.wait_ge(turned, t_base(t) + q + 1)
                    for k in range(2 * q, min(2 * q + 2, T_BLOCKS[t])):
                        g = gain(t, k)
                        ins = act.activation(h_hi[:, k, :], bank(4 + q)[:, (k % 2) * S:(k % 2 + 1) * S], ACT.Copy,
                                             scale=1.0 if g is None else g)
                    ins.then_inc(h_hi_ready, 1)

            sums = [0]

            def squares(src, c, scale=1.0):
                if sums[0]:
                    act.wait_ge(ss_act, sums[0])
                sums[0] += 1
                act.activation(junk[:, 0:src.shape[-1]], src, ACT.Square, scale=scale,
                               accum_out=ssq[:, c:c + 1]).then_inc(ss_act, 1)

            def squares_x(jobs, x_at):
                for tb in range(TB):
                    act.wait_ge(x_ready, x_at + 2 * tb + 2)
                    squares(x[:, tb, :], JOBS[jobs[tb]][0])

            def row_out(n, b):
                act.wait_ge(row_spread, n + 1)
                act.activation(r_row[:, :], bank(b)[:, 0:S], ACT.Copy).then_inc(row_ready, 1)

            def rs(name, i=0):
                c = JOBS[name][0] + i
                return rstd[:, c:c + 1]

            for name, r0 in VEC.items():
                v = d[name]
                if name == "ab_conv":
                    v = v[0].rearrange("w (k p) -> (w k) p", p=P)
                elif name == "ab_bs":
                    v = v[0]
                elif name == "final_norm":
                    v = v.rearrange("(k p) -> k p", p=P)
                else:
                    v = v.rearrange("l (k p) -> (l k) p", p=P)
                act.dma_start(vecs[r0:r0 + v.shape[0], :], v).then_inc(vecs_loaded, 16)
            act.dma_start(ws_raw[:, :, :], d["ab_ws"][0].rearrange("g t s -> t g s")).then_inc(ws_loaded, 16)
            act.dma_start(gw_raw[:, :, :], w_in[:, :, 4 * A_W:4 * A_W + 16]).then_inc(ab_small, 16)
            act.dma_start(gb_row, d["ab_gate_b"][0].partition_broadcast(P)).then_inc(ab_small, 16)
            act.dma_start(vg_row, d["ab_v_g"][0].partition_broadcast(P)).then_inc(ab_small, 16)
            act.dma_start(pos_i[:, :], d["positions"][0].rearrange("(t p) -> p t", p=P),
                          allow_slow_non_contiguous=True).then_inc(pos_loaded, 16)
            act.dma_start(rel_t[:, :], d["rel_bias_2"][0]).then_inc(rel_loaded, 16)
            for tb in range(TB):
                act.wait_ge(x_loaded, 32)
                squares(x[:, tb, :], JOBS["ab0"][0] + tb)
            act.wait_ge(vecs_turned, 1)
            act.activation(cols[:, :], bank(0)[:, 0:VECS], ACT.Copy).then_inc(cols_ready, 1)
            act.wait_ge(ab_small, 48)
            act.activation(gw_hi[:, :, :], gw_raw[:, :, :], ACT.Copy).then_inc(gw_hi_ready, 1)
            hi(0)
            act.wait_ge(cols_ready, 1)
            turn(T_AB)
            hi(1)
            hi(2)
            act.wait_ge(vecs_turned, 2)
            act.activation(wsT[:, :, :], bank(1).rearrange("p (g t) -> p g t", g=B_G), ACT.Copy).then_inc(cols_ready, 1)
            act.wait_ge(gate_abs, 1)
            step(act.activation(g_exp[:, :, :], g_abs[:, :, :], ACT.Exp, scale=-1.0))
            act.activation(g_ln[:, :, :], g_exp[:, :, :], ACT.Ln, bias=1.0).then_inc(gate_ln, 1)

            def qk_out(j):
                act.wait_ge(piece_used, P_QK + j + 1)
                b0 = 2 * QK_ORDER[j]
                act.activation(qk_pad[:, b0:b0 + 2, PAD:PAD + S],
                               bank(QK_ORDER[j]).rearrange("p (b t) -> p b t", b=2), ACT.Copy).then_inc(evac_qk, 1)

            def silu(j):
                act.wait_ge(conv_done, j + 1)
                b0 = 2 * QK_ORDER[j]
                act.activation(qkT[:, b0:b0 + 2, :], qk_conv[:, b0:b0 + 2, :], ACT.Silu)\
                    .then_inc(silu_done, 1)

            for j in range(4):
                qk_out(j)
                hi(P_QK + j + RING)
            hi(P_VA + RING)
            silu(0)
            act.wait_ge(piece_used, P_VA + 2)
            for tb in range(TB):
                act.activation(v_ext[:, tb, :, 0:A_D], bank(4 + tb).rearrange("p (h e) -> p h e", h=A_H), ACT.Copy)\
                    .then_inc(evac_v, 1)
            hi(P_VA + 1 + RING)
            silu(1)
            hi(P_VB + RING)
            act.wait_ge(piece_used, P_VB + 2)
            hi(P_VB + 1 + RING)
            silu(2)
            silu(3)
            for tb in range(TB):
                act.activation(vb[:, tb, :], bank(tb), ACT.Gelu_apprx_tanh).then_inc(evac_vb, 1)
            act.wait_ge(cols_turned, 1)
            tc = bank(6)[:, 0:32].rearrange("p (q t e) -> p q t e", q=2, t=TB)
            act.activation(a_col[:, :, :], tc[:, 0], ACT.Copy).then_inc(gcols_ready, 1)
            act.activation(e_col[:, :, :], tc[:, 1], ACT.Exp, scale=-1.0).then_inc(gcols_ready, 1)
            act.wait_ge(gcols_ready, 2)

            def decay_of(u):
                h, back = u // 2, u % 2
                act.wait_ge(spread, u + 1)
                if u >= 2:
                    act.wait_ge(g_ready, u - 1)
                b = bank(u % 2)
                dst = decay[:, u % 2, :, :].rearrange("p b t -> p (b t)")
                at = back * A_H + h
                for s0, (c0, c1) in enumerate([((0, 256), (384, 512)), ((0, 128), (256, 512))][back]):
                    ins = act.activation(dst[:, c0:c1], b[:, c0:c1], ACT.Exp, bias=a_col[:, s0, at:at + 1])
                ins.then_inc(w_ready, 1)

            for i in range(4):
                decay_of(2 * i)
                decay_of(2 * i + 1)
                if i == 1:
                    act.wait_ge(piece_used, P_OA + 2)
                    for tb in range(TB):
                        act.activation(oa[:, tb, :], bank(6 + tb), ACT.Sigmoid).then_inc(evac_oa, 1)
                hi(P_OA + i + RING)
            act.wait_ge(piece_used, P_U + 2)
            for tb in range(TB):
                act.activation(u_act[:, tb, :], bank(6 + tb), ACT.Gelu_apprx_tanh).then_inc(evac_u, 1)
            turn(T_AMIX)
            for j in range(4):
                hi(P_AOUT + j + RING)
            act.wait_ge(trig_in, 1)
            act.activation(trig[:, :, :, :], ang2[:, :, :, :], ACT.Sin).then_inc(trig_ready, 1)

            def ffn(first, hb, t, jobs, x_at):
                turn(t)
                squares_x(jobs, x_at)

                def hidden(c, r, n_w1):
                    act.wait_ge(piece_used, n_w1 + 1)
                    if not (isinstance(c, int) and c < 3):
                        act.wait_ge(g_lo_ready, hb + c - 2)
                    act.activation(g_act[:, r, :], bank(4 + r), ACT.Relu).then_inc(act_out, 1)
                    act.wait_ge(act_out, hb + c + 1)
                    act.activation(g_hi[:, r, :], g_act[:, r, :], ACT.Square).then_inc(g_hi_ready, 1)

                hidden(0, 0, first)
                hi(first + RING)

                def chunk(c, j, i):
                    n = first + 1 + 2 * j
                    hidden(c + 1, (j + 1) % 3, n + 6 * i)
                    if isinstance(i, int):
                        hi(n + 6 * i + RING)
                        hi(n + 6 * i + 1 + RING)
                    else:
                        hi_loop(n + RING, i)
                        hi_loop(n + 1 + RING, i)

                for j in range(3):
                    chunk(j, j, 0)
                with act.Fori(1, (FC - 1) // 3) as i:
                    for j in range(3):
                        chunk(3 * i + j, j, i)
                hi(first + 2 * FC - 1 + RING)

            ffn(P_FFN0, 0, T_FFN0, ("ffn00", "ffn01"), X_AT["ffn0"])

            turn(T_C)
            squares_x(("c0", "c1"), X_AT["c"])
            act.wait_ge(rstd_ready, JOB_AT["c1"] + 1)
            for j in range(2):
                hi(P_CIN + j + RING)
            act.wait_ge(piece_used, P_CIN + 3)
            for name, c0, w in (("cq", 0, Q_LORA), ("ckv", Q_LORA, KV_LORA)):
                for tb in range(TB):
                    squares(bank(2 * tb, 2)[:, c0:c0 + w], JOBS[name][0] + tb, rs(f"c{tb}"))
            hi(P_CIN + 2 + RING)
            turn(T_LAT)
            act.wait_ge(krr_turned, 1)
            act.activation(krT[C_NOPE:C_QK, :], psum[C_NOPE:C_QK, 7, 0:S], ACT.Copy).then_inc(krT_ready, 1)
            for j in range(3):
                act.wait_ge(piece_used, P_UQ + j + 1)
                for tb in range(TB):
                    ins = act.activation(q_tok[:, tb, j * 512:(j + 1) * 512], bank(2 * j + tb), ACT.Copy,
                                         scale=float(C_QK) ** -0.5)
                ins.then_inc(evac_q, 1)
                hi(P_UQ + j + RING)
            for j in range(2):
                act.wait_ge(piece_used, P_UKV + j + 1)
                act.activation(kfT[0:C_NOPE, 8 * j:8 * j + 8:2, :],
                               bank((6, 2)[j], 2)[0:C_NOPE, :].rearrange("p (h t) -> p h t", h=4), ACT.Copy)\
                    .then_inc(evac_k, 1)
                hi(P_UKV + j + RING)
            for n in range(1, 8, 2):
                act.wait_ge(qf_turned, n + 1)
                act.activation(qfT[0:C_QK, 2 * n:2 * n + 2, :],
                               bank((6, 7, 0, 1)[n % 4])[0:C_QK, :].rearrange("p (h t) -> p h t", h=2), ACT.Copy)\
                    .then_inc(qf_ready, 1)
            for h in range(C_H):
                act.wait_ge(at_max[0], h + 1)
                if h >= 2:
                    act.wait_ge(at_pt[0], h - 1)
                for qb in range(2):
                    ins = act.activation(prob[:, h % 2, qb * S:(qb + 1) * S], bank(4 + h % 2)[:, qb * S:(qb + 1) * S],
                                         ACT.Exp, bias=nmax[:, qb, h:h + 1], accum_out=psm[:, qb, h:h + 1])
                ins.then_inc(at_exp[0], 1)
            turn(T_CMIX)
            for j in range(4):
                hi(P_COUT + j + RING)
            ffn(P_FFN1, FC, T_FFN1, ("ffn10", "ffn11"), X_AT["ffn1"])

            turn(T_2)
            squares_x(("fin0", "fin1"), X_AT["fin"])
            squares_x(("pre0", "pre1"), X_AT["pre"])
            row_out(0, 5)
            hi(P_V2 + RING)
            for n in range(2):
                act.wait_ge(piece_used, P_V2 + 2 * n + 2)
                act.wait_ge(r_both_ready, 1)
                for tb in range(TB):
                    act.activation(v2[:, tb, n * 512:(n + 1) * 512], bank(2 * n + tb), ACT.Copy,
                                   scale=r_both[:, tb:tb + 1]).then_inc(evac_v2, 1)
                hi(P_V2 + 2 * n + 1 + RING)
                if n == 0:
                    hi(P_V2 + 2 + RING)

            def copy_pt(h):
                act.wait_ge(at_pt[1], h + 1)
                if h >= 2:
                    act.wait_ge(at_pv[1], h - 1)
                act.activation(probT2[:, h % 2, :], bank(4 + h % 2)[:, 0:3 * P], ACT.Copy).then_inc(at_ptsb[1], 1)

            def exp2(h):
                act.wait_ge(at_max[1], h + 1)
                if h >= 2:
                    act.wait_ge(at_pt[1], h - 1)
                for qb, (c0, c1) in enumerate(((0, P), (P, 3 * P))):
                    ins = act.activation(prob2[:, h % 2, c0:c1], s2[:, h % 2, c0:c1], ACT.Exp, scale=-1.0,
                                         bias=nmax2[:, qb, h:h + 1], accum_out=psm2[:, qb, h:h + 1])
                ins.then_inc(at_exp[1], 1)

            for j in range(8):
                if j >= 2:
                    exp2(2 * j - 4)
                    if j > 2:
                        copy_pt(2 * j - 5)
                hi(P_QK2 + j + RING)
                if j >= 2:
                    exp2(2 * j - 3)
                    copy_pt(2 * j - 4)
            for h in range(12, H2):
                exp2(h)
                copy_pt(h - 1)
            copy_pt(H2 - 1)
            turn(T_2MIX)
            for j in range(4):
                hi(P_O2 + j + RING)

            def squares_acc(stage, last, jobs, pre):
                for tb in range(TB):
                    if tb == 0:
                        act.wait_ge(acc_half, stage + 1)
                    else:
                        act.wait_ge(piece_used, last + 1)
                    squares(bank(2 * tb, 2), JOBS[jobs[tb]][0], pre[tb])

            squares_acc(4, P_O2 + 3, ("pm0", "pm1"), (1.0, 1.0))
            turn(T_GLU)
            squares_x(("glu0", "glu1"), X_AT["glu"])
            row_out(1, 0)
            hb, first = 2 * FC, P_GLU

            def silu_glu(c, r):
                act.wait_ge(gate_scaled, c + 1)
                act.activation(g_act[:, r, :], g_act[:, r, :], ACT.Silu).then_inc(act_out, 1)

            def glu_hi(c, r):
                act.wait_ge(mul_out, hb + c + 1)
                act.activation(g_hi[:, r, :], g_mul[:, r, :], ACT.Copy).then_inc(g_hi_ready, 1)

            silu_glu(0, 0)
            hi(first + RING)
            glu_hi(0, 0)
            hi(first + 1 + RING)

            def glu_chunk(c, j, i):
                n = first + 2 + 3 * j
                silu_glu(c + 1, (j + 1) % 2)
                ahead = hi if isinstance(i, int) else hi_loop
                a = (lambda k: (n + 6 * i + k + RING,)) if isinstance(i, int) else (lambda k: (n + k + RING, i))
                ahead(*a(0))
                glu_hi(c + 1, (j + 1) % 2)
                ahead(*a(1))
                ahead(*a(2))

            for j in range(2):
                glu_chunk(j, j, 0)
            with act.Fori(1, (GC - 1) // 2 - 1) as i:
                for j in range(2):
                    glu_chunk(2 * i + j, j, i)
            i = (GC - 1) // 2 - 1
            for j in range(2):
                glu_chunk(2 * i + j, j, i)
            squares_acc(5, PIECES - 1, ("pf0", "pf1"), (rs("glu0"), rs("glu1")))

        @block.vector
        def _(dve):
            steps = [0]

            def step(ins):
                steps[0] += 1
                ins.then_inc(dve_step, 1)
                dve.wait_ge(dve_step, steps[0])

            def lo(n):
                if n >= PIECES:
                    return
                dve.wait_ge(hi_ready, n + 1)
                for dst, src, high in zip(views(n, w_lo, False), views(n, raw, True), views(n, w_hi, False)):
                    ins = dve.tensor_tensor(dst, src, high, ALU.subtract)
                ins.then_inc(lo_ready, 1)

            def lo_loop(n0, i):
                slot = n0 % RING
                dve.wait_ge(hi_ready, n0 + 1 + 6 * i)
                dve.tensor_tensor(w_lo[:, slot, :], raw[:, slot, :], w_hi[:, slot, :], ALU.subtract)\
                    .then_inc(lo_ready, 1)

            def turn(t):
                for q in range(T_BANKS[t]):
                    dve.wait_ge(h_hi_ready, t_base(t) + q + 1)
                    for k in range(2 * q, min(2 * q + 2, T_BLOCKS[t])):
                        g = gain(t, k)
                        ins = dve.scalar_tensor_tensor(
                            out=h_lo[:, k, :], in0=bank(4 + q)[:, (k % 2) * S:(k % 2 + 1) * S],
                            scalar=1.0 if g is None else g, in1=h_hi[:, k, :], op0=ALU.mult, op1=ALU.subtract)
                    ins.then_inc(h_lo_ready, 1)

            def rs(name, i=0):
                c = JOBS[name][0] + i
                return rstd[:, c:c + 1]

            def rs_wait(name):
                dve.wait_ge(rstd_ready, JOB_AT[name] + 1)

            def scaled(jobs):
                for tb in range(TB):
                    rs_wait(jobs[tb])
                    dve.tensor_scalar(xn[:, tb, :], x[:, tb, :], rs(jobs[tb]), None, ALU.mult).then_inc(xn_ready, 1)

            def acc_wait(stage, last, tb):
                if tb == 0:
                    dve.wait_ge(acc_half, stage + 1)
                else:
                    dve.wait_ge(piece_used, last + 1)

            def residual(stage, last, jobs=None):
                for tb in range(TB):
                    if jobs:
                        rs_wait(jobs[tb])
                    acc_wait(stage, last, tb)
                    for half in range(2):
                        xh = x[:, tb, half * 512:(half + 1) * 512]
                        dve.scalar_tensor_tensor(out=xh, in0=bank(2 * tb + half), scalar=rs(jobs[tb]) if jobs else 1.0,
                                                 in1=xh, op0=ALU.mult, op1=ALU.add).then_inc(x_ready, 1)

            def diagonal(cols_of_r):
                for tb in range(TB):
                    dve.tensor_scalar(diag[:, tb, :], ident[:, :], cols_of_r[tb], None, ALU.mult)\
                        .then_inc(diag_ready, 1)

            step(dve.memset(qk_pad[:, :, 0:PAD], 0.0))
            step(dve.memset(qk_pad[:, :, PAD + S:], 0.0))
            step(dve.memset(v_ext[:, :, :, A_D:A_D + 1], 1.0))
            step(dve.memset(ones_row[0:A_H, :], 1.0))
            dve.wait_ge(x_loaded, 32)
            scaled(("ab0", "ab1"))
            dve.wait_ge(gw_hi_ready, 1)
            dve.tensor_tensor(gw_lo[:, :, :], gw_raw[:, :, :], gw_hi[:, :, :], ALU.subtract).then_inc(gw_ready, 1)
            lo(0)
            dve.wait_ge(cols_ready, 1)
            turn(T_AB)
            lo(1)
            lo(2)
            step(dve.tensor_tensor(gain2[:, :], cols[:, VEC["final_norm"]:VEC["final_norm"] + KB],
                                   cols[:, VEC["g_pre_mix_2"]:VEC["g_pre_mix_2"] + KB], ALU.mult))
            dve.wait_ge(ident_ready, 1)
            step(dve.tensor_scalar(nsel[0:A_H, :, :],
                                   ident[0:A_H, 0:A_H].unsqueeze(2).to_broadcast([A_H, A_H, P]), -1.0, None, ALU.mult))
            dve.wait_ge(gates_done, 1)
            for tb in range(TB):
                step(dve.tensor_tensor(gates[:, 2 * tb:2 * tb + 2, :],
                                       bank(7)[:, 16 * tb:16 * tb + 16].rearrange("p (a b) -> p a b", a=2),
                                       gb_row.rearrange("p (a b) -> p a b", a=2), ALU.add))
            fg = gates[:, :, A_H:2 * A_H]
            dve.scalar_tensor_tensor(out=g_abs[:, :, :], in0=fg, scalar=-1.0, in1=fg, op0=ALU.mult, op1=ALU.max)\
                .then_inc(gate_abs, 1)

            def conv(j):
                dve.wait_ge(evac_qk, j + 1)
                b0 = 2 * QK_ORDER[j]
                for b in (b0, b0 + 1):
                    step(dve.tensor_scalar(qk_conv[:, b, :], qk_pad[:, b, 0:S], col("ab_conv", b), None, ALU.mult))
                    for t in range(1, TAPS):
                        ins = dve.scalar_tensor_tensor(out=qk_conv[:, b, :], in0=qk_pad[:, b, t:t + S],
                                                       scalar=col("ab_conv", 8 * t + b), in1=qk_conv[:, b, :],
                                                       op0=ALU.mult, op1=ALU.add)
                        if t < TAPS - 1 or b == b0:
                            step(ins)
                ins.then_inc(conv_done, 1)

            lo(3)
            conv(0)
            dve.wait_ge(gate_ln, 1)
            dve.scalar_tensor_tensor(out=fg, in0=fg, scalar=0.0, in1=g_ln[:, :, :], op0=ALU.min, op1=ALU.subtract)\
                .then_inc(gates_ready, 1)
            lo(4)
            dve.wait_ge(rows_turned, 1)
            rows = bank(6, 2)[0:A_H, :].rearrange("p (d q t) -> p d q t", d=2, q=2)
            one = ones_row[0:A_H, :]
            step(dve.tensor_tensor_scan(cumf[0:A_H, 0, :], one, rows[:, 0, 1, :], 0.0, ALU.mult, ALU.add))
            step(dve.tensor_tensor_scan(cumf[0:A_H, 1, ::-1], one, rows[:, 1, 1, ::-1], 0.0, ALU.mult, ALU.add))
            step(dve.tensor_tensor(a_row[0:A_H, :, :], rows[:, :, 0, :], cumf[0:A_H, :, :], ALU.subtract))
            step(dve.tensor_tensor_scan(m_row[0:A_H, 0, :], a_row[0:A_H, 0, :], a_row[0:A_H, 0, :], 0.0,
                                        ALU.max, ALU.max))
            step(dve.tensor_tensor_scan(m_row[0:A_H, 1, ::-1], a_row[0:A_H, 1, ::-1], a_row[0:A_H, 1, ::-1], 0.0,
                                        ALU.max, ALU.max))
            dve.tensor_tensor(mt_row[0:A_H, :, :], cumf[0:A_H, :, :], m_row[0:A_H, :, :], ALU.add)\
                .then_inc(rows_ready, 1)
            conv(1)
            lo(5)
            lo(6)
            conv(2)
            lo(7)
            lo(8)
            conv(3)
            lo(9)
            lo(10)
            dve.wait_ge(evac_vb, 2)
            groups = vb[:, :, :].rearrange("p t (g c) -> p (t g) c", g=B_G)
            sq_g = sq_tmp[:, :, :].rearrange("p t (g c) -> p (t g) c", g=B_G)
            step(dve.tensor_tensor(sq_g, groups, groups, ALU.mult))
            c0 = JOBS["vb"][0]
            dve.tensor_reduce(ssq[:, c0:c0 + 8], sq_g, AX.X, ALU.add).then_inc(ss_dve, 1)

            def weigh(u):
                h, back = u // 2, u % 2
                dve.wait_ge(w_ready, u + 1)
                dve.wait_ge(s_ready, h + 1)
                src = bank(2 + h % 2)
                w = decay[:, u % 2, :, :].rearrange("p b t -> p (b t)")
                dst = score[:, u % 2, :, :].rearrange("p b t -> p (b t)")
                for c0, c1 in [((0, 256), (384, 512)), ((0, 128), (256, 512))][back]:
                    ins = dve.scalar_tensor_tensor(out=dst[:, c0:c1], in0=src[:, c0:c1], scalar=float(A_D) ** -0.5,
                                                   in1=w[:, c0:c1], op0=ALU.mult, op1=ALU.mult)
                ins.then_inc(g_ready, 1)

            def unit_out(u):
                h, back = u // 2, u % 2
                dve.wait_ge(o_ready, u + 1)
                o = bank(4 + u % 2)[:, 0:2 * (A_D + 1)].rearrange("p (t e) -> p t e", t=TB)
                at = back * A_H + h
                den = o[:, :, A_D]
                step(dve.tensor_tensor(dmax, den, e_col[:, :, at], ALU.max))
                step(dve.scalar_tensor_tensor(out=dmax, in0=den, scalar=-1.0, in1=dmax, op0=ALU.mult, op1=ALU.max))
                step(dve.reciprocal(dinv, dmax))
                for tb in range(TB):
                    dst = hsum[:, tb, h * A_D:(h + 1) * A_D]
                    if back:
                        ins = dve.scalar_tensor_tensor(out=dst, in0=o[:, tb, 0:A_D], scalar=dinv[:, tb:tb + 1],
                                                       in1=dst, op0=ALU.mult, op1=ALU.add)
                    else:
                        ins = dve.tensor_scalar(dst, o[:, tb, 0:A_D], dinv[:, tb:tb + 1], None, ALU.mult)
                    if tb == 0:
                        step(ins)
                ins.then_inc(unit_done, 1)
                dve.wait_ge(unit_done, u + 1)

            dve.wait_ge(gcols_ready, 2)
            for u in range(2 * A_H):
                weigh(u)
                if u % 2 == 1:
                    lo(P_OA + u // 2 + RING)
                if u == 2:
                    rs_wait("vb")
                    step(dve.tensor_tensor(groups, groups,
                                           rstd[:, c0:c0 + 8].unsqueeze(2).to_broadcast([P, 8, 128]), ALU.mult))
                    dve.tensor_tensor(vb[:, :, :], vb[:, :, :], vg_row.unsqueeze(1).to_broadcast([P, TB, B_W]),
                                      ALU.mult).then_inc(vbn_ready, 1)
                if u >= 1:
                    unit_out(u - 1)
            unit_out(2 * A_H - 1)
            heads = hsum[:, :, :].rearrange("p t (g c) -> p (t g) c", g=A_H)
            step(dve.tensor_tensor(sq_g, heads, heads, ALU.mult))
            c1 = JOBS["ha"][0]
            dve.tensor_reduce(ssq[:, c1:c1 + 8], sq_g, AX.X, ALU.add).then_inc(ss_dve, 1)
            dve.wait_ge(sgu_done, 1)
            dve.wait_ge(evac_u, 2)
            for g in range(B_G):
                step(dve.scalar_tensor_tensor(
                    out=xn[:, :, A_W + g * 128:A_W + (g + 1) * 128],
                    in0=bank(0, 2)[:, g * S:(g + 1) * S].rearrange("p (n c) -> p n c", n=TB),
                    scalar=col("ab_bs", g), in1=u_act[:, :, g * 128:(g + 1) * 128], op0=ALU.add, op1=ALU.mult))
            rs_wait("ha")
            step(dve.tensor_tensor(heads, heads, rstd[:, c1:c1 + 8].unsqueeze(2).to_broadcast([P, 8, 128]), ALU.mult))
            for tb in range(TB):
                dve.tensor_tensor(xn[:, tb, 0:A_W], hsum[:, tb, :], oa[:, tb, :], ALU.mult).then_inc(xn_ready, 1)
            turn(T_AMIX)
            for j in range(4):
                lo(P_AOUT + j + RING)
            dve.wait_ge(rel_loaded, 16)
            n0 = P
            n1 = n0 + N_REL - 1
            step(dve.tensor_copy(rel_ext[:, 0:n0], rel_t[:, N_REL - 1:N_REL].to_broadcast([H2, n0])))
            step(dve.tensor_copy(rel_ext[:, n0:n1], rel_t[:, N_REL - 2::-1]))
            dve.tensor_copy(rel_ext[:, n1:EXT], rel_t[:, 0:1].to_broadcast([H2, EXT - n1])).then_inc(rel_built, 1)
            dve.wait_ge(pos_loaded, 16)
            dve.wait_ge(consts_ready, 3)
            step(dve.tensor_copy(pos_f[:, :], pos_i[:, :]))
            for tb in range(TB):
                step(dve.tensor_scalar(ang[:, tb, :], freq[:, :], pos_f[:, tb:tb + 1], None, ALU.mult))
            step(dve.tensor_scalar(turns[:, :, :], ang[:, :, :], 1.0 / TWO_PI, ROUND, ALU.mult, ALU.add))
            step(dve.tensor_scalar(turns[:, :, :], turns[:, :, :], -ROUND, None, ALU.add))
            for c in (PI_1, PI_2, PI_3):
                step(dve.scalar_tensor_tensor(out=ang[:, :, :], in0=turns[:, :, :], scalar=-c, in1=ang[:, :, :],
                                              op0=ALU.mult, op1=ALU.add))
            step(dve.tensor_scalar(ang2[:, 1, :, :], ang[:, :, :], PI_IN, -PI_IN, ALU.min, ALU.max))
            step(dve.tensor_scalar(ang[:, :, :], ang[:, :, :], math.pi / 2, None, ALU.add))
            step(dve.tensor_scalar(turns[:, :, :], ang[:, :, :], math.pi, -TWO_PI, ALU.is_gt, ALU.mult))
            step(dve.tensor_tensor(ang[:, :, :], ang[:, :, :], turns[:, :, :], ALU.add))
            dve.tensor_scalar(ang2[:, 0, :, :], ang[:, :, :], PI_IN, -PI_IN, ALU.min, ALU.max).then_inc(trig_in, 1)
            residual(0, P_AOUT + 3)

            def ffn(first, hb, t, jobs, stage):
                turn(t)

                def hidden(c, r):
                    dve.wait_ge(act_out, hb + c + 1)
                    dve.tensor_tensor(g_mul[:, r, :], g_act[:, r, :], g_act[:, r, :], ALU.mult).then_inc(mul_out, 1)
                    dve.wait_ge(mul_out, hb + c + 1)
                    dve.wait_ge(g_hi_ready, hb + c + 1)
                    dve.tensor_tensor(g_lo[:, r, :], g_mul[:, r, :], g_hi[:, r, :], ALU.subtract)\
                        .then_inc(g_lo_ready, 1)

                hidden(0, 0)
                lo(first + RING)

                def chunk(c, j, i):
                    n = first + 1 + 2 * j
                    hidden(c + 1, (j + 1) % 3)
                    if isinstance(i, int):
                        lo(n + 6 * i + RING)
                        lo(n + 6 * i + 1 + RING)
                    else:
                        lo_loop(n + RING, i)
                        lo_loop(n + 1 + RING, i)

                for j in range(3):
                    chunk(j, j, 0)
                with dve.Fori(1, (FC - 1) // 3) as i:
                    for j in range(3):
                        chunk(3 * i + j, j, i)
                lo(first + 2 * FC - 1 + RING)
                residual(stage, first + 2 * FC - 1, jobs)

            ffn(P_FFN0, 0, T_FFN0, ("ffn00", "ffn01"), 1)

            dve.memset(krr[:, :, 0:C_NOPE], 0.0).then_inc(krr_zero, 1)
            turn(T_C)
            for j in range(2):
                lo(P_CIN + j + RING)
            dve.wait_ge(piece_used, P_CIN + 3)

            def rope(lo_half, hi_half, out_lo, out_hi, cos, sin, t):
                step(dve.tensor_tensor(t[0], lo_half, cos, ALU.mult))
                step(dve.tensor_tensor(t[1], hi_half, sin, ALU.mult))
                step(dve.tensor_tensor(t[2], lo_half, sin, ALU.mult))
                step(dve.tensor_tensor(t[3], hi_half, cos, ALU.mult))
                step(dve.tensor_tensor(out_lo, t[0], t[1], ALU.subtract))
                return dve.tensor_tensor(out_hi, t[2], t[3], ALU.add)

            for name, c0, w in (("cq", 0, Q_LORA), ("ckv", Q_LORA, KV_LORA)):
                rs_wait(name)
                if name == "cq":
                    dve.wait_ge(ss_act, SS_ACT.index("ckv") + 1)
                for tb in range(TB):
                    ins = dve.tensor_scalar(xn[:, tb, c0:c0 + w], bank(2 * tb, 2)[:, c0:c0 + w], rs(f"c{tb}"),
                                            rs(name, tb), ALU.mult, ALU.mult)
                    if name == "ckv":
                        ins.then_inc(xn_ready, 1)
            kr = psum[:, :, :].rearrange("p (t b) c -> p t (b c)", b=2)[:, 0:TB, Q_LORA + KV_LORA:C_IN]
            dve.wait_ge(trig_ready, 1)
            for tb in range(TB):
                step(dve.tensor_scalar(krs[:, tb, :], kr[:, tb, :], rs(f"c{tb}"), None, ALU.mult))
            rope(krs[:, :, 0:HALF], krs[:, :, HALF:], krr[:, :, C_NOPE:C_NOPE + HALF], krr[:, :, C_NOPE + HALF:],
                 trig[:, 0], trig[:, 1], rk).then_inc(krr_ready, 1)
            lo(P_CIN + 2 + RING)
            turn(T_LAT)
            for j in range(3):
                lo(P_UQ + j + RING)
            dve.wait_ge(turned, t_base(T_LAT) + 3)
            qv = q_tok[:, :, :].rearrange("p t (h e) -> p t h e", h=C_H)
            cs = [trig[:, i].unsqueeze(2).to_broadcast([P, TB, C_H, HALF]) for i in range(2)]
            dve.wait_ge(evac_q, 3)
            for tb in range(TB):
                ins = rope(qv[:, tb, :, C_NOPE:C_NOPE + HALF], qv[:, tb, :, C_NOPE + HALF:],
                           qv[:, tb, :, C_NOPE:C_NOPE + HALF], qv[:, tb, :, C_NOPE + HALF:],
                           cs[0][:, tb], cs[1][:, tb], [t[:, tb] for t in rp])
                ins.then_inc(q_roped, 1)
                j = tb
                dve.wait_ge(piece_used, P_UKV + j + 1)
                for half in range(TB):
                    ins = dve.tensor_copy(v_tok[:, half, j * 512:(j + 1) * 512], bank((0, 4)[j] + half))
                ins.then_inc(evac_vc, 1)
                dve.wait_ge(evac_k, j + 1)
                dve.tensor_copy(kfT[0:C_NOPE, 8 * j + 1:8 * j + 8:2, :],
                                bank((6, 2)[j], 2)[C_NOPE:P, :].rearrange("p (h t) -> p h t", h=4)).then_inc(evac_k2, 1)
                lo(P_UKV + j + RING)
            for n in range(0, 8, 2):
                dve.wait_ge(qf_turned, n + 1)
                dve.tensor_copy(qfT[0:C_QK, 2 * n:2 * n + 2, :],
                                bank((6, 7, 0, 1)[n % 4])[0:C_QK, :].rearrange("p (h t) -> p h t", h=2))\
                    .then_inc(evac_k2, 1)

            def pt_out(h):
                dve.wait_ge(at_pt[0], h + 1)
                if h >= 2:
                    dve.wait_ge(at_pv[0], h - 1)
                dve.tensor_copy(probT[:, h % 2, :], bank(6 + h % 2)).then_inc(at_ptsb[0], 1)

            def head_max(h):
                dve.wait_ge(at_s[0], h + 1)
                dve.tensor_reduce(nmax[:, :, h], bank(4 + h % 2).rearrange("p (q k) -> p q k", q=2), AX.X, ALU.max,
                                  negate=True).then_inc(at_max[0], 1)

            def mixed(g, banks, hd, sums, inv, exped, pv):
                hs = slice(8 * g, 8 * g + 8)
                dve.wait_ge(exped, 8 * g + 8)
                step(dve.reciprocal(inv[:, :, hs], sums[:, :, hs]))
                dve.wait_ge(pv, 8 * g + 8)
                for qb in range(TB):
                    dve.tensor_tensor(xn[:, qb, g * 512:(g + 1) * 512].rearrange("p (h e) -> p h e", h=8),
                                      bank(banks[qb]).rearrange("p (h e) -> p h e", h=8),
                                      inv[:, qb, hs].unsqueeze(2).to_broadcast([P, 8, hd]), ALU.mult)\
                        .then_inc(xn_ready, 1)

            for h in range(C_H + 1):
                if h < C_H:
                    head_max(h)
                if h >= 1:
                    pt_out(h - 1)
                if h == 10:
                    mixed(0, (0, 2), C_V, psm, pinv, at_exp[0], at_pv[0])
            mixed(1, (1, 3), C_V, psm, pinv, at_exp[0], at_pv[0])
            turn(T_CMIX)
            for j in range(4):
                lo(P_COUT + j + RING)
            residual(2, P_COUT + 3)
            ffn(P_FFN1, FC, T_FFN1, ("ffn10", "ffn11"), 3)

            turn(T_2)
            dve.wait_ge(rows2_loaded, 48)
            for tb in range(TB):
                rs_wait(f"fin{tb}")
                for half in range(2):
                    cs = slice(half * 512, (half + 1) * 512)
                    dve.scalar_tensor_tensor(out=x[:, tb, cs], in0=x[:, tb, cs], scalar=rs(f"fin{tb}"),
                                             in1=fin_row[:, cs], op0=ALU.mult, op1=ALU.mult).then_inc(x_ready, 1)
            rs_wait("pre1")
            c0, c1 = JOBS["fin0"][0], JOBS["pre0"][0]
            dve.tensor_tensor(r_both[:, :], rstd[:, c0:c0 + TB], rstd[:, c1:c1 + TB], ALU.mult)\
                .then_inc(r_both_ready, 1)
            dve.wait_ge(r_both_ready, 1)
            diagonal([r_both[:, tb:tb + 1] for tb in range(TB)])
            for j in range(4):
                lo(P_V2 + j + RING)
            dve.wait_ge(bias_ready, 1)
            dve.wait_ge(row_ready, 1)

            def bias_max(h):
                dve.wait_ge(at_s[1], h + 1)
                if h >= 2:
                    dve.wait_ge(at_exp[1], h - 1)
                for qb, (c0, c1, k0) in enumerate(((0, P, P), (P, 3 * P, 0))):
                    ins = dve.tensor_tensor_reduce(s2[:, h % 2, c0:c1], bank(2 + h % 2)[:, c0:c1],
                                                   bias2[:, h, k0:S], -1.0, -NEG, ALU.add, ALU.min,
                                                   nmax2[:, qb, h:h + 1])
                ins.then_inc(at_max[1], 1)

            for j in range(8):
                if j >= 2:
                    bias_max(2 * j - 4)
                dve.wait_ge(piece_used, P_QK2 + j + 1)
                dst = (kT2 if j % 2 else qT2)[:, 2 * (j // 2):2 * (j // 2) + 2, :]
                dve.scalar_tensor_tensor(out=dst, in0=bank(6 + j % 2).rearrange("p (b t) -> p b t", b=2),
                                         scalar=1.0 if j % 2 else float(HD2) ** -0.5,
                                         in1=r_row[:, :].unsqueeze(1).to_broadcast([P, 2, S]),
                                         op0=ALU.mult, op1=ALU.mult).then_inc(evac_qk2, 1)
                lo(P_QK2 + j + RING)
                if j >= 2:
                    bias_max(2 * j - 3)
                if 2 * j - 3 == 9:
                    mixed(0, (0, 1), HD2, psm2, pinv2, at_exp[1], at_pv[1])
            for h in range(12, H2):
                bias_max(h)
            mixed(1, (0, 1), HD2, psm2, pinv2, at_exp[1], at_pv[1])
            turn(T_2MIX)
            for j in range(4):
                lo(P_O2 + j + RING)

            def post_norm(jobs, pre, row):
                for tb in range(TB):
                    dve.wait_ge(ss_act, SS_ACT.index(jobs[tb]) + 1)
                    step(dve.scalar_tensor_tensor(out=xn[:, tb, :], in0=bank(2 * tb, 2), scalar=pre[tb],
                                                  in1=row, op0=ALU.mult, op1=ALU.mult))
                for tb in range(TB):
                    rs_wait(jobs[tb])
                    for half in range(2):
                        cs = slice(half * 512, (half + 1) * 512)
                        dve.scalar_tensor_tensor(out=x[:, tb, cs], in0=xn[:, tb, cs], scalar=rs(jobs[tb]),
                                                 in1=x[:, tb, cs], op0=ALU.mult, op1=ALU.add).then_inc(x_ready, 1)

            post_norm(("pm0", "pm1"), (1.0, 1.0), pm_row)
            turn(T_GLU)
            rs_wait("glu1")
            diagonal([rs("glu0"), rs("glu1")])
            hb, first = 2 * FC, P_GLU

            def glu_scale(c, r, n_gate):
                dve.wait_ge(piece_used, n_gate + 1)
                dve.tensor_tensor(g_act[:, r, :].rearrange("p (f t) -> p f t", f=2),
                                  bank(4 + 2 * r).rearrange("p (f t) -> p f t", f=2),
                                  r_row[:, :].unsqueeze(1).to_broadcast([P, 2, S]), ALU.mult).then_inc(gate_scaled, 1)

            def glu_mul(c, r, n_up):
                dve.wait_ge(act_out, hb + c + 1)
                dve.wait_ge(piece_used, n_up + 1)
                dve.tensor_tensor(g_mul[:, r, :], g_act[:, r, :], bank(5 + 2 * r), ALU.mult).then_inc(mul_out, 1)

            def glu_lo(c, r):
                dve.wait_ge(g_hi_ready, hb + c + 1)
                dve.tensor_tensor(g_lo[:, r, :], g_mul[:, r, :], g_hi[:, r, :], ALU.subtract).then_inc(g_lo_ready, 1)

            dve.wait_ge(row_ready, 2)
            glu_scale(0, 0, first)
            lo(first + RING)
            glu_mul(0, 0, first + 1)
            glu_lo(0, 0)
            lo(first + 1 + RING)

            def glu_chunk(c, j, i):
                n = first + 2 + 3 * j
                r = (j + 1) % 2
                ahead = lo if isinstance(i, int) else lo_loop
                a = (lambda k: (n + 6 * i + k + RING,)) if isinstance(i, int) else (lambda k: (n + k + RING, i))
                glu_scale(c + 1, r, n + 6 * i)
                ahead(*a(0))
                glu_mul(c + 1, r, n + 1 + 6 * i)
                glu_lo(c + 1, r)
                ahead(*a(1))
                ahead(*a(2))

            for j in range(2):
                glu_chunk(j, j, 0)
            with dve.Fori(1, (GC - 1) // 2 - 1) as i:
                for j in range(2):
                    glu_chunk(2 * i + j, j, i)
            i = (GC - 1) // 2 - 1
            for j in range(2):
                glu_chunk(2 * i + j, j, i)
            post_norm(("pf0", "pf1"), (rs("glu0"), rs("glu1")), pf_row)

        @block.tensor
        def _(pe):
            def product(dst, stat, mov, first, last):
                pe.matmul(dst, stat[0], mov[0], start=first, stop=False)
                pe.matmul(dst, stat[0], mov[1], start=False, stop=False)
                return pe.matmul(dst, stat[1], mov[0], start=False, stop=last)

            def h_block(k, tb=None):
                if tb is None:
                    return h_hi[:, k, :], h_lo[:, k, :]
                return h_hi[:, k, tb * P:(tb + 1) * P], h_lo[:, k, tb * P:(tb + 1) * P]

            def split(n):
                pe.wait_ge(lo_ready, n + 1)

            def turn(t, x_at=None, by_groups=False):
                n = T_BLOCKS[t]
                if by_groups:
                    parts = [(tb, 4 * g, 4 * g + 4) for g in range(2) for tb in range(TB)]
                elif x_at is not None:
                    parts = [(tb, 4 * g, 4 * g + 4) for tb in range(TB) for g in range(2)]
                else:
                    parts = [(tb, 0, n) for tb in range(TB)]
                for i, (tb, k0, k1) in enumerate(parts):
                    if x_at is not None:
                        pe.wait_ge(x_ready, x_at + i + 1)
                    else:
                        pe.wait_ge(xn_ready, XN_AT[t] + i + 1)
                    for k in range(k0, k1):
                        at = (k % 2) * S + tb * P
                        ins = pe.transpose(bank(4 + k // 2)[:, at:at + P],
                                           (x if x_at is not None else xn)[:, tb, k * P:(k + 1) * P], ident[:, :])
                        if tb == TB - 1 and (k % 2 or k == n - 1):
                            ins.then_inc(turned, 1)

            def h_wait(t, k):
                pe.wait_ge(h_lo_ready, t_base(t) + k // 2 + 1)

            def stationary_slice(slot, t, b, i, first_use=False):
                wh = w_hi[:, slot, :].rearrange("p (k c) -> p k c", k=KB)
                wl = w_lo[:, slot, :].rearrange("p (k c) -> p k c", k=KB)
                f = i // 2
                for k in range((i % 2) * KB // 2, (i % 2 + 1) * KB // 2):
                    if first_use and f == 0 and k % 2 == 0:
                        h_wait(t, k)
                    ins = product(bank(b)[:, f * S:(f + 1) * S],
                                  (wh[:, k, f * P:(f + 1) * P], wl[:, k, f * P:(f + 1) * P]),
                                  h_block(k), k == 0, k == KB - 1)
                if i == 3:
                    ins.then_inc(piece_used, 1)

            def stationary(slot, t, b, first_use=False):
                for i in range(4):
                    stationary_slice(slot, t, b, i, first_use)

            def moving_slice(first, j, banks, i):
                if i == 0:
                    split(first + j)
                wh, wl = part(w_hi, first + j, 4), part(w_lo, first + j, 4)
                tb = i // 2
                for k in (2 * (i % 2), 2 * (i % 2) + 1):
                    ins = product(bank(banks[tb]), h_block(4 * j + k, tb), (wh[:, k, :], wl[:, k, :]),
                                  j == 0 and k == 0, j == 1 and k == 3)
                if i == 3:
                    ins.then_inc(piece_used, 1)

            def moving(first, banks):
                for j in range(2):
                    for i in range(4):
                        moving_slice(first, j, banks, i)

            def out_piece(act_of, n_slot, first, last):
                wh = w_hi[:, n_slot, :].rearrange("p (k c) -> p k c", k=2)
                wl = w_lo[:, n_slot, :].rearrange("p (k c) -> p k c", k=2)
                for tb in range(TB):
                    for k in range(2):
                        for h in range(2):
                            ins = product(bank(2 * tb + h), act_of(k, tb),
                                          (wh[:, k, h * 512:(h + 1) * 512], wl[:, k, h * 512:(h + 1) * 512]),
                                          first and k == 0, last and k == 1)
                    if last and tb == 0:
                        ins.then_inc(acc_half, 1)
                ins.then_inc(piece_used, 1)

            def out_product(first, t):
                for j in range(4):
                    split(first + j)
                    h_wait(t, 2 * j)
                    out_piece(lambda k, tb: h_block(2 * j + k, tb), (first + j) % RING, j == 0, j == 3)

            pe.wait_ge(ident_ready, 1)
            pe.wait_ge(vecs_loaded, 16 * len(VEC))
            pe.transpose(bank(0)[:, 0:VECS], vecs[:, :], ident[0:VECS, 0:VECS]).then_inc(vecs_turned, 1)
            turn(T_AB)
            pe.wait_ge(gw_ready, 1)
            h_wait(T_AB, KB - 1)
            for tb in range(TB):
                for k in range(KB):
                    ins = product(bank(7)[:, 16 * tb:16 * tb + 16], h_block(k, tb), (gw_hi[:, k, :], gw_lo[:, k, :]),
                                  k == 0, k == KB - 1)
            ins.then_inc(gates_done, 1)
            pe.wait_ge(cols_ready, 1)
            for j in range(2):
                split(P_QK + j)
                stationary((P_QK + j) % RING, T_AB, (0, 2)[j])
                if j == 0:
                    pe.wait_ge(ws_loaded, 16)
                    for g in range(B_G):
                        ins = pe.transpose(bank(1)[:, g * P:(g + 1) * P], ws_raw[:, g, :], ident[:, :])
                    ins.then_inc(vecs_turned, 1)
            pe.wait_ge(gates_ready, 1)
            for dq in range(4):
                for tb in range(TB):
                    at = dq * S + tb * P
                    src = gates[:, 2 * tb + dq // 2, (dq % 2) * A_H:(dq % 2 + 1) * A_H]
                    ins = pe.transpose(bank(6, 2)[0:A_H, at:at + P], src, ident[:, :])
            ins.then_inc(rows_turned, 1)
            for j in range(2, 4):
                split(P_QK + j)
                if j == 2:
                    pe.wait_ge(cols_ready, 2)
                stationary((P_QK + j) % RING, T_AB, (1, 3)[j - 2])
            moving(P_VA, (4, 5))
            pe.wait_ge(rows_ready, 1)
            for q, rows in enumerate((a_row, mt_row)):
                for tb in range(TB):
                    for back in range(2):
                        at = 16 * q + 8 * tb + A_H * back
                        ins = pe.transpose(bank(6)[:, at:at + A_H], rows[0:A_H, back, tb * P:(tb + 1) * P],
                                           ident[0:A_H, 0:A_H])
            ins.then_inc(cols_turned, 1)
            pe.wait_ge(evac_qk, 3)
            moving(P_VB, (0, 1))

            def spread_m(u):
                h, back = u // 2, u % 2
                if u == 0:
                    pe.wait_ge(evac_vb, 2)
                    pe.wait_ge(consts_ready, 3)
                if u >= 2:
                    pe.wait_ge(w_ready, u - 1)
                b = bank(u % 2)
                whole, half = (((0, 256), (384, 512)), ((256, 512), (0, 128)))[back]
                m = m_row[0:A_H, back, :]
                msk = mask[:, back, :]
                pe.matmul(b[:, whole[0]:whole[1]], nsel[0:A_H, h, :], m, start=True, stop=False)
                wd = whole[0] + (P if back else 0)
                pe.matmul(b[:, wd:wd + P], ident[:, :], msk, start=False, stop=True)
                pe.matmul(b[:, half[0]:half[1]], nsel[0:A_H, h, :], m[:, P:S] if not back else m[:, 0:P],
                          start=True, stop=False)
                pe.matmul(b[:, half[0]:half[1]], ident[:, :], msk, start=False, stop=True).then_inc(spread, 1)

            def head_scores(h):
                if h == 0:
                    pe.wait_ge(silu_done, 2)
                    pe.wait_ge(evac_qk, 4)
                if h == 2:
                    pe.wait_ge(silu_done, 4)
                if h >= 2:
                    pe.wait_ge(g_ready, 2 * h - 2)
                for s0 in range(2):
                    ins = pe.matmul(bank(2 + h % 2)[:, s0 * S:(s0 + 1) * S], qkT[:, 4 + h, s0 * P:(s0 + 1) * P],
                                    qkT[:, h, :], start=True, stop=True)
                ins.then_inc(s_ready, 1)

            def unit_pv(u):
                h, back = u // 2, u % 2
                if u == 0:
                    pe.wait_ge(evac_v, 2)
                pe.wait_ge(g_ready, u + 1)
                if u >= 2:
                    pe.wait_ge(unit_done, u - 1)
                for t0, sources in enumerate([((0,), (0, 1)), ((0, 1), (1,))][back]):
                    for s0 in sources:
                        ins = pe.matmul(bank(4 + u % 2)[:, t0 * (A_D + 1):(t0 + 1) * (A_D + 1)],
                                        score[:, u % 2, 2 * s0 + t0, :], v_ext[:, s0, h, :],
                                        start=s0 == sources[0], stop=s0 == sources[-1])
                ins.then_inc(o_ready, 1)

            def unit_step(u):
                if u + 2 < 2 * A_H:
                    spread_m(u + 2)
                if u % 2 == 1 and u // 2 + 1 < A_H:
                    head_scores(u // 2 + 1)
                if u == 2 * A_H - 1:
                    pe.wait_ge(vbn_ready, 1)
                    pe.wait_ge(w_ready, 2 * A_H)
                    for g in range(B_G):
                        ins = pe.matmul(bank(0, 2)[:, g * S:(g + 1) * S].rearrange("p (n c) -> p n c", n=TB),
                                        wsT[:, g, :], vb[:, :, g * 128:(g + 1) * 128], start=True, stop=True)
                    ins.then_inc(sgu_done, 1)
                unit_pv(u)

            pe.wait_ge(gcols_ready, 2)
            for n in range(4):
                first, j = (P_OA, P_U)[n // 2], n % 2
                if n == 2:
                    pe.wait_ge(evac_oa, 2)
                for i in range(4):
                    moving_slice(first, j, (6, 7), i)
                    if n == 0 and i == 0:
                        spread_m(0)
                        head_scores(0)
                        spread_m(1)
                    if i % 2:
                        unit_step(2 * n + i // 2)
            pe.wait_ge(evac_u, 2)
            turn(T_AMIX)
            out_product(P_AOUT, T_AMIX)

            def ffn(first, hb, t, x_at):
                turn(t, x_at)
                split(first)
                stationary(first % RING, t, 4, True)

                def chunk(c, j, i):
                    n = first + 1 + 2 * j
                    r1 = (j + 1) % 3
                    split(n + 6 * i)
                    if not (isinstance(c, int) and c < 2):
                        pe.wait_ge(act_out, hb + c - 1)
                    stationary(n % RING, t, 4 + r1)
                    split(n + 1 + 6 * i)
                    pe.wait_ge(g_lo_ready, hb + c + 1)
                    down(j % 3, (n + 1) % RING, isinstance(c, int) and c == 0, False)

                def down(r, slot, start, stop):
                    out_piece(lambda k, tb: (g_hi[:, r, k * S + tb * P:k * S + (tb + 1) * P],
                                             g_lo[:, r, k * S + tb * P:k * S + (tb + 1) * P]), slot, start, stop)

                for j in range(3):
                    chunk(j, j, 0)
                with pe.Fori(1, (FC - 1) // 3) as i:
                    for j in range(3):
                        chunk(3 * i + j, j, i)
                n = first + 2 * FC - 1
                split(n)
                pe.wait_ge(g_lo_ready, hb + FC)
                down((FC - 1) % 3, n % RING, False, True)

            ffn(P_FFN0, 0, T_FFN0, X_AT["ffn0"])

            turn(T_C, X_AT["c"])
            for j, (k0, k1) in enumerate(((0, 3), (3, 6), (6, 8))):
                n = P_CIN + j
                split(n)
                wh, wl = part(w_hi, n, k1 - k0), part(w_lo, n, k1 - k0)
                for tb in range(TB):
                    for k in range(k0, k1):
                        if tb == 0:
                            h_wait(T_C, k)
                        for c0, c1 in ((0, 512), (512, C_IN)):
                            ins = product(bank(2 * tb, 2)[:, c0:c1], h_block(k, tb),
                                          (wh[:, k - k0, c0:c1], wl[:, k - k0, c0:c1]), k == 0, k == KB - 1)
                ins.then_inc(piece_used, 1)
            turn(T_LAT)
            pe.wait_ge(krr_ready, 1)
            pe.wait_ge(krr_zero, 1)
            pe.wait_ge(h_lo_ready, t_base(T_C) + 4)
            for tb in range(TB):
                ins = pe.transpose(psum[0:C_QK, 7, tb * P:(tb + 1) * P], krr[:, tb, :], ident[:, :])
            ins.then_inc(krr_turned, 1)
            h_wait(T_LAT, 4)
            for j in range(3):
                n = P_UQ + j
                split(n)
                wh, wl = part(w_hi, n, 3), part(w_lo, n, 3)
                for tb in range(TB):
                    for k in range(3):
                        ins = product(bank(2 * j + tb), h_block(k, tb), (wh[:, k, :], wl[:, k, :]), k == 0, k == 2)
                ins.then_inc(piece_used, 1)
            pe.wait_ge(krT_ready, 1)
            for j in range(2):
                n = P_UKV + j
                split(n)
                wh, wl = part(w_hi, n, 2), part(w_lo, n, 2)
                pe.wait_ge(evac_q, j + 1)
                for pair in range(4):
                    hs = slice(pair * P, (pair + 1) * P)
                    for k in range(2):
                        product(bank((6, 2)[j], 2)[:, pair * S:(pair + 1) * S],
                                (wh[:, k, hs], wl[:, k, hs]), h_block(3 + k), k == 0, k == 1)
                if j == 1:
                    pe.wait_ge(evac_q, 3)
                for tb in range(TB):
                    for k in range(2):
                        ins = product(bank((0, 4)[j] + tb), h_block(3 + k, tb), (wh[:, k, 512:], wl[:, k, 512:]),
                                      k == 0, k == 1)
                ins.then_inc(piece_used, 1)
            pe.wait_ge(q_roped, 2)
            pe.wait_ge(evac_k2, 1)
            pe.wait_ge(evac_vc, 1)
            for n in range(8):
                if n >= 4:
                    if n % 2:
                        pe.wait_ge(qf_ready, (n - 4) // 2 + 1)
                    else:
                        pe.wait_ge(evac_k2, 2 + (n - 4) // 2 + 1)
                for i in range(2):
                    h = 2 * n + i
                    for tb in range(TB):
                        at = i * S + tb * P
                        ins = pe.transpose(bank((6, 7, 0, 1)[n % 4])[0:C_QK, at:at + P],
                                           q_tok[:, tb, h * C_QK:(h + 1) * C_QK], ident[:, :])
                ins.then_inc(qf_turned, 1)
            pe.wait_ge(qf_ready, 4)
            pe.wait_ge(evac_k2, 6)
            pe.wait_ge(evac_vc, 2)
            pe.wait_ge(kfT_rope, 1)

            def c_scores(h):
                if h >= 2:
                    pe.wait_ge(at_exp[0], h - 1)
                for qb in range(2):
                    ins = pe.matmul(bank(4 + h % 2)[:, qb * S:(qb + 1) * S], qfT[0:C_QK, h, qb * P:(qb + 1) * P],
                                    kfT[0:C_QK, h, :], start=True, stop=True)
                ins.then_inc(at_s[0], 1)

            def c_turn(h):
                pe.wait_ge(at_exp[0], h + 1)
                if h >= 2:
                    pe.wait_ge(at_ptsb[0], h - 1)
                for kb in range(2):
                    for qb in range(2):
                        at = kb * S + qb * P
                        ins = pe.transpose(bank(6 + h % 2)[:, at:at + P],
                                           prob[:, h % 2, qb * S + kb * P:qb * S + (kb + 1) * P], ident[:, :])
                ins.then_inc(at_pt[0], 1)

            def c_pv(h):
                pe.wait_ge(at_ptsb[0], h + 1)
                for qb in range(2):
                    for kb in range(2):
                        ins = pe.matmul(bank(2 * qb, 2)[:, h * C_V:(h + 1) * C_V],
                                        probT[:, h % 2, kb * S + qb * P:kb * S + (qb + 1) * P],
                                        v_tok[:, kb, h * C_V:(h + 1) * C_V], start=kb == 0, stop=kb == 1)
                ins.then_inc(at_pv[0], 1)

            def pipeline(n, *stages):
                for i in range(n + len(stages) - 1):
                    for lag, stage in enumerate(stages):
                        if 0 <= i - lag < n:
                            stage(i - lag)

            pipeline(C_H, c_scores, c_turn, c_pv)
            turn(T_CMIX, by_groups=True)
            out_product(P_COUT, T_CMIX)
            ffn(P_FFN1, FC, T_FFN1, X_AT["ffn1"])

            def spread_row(n, b):
                pe.wait_ge(diag_ready, 2 * n + 2)
                for tb in range(TB):
                    ins = pe.matmul(bank(b)[:, tb * P:(tb + 1) * P], ones[:, :], diag[:, tb, :], start=True, stop=True)
                ins.then_inc(row_spread, 1)

            turn(T_2, X_AT["fin"])
            h_wait(T_2, KB - 1)
            moving(P_V2, (0, 1))
            moving_slice(P_V2 + 2, 0, (2, 3), 0)
            spread_row(0, 5)
            for i in range(1, 4):
                moving_slice(P_V2 + 2, 0, (2, 3), i)
            for i in range(4):
                moving_slice(P_V2 + 2, 1, (2, 3), i)

            def scores2(h):
                if h % 4 == 0:
                    pe.wait_ge(evac_qk2, h // 2 + 2)
                if h == 0:
                    pe.wait_ge(evac_v2, 4)
                if h >= 2:
                    pe.wait_ge(at_max[1], h - 1)
                rows = slice(HD2 * (h % 2), HD2 * (h % 2 + 1))
                for qb, (c0, c1) in enumerate(((0, P), (P, 3 * P))):
                    ins = pe.matmul(bank(2 + h % 2)[:, c0:c1], qT2[rows, h // 2, qb * P:(qb + 1) * P],
                                    kT2[rows, h // 2, 0:c1 - c0], start=True, stop=True)
                ins.then_inc(at_s[1], 1)

            def turn2(h):
                pe.wait_ge(at_exp[1], h + 1)
                if h >= 2:
                    pe.wait_ge(at_ptsb[1], h - 1)
                for b in range(3):
                    ins = pe.transpose(bank(4 + h % 2)[:, b * P:(b + 1) * P], prob2[:, h % 2, b * P:(b + 1) * P],
                                       ident[:, :])
                ins.then_inc(at_pt[1], 1)

            def pv2(h):
                pe.wait_ge(at_ptsb[1], h + 1)
                if h == 8:
                    pe.wait_ge(xn_ready, XN_AT[T_2MIX] + 2)
                for qb, blocks in enumerate((((0, 0),), ((1, 0), (2, 1)))):
                    for b, kb in blocks:
                        ins = pe.matmul(bank(qb)[:, (h % 8) * HD2:(h % 8 + 1) * HD2], probT2[:, h % 2, b * P:(b + 1) * P],
                                        v2[:, kb, h * HD2:(h + 1) * HD2], start=kb == 0, stop=kb == qb)
                ins.then_inc(at_pv[1], 1)

            def step2(i):
                if i < H2:
                    scores2(i)
                if 0 <= i - 1 < H2:
                    turn2(i - 1)
                if 0 <= i - 2 < H2:
                    pv2(i - 2)

            for j in range(8):
                split(P_QK2 + j)
                if j >= 2:
                    pe.wait_ge(evac_qk2, j - 1)
                for i in range(4):
                    stationary_slice((P_QK2 + j) % RING, T_2, 6 + j % 2, i)
                    if j >= 2 and i % 2:
                        step2(2 * (j - 2) + i // 2)
            for i in range(12, H2 + 2):
                step2(i)
            turn(T_2MIX, by_groups=True)
            out_product(P_O2, T_2MIX)

            turn(T_GLU, X_AT["glu"])
            hb, first = 2 * FC, P_GLU

            def gate_up(c, r, n0, i):
                split(n0 + 6 * i)
                if not (isinstance(c, int) and c < 2):
                    pe.wait_ge(gate_scaled, c - 1)
                stationary(n0 % RING, T_GLU, 4 + 2 * r, isinstance(c, int) and c == 0)
                split(n0 + 1 + 6 * i)
                if isinstance(c, int) and c == 0:
                    stationary_slice((n0 + 1) % RING, T_GLU, 5, 0)
                    spread_row(1, 0)
                    for q in range(1, 4):
                        stationary_slice((n0 + 1) % RING, T_GLU, 5, q)
                    return
                if not (isinstance(c, int) and c < 2):
                    pe.wait_ge(mul_out, hb + c - 1)
                stationary((n0 + 1) % RING, T_GLU, 5 + 2 * r)

            def glu_down(c, r, n0, i, start, stop):
                split(n0 + 6 * i)
                pe.wait_ge(g_lo_ready, hb + c + 1)
                out_piece(lambda k, tb: (g_hi[:, r, k * S + tb * P:k * S + (tb + 1) * P],
                                         g_lo[:, r, k * S + tb * P:k * S + (tb + 1) * P]), n0 % RING, start, stop)

            gate_up(0, 0, first, 0)

            def glu_chunk(c, j, i):
                n = first + 2 + 3 * j
                gate_up(c + 1, (j + 1) % 2, n, i)
                glu_down(c, j % 2, n + 2, i, isinstance(c, int) and c == 0, False)

            for j in range(2):
                glu_chunk(j, j, 0)
            with pe.Fori(1, (GC - 1) // 2) as i:
                for j in range(2):
                    glu_chunk(2 * i + j, j, i)
            glu_down(GC - 1, (GC - 1) % 2, PIECES - 1, 0, False, True)


_INS = ["x", "positions", "ab_norm", "ab_w_in", "ab_conv", "ab_gate_b", "ab_head_g", "ab_v_g", "ab_ws", "ab_bs",
        "ab_w_out", "c_norm", "c_w_in", "c_q_g", "c_kv_g", "c_w_uq", "c_w_ukv", "c_w_out", "ffn_norm", "ffn_w1",
        "ffn_w2", "final_norm", "g_pre_mix_2", "g_post_mix_2", "w_qkv_2", "w_o_2", "rel_bias_2", "g_pre_ffn_2",
        "g_post_ffn_2", "w_gate_2", "w_up_2", "w_down_2"]


def kernel(**inputs):
    import numpy as _np
    import concourse.bacc as _bacc
    from concourse import mybir as _mybir
    from concourse.bass_utils import run_bass_kernel_spmd as _run

    nc = _bacc.Bacc("TRN2", target_bir_lowering=False, num_devices=1)
    arrays, d = {}, {}
    for name in _INS:
        a = _np.ascontiguousarray(inputs[name])
        arrays[f"in_{name}"] = a
        d[name] = nc.dram_tensor(f"in_{name}", a.shape, _mybir.dt.from_np(a.dtype), kind="ExternalInput").ap()
    out = nc.dram_tensor("out", (1, S, D), _mybir.dt.float32, kind="ExternalOutput").ap()
    build(nc, d, out)
    r = _run(nc, [arrays], core_ids=[0])
    return r.results[0]["out"]
```

```python
import math
from contextlib import ExitStack

import concourse.bass as bass
import numpy as np
from concourse import mybir

F32 = mybir.dt.float32
F32R = mybir.dt.float32r
I32 = mybir.dt.int32
ALU = mybir.AluOpType
ACT = mybir.ActivationFunctionType
AX = mybir.AxisListType

P = 128
D = 1024
KB = D // P
S = 256
TB = S // P
PIECE = 2048
RING = 3
EPS = 1e-6
NEG = -1.0e30

A_W, A_H, A_D, TAPS = 512, 4, 128, 5
PAD = (TAPS - 1) // 2
B_W, B_G = 512, 4
C_H, C_NOPE, C_ROPE, C_V = 16, 64, 32, 64
C_QK = C_NOPE + C_ROPE
HALF = C_ROPE // 2
Q_LORA, KV_LORA = 384, 256
C_IN = Q_LORA + KV_LORA + C_ROPE
CH = 256
D_FF = 4096
FC = D_FF // CH
H2, HD2, CHUNK = 16, 64, 64
REL_CLIP = 128
N_REL = CHUNK - 1 + REL_CLIP + 1
EXT = 384
D_FF2 = 2816
GC = D_FF2 // CH

P_QK, P_VA, P_VB, P_U, P_OA, P_AOUT = 0, 4, 6, 8, 10, 12
P_FFN0 = 16
P_CIN = P_FFN0 + 2 * FC
P_UQ = P_CIN + 3
P_UKV = P_UQ + 3
P_COUT = P_UKV + 2
P_FFN1 = P_COUT + 4
P_V2 = P_FFN1 + 2 * FC
P_QK2 = P_V2 + 4
P_O2 = P_QK2 + 8
P_GLU = P_O2 + 4
PIECES = P_GLU + 3 * GC

QK_ORDER = (0, 2, 1, 3)

T_AB, T_AMIX, T_FFN0, T_C, T_LAT, T_CMIX, T_FFN1, T_2, T_2MIX, T_GLU = range(10)
T_BANKS = [4, 4, 4, 4, 3, 4, 4, 4, 4, 4]
DIRECT = (T_CMIX, T_2MIX)
QF_BANKS = (6, 7, 0, 1, 6, 7, 2, 3)
OUT2 = (0, 1, 6, 7)
T_BLOCKS = [8, 8, 8, 8, 5, 8, 8, 8, 8, 8]

VEC = {"ab_norm": 0, "ab_head_g": 8, "ab_bs": 12, "c_norm": 16, "c_q_g": 24, "c_kv_g": 27,
       "ffn_norm": 29, "g_pre_mix_2": 45, "g_pre_ffn_2": 53, "final_norm": 61, "ab_conv": 69}
VECS = 69 + TAPS * KB

JOBS = {}
for _name, _n, _w in [("ab0", 1, D), ("ab1", 1, D), ("vb", 8, 128), ("ha", 8, 128), ("ffn00", 1, D), ("ffn01", 1, D),
                      ("c0", 1, D), ("c1", 1, D), ("cq0", 1, Q_LORA), ("ckv0", 1, KV_LORA),
                      ("cq1", 1, Q_LORA), ("ckv1", 1, KV_LORA), ("ffn10", 1, D),
                      ("ffn11", 1, D), ("fin0", 1, D), ("fin1", 1, D), ("pre0", 1, D), ("pre1", 1, D),
                      ("pm0", 1, D), ("pm1", 1, D), ("glu0", 1, D), ("glu1", 1, D), ("pf0", 1, D), ("pf1", 1, D)]:
    JOBS[_name] = (sum(v[1] for v in JOBS.values()), _n, _w)
JOB_AT = {name: i for i, name in enumerate(JOBS)}
SS_ACT = ["ab0", "ab1", "ffn00", "ffn01", "c0", "c1", "cq0", "ckv0", "cq1", "ckv1", "ffn10", "ffn11", "fin0", "fin1",
          "pre0", "pre1", "pm0", "pm1", "glu0", "glu1", "pf0", "pf1"]
SQUARED = ("ffn00", "ffn01", "ffn10", "ffn11")
SS_DVE = ["vb", "ha"]
X_AT = {"ffn0": 0, "c": 4, "ffn1": 8, "fin": 12, "pre": 16, "glu": 20, "out": 24}
XN_AT = {T_AMIX: 0, T_LAT: 2}
PAIRS = {t: (2, 3, 0, 1) if t == T_AMIX else tuple(range(T_BANKS[t])) for t in range(len(T_BANKS))}

TWO_PI = 2 * math.pi
PI_1 = 6.28125
PI_2 = float(np.float32(round((TWO_PI - PI_1) * 2 ** 20) / 2 ** 20))
PI_3 = TWO_PI - PI_1 - PI_2
ROUND = 1.5 * 2.0 ** 23
PI_IN = 3.1415925


def build(nc, d, out):
    ctx = ExitStack()
    with ctx:
        def sb(name, shape, dt=F32):
            return ctx.enter_context(nc.sbuf_tensor(name, shape, dt))

        def sem(name):
            return ctx.enter_context(nc.semaphore(name))

        psum = ctx.enter_context(nc.psum_tensor("psum", [P, 8, 512], F32))
        raw = sb("raw", [P, RING, PIECE])
        w_hi = sb("w_hi", [P, RING, PIECE], F32R)
        w_lo = sb("w_lo", [P, RING, PIECE], F32R)
        x = sb("x", [P, TB, D])
        xn = sb("xn", [P, TB, D])
        h_hi = sb("h_hi", [P, KB, S], F32R)
        h_lo = sb("h_lo", [P, KB, S], F32R)
        junk = sb("junk", [P, D])
        g_act = sb("g_act", [P, 3, 2 * S])
        g_mul = sb("g_mul", [P, 3, 2 * S])
        g_hi = sb("g_hi", [P, 3, 2 * S], F32R)
        g_lo = sb("g_lo", [P, 3, 2 * S], F32R)
        ident = sb("ident", [P, P])
        mask = sb("mask", [P, 2, P])
        vecs = sb("vecs", [VECS, P])
        cols = sb("cols", [P, VECS])
        mhalf = sb("mhalf", [P, 8])
        mone = sb("mone", [P, 1])
        ones = sb("ones", [P, P])
        diag = sb("diag", [P, TB, P])
        r_row = sb("r_row", [P, S])
        gain2 = sb("gain2", [P, KB])
        r_both = sb("r_both", [P, TB])
        n_stat = sum(v[1] for v in JOBS.values())
        ssq = sb("ssq", [P, n_stat])
        msq = sb("msq", [P, n_stat])
        rstd = sb("rstd", [P, n_stat])
        pos_i = sb("pos_i", [P, TB], I32)
        pos_f = sb("pos_f", [P, TB])
        freq = sb("freq", [P, HALF])
        ang = sb("ang", [P, TB, HALF])
        turns = sb("turns", [P, TB, HALF])
        ang2 = sb("ang2", [P, 2, TB, HALF])
        trig = sb("trig", [P, 2, TB, HALF])
        rel_t = sb("rel_t", [H2, N_REL])
        rel_ext = sb("rel_ext", [H2, EXT])
        rel_dram = nc.dram_tensor("rel_scratch", (H2, P, EXT), F32, kind="Internal")

        ARENA = 16640
        arena = sb("arena", [P, ARENA])

        class Carve:
            def __init__(self):
                self.at = 0

            def __call__(self, *shape):
                n = int(np.prod(shape))
                assert self.at + n <= ARENA, (self.at, n)
                v = arena[:, self.at:self.at + n]
                self.at += n
                if len(shape) == 2:
                    v = v.rearrange("p (a b) -> p a b", a=shape[0])
                if len(shape) == 3:
                    v = v.rearrange("p (a b c) -> p a b c", a=shape[0], b=shape[1])
                return v

        ca = Carve()
        qk_pad = ca(8, S + 2 * PAD)
        qk_conv = ca(8, S)
        qkT = qk_conv
        v_ext = ca(TB, A_H, A_D + 1)
        oa = ca(TB, A_W)
        u_act = ca(TB, B_W)
        vb = ca(TB, B_W)
        sq_tmp = ca(TB, A_W)
        hsum = ca(TB, A_W)
        decay = g_act[:, 0:2, :].rearrange("p u (b t) -> p u b t", b=4)
        score = g_mul[:, 0:2, :].rearrange("p u (b t) -> p u b t", b=4)
        ws_raw = g_act[:, 2, :].rearrange("p (g t) -> p g t", g=B_G)
        wsT = ca(B_G, P)
        vg_row = ca(B_W)
        gw_raw = ca(KB, 16)
        gb_row = ca(16)
        gates = ca(4, 8)
        g_abs = ca(4, 4)
        g_exp = ca(4, 4)
        g_ln = ca(4, 4)
        cumf = ca(2, S)
        a_row = ca(2, S)
        m_row = ca(2, S)
        mt_row = ca(2, S)
        ones_row = ca(S)
        nsel = ca(A_H, P)
        a_col = ca(TB, 8)
        e_col = ca(TB, 8)
        dmax = ca(2)
        dinv = ca(2)
        gw_hi = sb("gw_hi", [P, KB, 16], F32R)
        gw_lo = sb("gw_lo", [P, KB, 16], F32R)

        cc = Carve()
        q_tok = cc(TB, C_H * C_QK)
        kfT = cc(C_H, S)
        qfT = cc(C_H, S)
        v_tok = cc(TB, D)
        prob = cc(3, 2 * S)
        probT = cc(2, 2 * S)
        krr = cc(TB, C_QK)
        krs = cc(TB, C_ROPE)
        krT = cc(S)
        nmax = cc(2, C_H)
        psm = cc(2, C_H)
        pinv = cc(2, C_H)
        rp = [xn[:, :, i * S:(i + 1) * S].rearrange("p t (h e) -> p t h e", h=C_H) for i in range(4)]
        rk = [junk[:, i * 32:(i + 1) * 32].rearrange("p (t e) -> p t e", t=TB) for i in range(4)]

        c2 = Carve()
        qT2 = c2(8, S)
        kT2 = c2(8, S)
        v2 = c2(TB, D)
        s2 = c2(2, 3 * P)
        prob2 = c2(3, 3 * P)
        probT2 = c2(2, 3 * P)
        nmax2 = c2(2, H2)
        psm2 = c2(2, H2)
        pinv2 = c2(2, H2)
        bias2 = c2(H2, S)
        fin_row = c2(D)
        pm_row = c2(D)
        pf_row = c2(D)

        arrived = [sem(f"arrived{i}") for i in range(RING)]
        hi_ready = sem("hi_ready")
        lo_ready = sem("lo_ready")
        hi_half = sem("hi_half")
        lo_half = sem("lo_half")
        piece_used = sem("piece_used")
        x_loaded = [sem(f"x_loaded{tb}") for tb in range(TB)]
        norm_loaded = sem("norm_loaded")
        vecs_loaded = sem("vecs_loaded")
        ws_loaded = sem("ws_loaded")
        gw_loaded = sem("gw_loaded")
        ab_small = sem("ab_small")
        vg_loaded = sem("vg_loaded")
        pos_loaded = sem("pos_loaded")
        rel_loaded = sem("rel_loaded")
        rel_stored = sem("rel_stored")
        rows2_loaded = sem("rows2_loaded")
        bias_loaded = sem("bias_loaded")
        x_stored = sem("x_stored")
        ident_ready = sem("ident_ready")
        consts_ready = sem("consts_ready")
        pool_step = sem("pool_step")
        dve_step = sem("dve_step")
        act_step = sem("act_step")
        vecs_turned = sem("vecs_turned")
        cols_ready = sem("cols_ready")
        gw_hi_ready = sem("gw_hi_ready")
        gw_ready = sem("gw_ready")
        ss_act = sem("ss_act")
        ss_dve = sem("ss_dve")
        rstd_ready = sem("rstd_ready")
        x_ready = sem("x_ready")
        xn_ready = sem("xn_ready")
        turned = sem("turned")
        h_hi_ready = sem("h_hi_ready")
        h_lo_ready = sem("h_lo_ready")
        acc_half = sem("acc_half")
        gates_done = sem("gates_done")
        gate_abs = sem("gate_abs")
        gate_ln = sem("gate_ln")
        gates_ready = sem("gates_ready")
        rows_turned = sem("rows_turned")
        rows_ready = sem("rows_ready")
        cols_turned = sem("cols_turned")
        gcols_ready = sem("gcols_ready")
        evac_qk = sem("evac_qk")
        conv_done = sem("conv_done")
        silu_done = sem("silu_done")
        diag_ready = sem("diag_ready")
        row_spread = sem("row_spread")
        row_ready = sem("row_ready")
        gate_scaled = sem("gate_scaled")
        r_both_ready = sem("r_both_ready")
        evac_v = sem("evac_v")
        evac_oa = sem("evac_oa")
        evac_u = sem("evac_u")
        evac_vb = sem("evac_vb")
        vbn_ready = sem("vbn_ready")
        spread = sem("spread")
        w_ready = sem("w_ready")
        s_ready = sem("s_ready")
        g_ready = sem("g_ready")
        o_ready = sem("o_ready")
        unit_done = sem("unit_done")
        sgu_done = sem("sgu_done")
        sgu_read = sem("sgu_read")
        cin_half = sem("cin_half")
        rel_built = sem("rel_built")
        trig_in = sem("trig_in")
        trig_ready = sem("trig_ready")
        act_out = sem("act_out")
        mul_out = sem("mul_out")
        g_hi_ready = sem("g_hi_ready")
        g_lo_ready = sem("g_lo_ready")
        krr_ready = sem("krr_ready")
        krr_turned = sem("krr_turned")
        krT_ready = sem("krT_ready")
        kfT_rope = sem("kfT_rope")
        krr_zero = sem("krr_zero")
        evac_k = sem("evac_k")
        evac_k2 = sem("evac_k2")
        evac_vc = sem("evac_vc")
        evac_vc1 = sem("evac_vc1")
        evac_q = sem("evac_q")
        q_roped = sem("q_roped")
        qf_turned = sem("qf_turned")
        qf_ready = sem("qf_ready")
        at_s, at_max, at_exp, at_norm, at_pt, at_ptsb, at_pv = [
            [sem(f"{n}{i}") for i in range(2)]
            for n in ("scores", "maxed", "exped", "normed", "pturned", "pcopied", "pv")]
        evac_qk2 = sem("evac_qk2")
        evac_v2 = sem("evac_v2")
        bias_ready = sem("bias_ready")

        w_in = d["ab_w_in"][0].rearrange("(k p) n -> p k n", p=P)
        w_uv0 = 4 * A_W + 4 * A_H

        def rows_of(w, k0, k1):
            return w.rearrange("(k p) n -> p k n", p=P)[:, k0:k1, :]

        def cols_of(w, k0, k1, c0, c1):
            return w.rearrange("(k p) n -> p k n", p=P)[:, k0:k1, c0:c1]

        ab_w, c_w, qkv = d["ab_w_in"][0], d["c_w_in"][0], d["w_qkv_2"][0]
        SRC = {}
        for j in range(4):
            SRC[P_QK + j] = cols_of(ab_w, 0, KB, QK_ORDER[j] * CH, (QK_ORDER[j] + 1) * CH)
        for first, c0 in ((P_VA, 1024), (P_OA, 1536), (P_U, w_uv0), (P_VB, w_uv0 + B_W)):
            for j in range(2):
                SRC[first + j] = cols_of(ab_w, 4 * j, 4 * j + 4, c0, c0 + 512)
        for first, w in ((P_AOUT, d["ab_w_out"][0]), (P_COUT, d["c_w_out"][0]), (P_O2, d["w_o_2"][0])):
            for j in range(4):
                rows = PAIRS[T_AMIX][j] if first == P_AOUT else j
                SRC[first + j] = rows_of(w, 2 * rows, 2 * rows + 2)
        for j, (k0, k1) in enumerate(((0, 3), (3, 6), (6, 8))):
            SRC[P_CIN + j] = rows_of(c_w, k0, k1)
        for j in range(2):
            SRC[P_UKV + j] = cols_of(d["c_w_ukv"][0], 0, 2, j * 1024, (j + 1) * 1024)
        for j in range(3):
            SRC[P_UQ + j] = cols_of(d["c_w_uq"][0], 0, 3, j * 512, (j + 1) * 512)
        for j in range(8):
            c0 = (j % 2) * D + (j // 2) * CH
            SRC[P_QK2 + j] = cols_of(qkv, 0, KB, c0, c0 + CH)
        for n in range(2):
            for j in range(2):
                SRC[P_V2 + 2 * n + j] = cols_of(qkv, 4 * j, 4 * j + 4, 2 * D + n * 512, 2 * D + (n + 1) * 512)

        def width(n):
            if n in SRC:
                return SRC[n].shape[1] * SRC[n].shape[2]
            return PIECE

        def part(t, n, a):
            w = width(n)
            return t[:, n % RING, 0:w].rearrange("p (a b) -> p a b", a=a)

        def views(n, t, is_raw):
            w = t[:, n % RING, 0:width(n)]
            if not P_UKV <= n < P_UKV + 2:
                return [w]
            if is_raw:
                w = w.rearrange("p (k h v e) -> p v k h e", k=2, h=8, v=2)
            else:
                w = w.rearrange("p (k v h e) -> p v k h e", k=2, h=8, v=2)
            return [w[:, 0], w[:, 1]]

        def t_base(t):
            return sum(T_BANKS[:t])

        def turned_base(t):
            return sum(T_BANKS[s] for s in range(t) if s not in DIRECT)

        def mix_part(t, q, h, g):
            if t == T_2MIX and q < 3:
                return g[:, q, :]
            return h[:, 2 * q:2 * q + 2, :].rearrange("p k s -> p (k s)")

        def bank(b, n=1):
            return psum[:, b:b + n, :].rearrange("p b c -> p (b c)")

        def col(name, i):
            c = VEC[name] + i
            return cols[:, c:c + 1]

        def gain(t, k):
            if t == T_AB:
                return col("ab_norm", k)
            if t == T_AMIX:
                return col("ab_head_g", k) if k < 4 else None
            if t == T_FFN0:
                return col("ffn_norm", k)
            if t == T_C:
                return col("c_norm", k)
            if t == T_LAT:
                return col("c_q_g", k) if k < 3 else col("c_kv_g", k - 3)
            if t == T_FFN1:
                return col("ffn_norm", 8 + k)
            if t == T_2:
                return gain2[:, k:k + 1]
            if t == T_GLU:
                return col("g_pre_ffn_2", k)
            return None

        def load_vec(engine, name):
            r0, v = VEC[name], d[name]
            if name == "ab_conv":
                v = v[0].rearrange("w (k p) -> (w k) p", p=P)
            elif name == "ab_bs":
                v = v[0]
            elif name == "final_norm":
                v = v.rearrange("(k p) -> k p", p=P)
            else:
                v = v.rearrange("l (k p) -> (l k) p", p=P)
            return engine.dma_start(vecs[r0:r0 + v.shape[0], :], v)

        block = ctx.enter_context(nc.Block())

        @block.sync
        def _(sp):
            def load(n, slot, src, wide=PIECE, a=None):
                if not (isinstance(n, int) and n < RING):
                    sp.wait_ge(lo_ready, n - RING + 1)
                dst = raw[:, slot, 0:wide].rearrange("p (a b) -> p a b", a=a)
                sp.dma_start(dst, src).then_inc(arrived[slot], 16)

            def load_static(n):
                load(n, n % RING, SRC[n], width(n), SRC[n].shape[1])

            def ffn(first, w1, w2):
                w1v = w1.rearrange("(k p) n -> p k n", p=P)
                w2v = w2.rearrange("(k p) n -> p k n", p=P)
                load(first, first % RING, w1v[:, :, 0:CH], a=KB)
                with sp.Fori(0, (FC - 1) // 3) as i:
                    for j in range(3):
                        n = first + 1 + 2 * j
                        load(n + 6 * i, n % RING, w1v[:, :, bass.ds((3 * i + j + 1) * CH, CH)], a=KB)
                        load(n + 1 + 6 * i, (n + 1) % RING, w2v[:, bass.ds((3 * i + j) * 2, 2), :], a=2)
                n = first + 2 * FC - 1
                load(n, n % RING, w2v[:, 2 * FC - 2:2 * FC, :], a=2)

            def glu(first):
                wg = d["w_gate_2"][0].rearrange("(k p) n -> p k n", p=P)
                wu = d["w_up_2"][0].rearrange("(k p) n -> p k n", p=P)
                wd = d["w_down_2"][0].rearrange("(k p) n -> p k n", p=P)
                load(first, first % RING, wg[:, :, 0:CH], a=KB)
                load(first + 1, (first + 1) % RING, wu[:, :, 0:CH], a=KB)
                with sp.Fori(0, GC - 1) as c:
                    n = first + 2
                    load(n + 3 * c, n % RING, wg[:, :, bass.ds((c + 1) * CH, CH)], a=KB)
                    load(n + 1 + 3 * c, (n + 1) % RING, wu[:, :, bass.ds((c + 1) * CH, CH)], a=KB)
                    load(n + 2 + 3 * c, (n + 2) % RING, wd[:, bass.ds(2 * c, 2), :], a=2)
                n = first + 3 * GC - 1
                load(n, n % RING, wd[:, 2 * GC - 2:2 * GC, :], a=2)

            x_v = d["x"][0].rearrange("(t p) c -> p t c", p=P)
            for tb in range(TB):
                sp.dma_start(x[:, tb, :], x_v[:, tb, :]).then_inc(x_loaded[tb], 16)
            for n in range(RING):
                load_static(n)
            sp.dma_start(gb_row, d["ab_gate_b"][0].partition_broadcast(P)).then_inc(ab_small, 16)
            sp.dma_start(ws_raw[:, :, :], d["ab_ws"][0].rearrange("g t s -> t g s")).then_inc(ws_loaded, 16)
            for name in VEC:
                if name != "ab_norm":
                    load_vec(sp, name).then_inc(vecs_loaded, 16)
            for n in range(RING, RING + 3):
                load_static(n)
            sp.dma_start(vg_row, d["ab_v_g"][0].partition_broadcast(P)).then_inc(vg_loaded, 16)
            sp.dma_start(pos_i[:, :], d["positions"][0].rearrange("(t p) -> p t", p=P),
                         allow_slow_non_contiguous=True).then_inc(pos_loaded, 16)
            sp.dma_start(rel_t[:, :], d["rel_bias_2"][0]).then_inc(rel_loaded, 16)
            for n in range(RING + 3, P_FFN0):
                load_static(n)
            ffn(P_FFN0, d["ffn_w1"][0], d["ffn_w2"][0])
            for n in range(P_CIN, P_FFN1):
                load_static(n)
            ffn(P_FFN1, d["ffn_w1"][1], d["ffn_w2"][1])
            for n in range(P_V2, P_GLU):
                load_static(n)
            glu(P_GLU)
            out_v = out[0].rearrange("(t p) c -> p t c", p=P)
            for tb in range(TB):
                for half in range(2):
                    cs = slice(half * 512, (half + 1) * 512)
                    sp.wait_ge(x_ready, X_AT["out"] + 2 * tb + half + 1)
                    sp.dma_start(out_v[:, tb, cs], x[:, tb, cs]).then_inc(x_stored, 16)
            sp.wait_ge(x_stored, 16 * 2 * TB)

        @block.gpsimd
        def _(pool):
            steps = [0]

            def step(ins):
                steps[0] += 1
                ins.then_inc(pool_step, 1)
                pool.wait_ge(pool_step, steps[0])

            step(pool.memset(ones[:, :], 1.0))
            step(pool.memset(ident[:, :], 0.0))
            pool.affine_select(out=ident[:, :], in_=ident[:, :], compare_op=ALU.not_equal, fill=1.0, base=0,
                               pattern=[[-1, P]], channel_multiplier=1).then_inc(ident_ready, 1)
            step(pool.memset(mhalf[:, :], -0.5))
            step(pool.memset(mone[:, :], -1.0))

            def rms(name):
                c0, n, w = JOBS[name]
                if name in SS_ACT:
                    pool.wait_ge(ss_act, SS_ACT.index(name) + 1)
                else:
                    pool.wait_ge(ss_dve, SS_DVE.index(name) + 1)
                step(pool.tensor_scalar(msq[:, c0:c0 + n], ssq[:, c0:c0 + n], 1.0 / w, EPS, ALU.mult, ALU.add))
                power = mone[:, :] if name in SQUARED else mhalf[:, 0:n]
                pool.tensor_tensor(rstd[:, c0:c0 + n], msq[:, c0:c0 + n], power, ALU.pow)\
                    .then_inc(rstd_ready, 1)

            rms("ab0")
            rms("ab1")
            step(pool.memset(mask[:, :, :], 0.0))
            pool.affine_select(out=mask[:, 0, :], in_=mask[:, 0, :], compare_op=ALU.is_ge, fill=NEG, base=0,
                               pattern=[[1, P]], channel_multiplier=-1).then_inc(consts_ready, 1)
            pool.affine_select(out=mask[:, 1, :], in_=mask[:, 1, :], compare_op=ALU.is_ge, fill=NEG, base=0,
                               pattern=[[-1, P]], channel_multiplier=1).then_inc(consts_ready, 1)
            for i in range(HALF):
                ins = pool.memset(freq[:, i:i + 1], float(np.float32(10000.0) ** np.float32(-i / HALF)))
            ins.then_inc(consts_ready, 1)
            rms("vb")
            rms("ha")
            pool.wait_ge(rel_built, 1)
            pool.dma_start(rel_dram.ap(), rel_ext[:, :].unsqueeze(1).to_broadcast([H2, P, EXT])).then_inc(rel_stored, 16)
            for name in ("ffn00", "ffn01", "c0", "c1", "cq0", "ckv0", "cq1", "ckv1"):
                rms(name)
            pool.wait_ge(krT_ready, 1)
            pool.tensor_copy(kfT[C_NOPE:C_QK, 0:C_H, :],
                             krT[C_NOPE:C_QK, :].unsqueeze(1).to_broadcast([C_ROPE, C_H, S])).then_inc(kfT_rope, 1)
            for name in ("ffn10", "ffn11", "fin0", "fin1", "pre0", "pre1"):
                if name == "ffn10":
                    pool.wait_ge(at_pv[0], C_H)
                    pool.wait_ge(rel_stored, 16)
                    pool.dma_start(bias2[:, :, :], bass.AP(rel_dram, P - 1, [[EXT - 1, P], [P * EXT, H2], [1, S]]))\
                        .then_inc(bias_loaded, 16)
                    pool.dma_start(fin_row, d["final_norm"].partition_broadcast(P)).then_inc(rows2_loaded, 16)
                    pool.dma_start(pm_row, d["g_post_mix_2"][0].partition_broadcast(P)).then_inc(rows2_loaded, 16)
                    pool.dma_start(pf_row, d["g_post_ffn_2"][0].partition_broadcast(P)).then_inc(rows2_loaded, 16)
                    pool.wait_ge(bias_loaded, 16)
                    pool.memset(bias2[0:CHUNK, :, P + CHUNK:S], NEG).then_inc(bias_ready, 1)
                rms(name)
            for name in ("pm0", "pm1", "glu0", "glu1", "pf0", "pf1"):
                rms(name)

        @block.scalar
        def _(act):
            steps = [0]

            def step(ins):
                steps[0] += 1
                ins.then_inc(act_step, 1)
                act.wait_ge(act_step, steps[0])

            def hi(n):
                if n >= PIECES:
                    return
                act.wait_ge(arrived[n % RING], 16 * (n // RING + 1))
                if n >= RING:
                    act.wait_ge(piece_used, n - RING + 1)
                for dst, src in zip(views(n, w_hi, False), views(n, raw, True)):
                    ins = act.activation(dst, src, ACT.Copy)
                ins.then_inc(hi_ready, 1)

            def hi_quarter(n, c):
                if c == 0:
                    act.wait_ge(arrived[n % RING], 16 * (n // RING + 1))
                    act.wait_ge(piece_used, n - RING + 1)
                cs = slice(c * PIECE // 4, (c + 1) * PIECE // 4)
                ins = act.activation(w_hi[:, n % RING, cs], raw[:, n % RING, cs], ACT.Copy)
                if c == 3:
                    ins.then_inc(hi_ready, 1)

            def hi_loop(n0, i):
                slot = n0 % RING
                act.wait_ge(arrived[slot], 16 * (n0 // RING + 1) + 32 * i)
                act.wait_ge(piece_used, n0 - RING + 1 + 6 * i)
                act.activation(w_hi[:, slot, :], raw[:, slot, :], ACT.Copy).then_inc(hi_ready, 1)

            def turn(t, *part_of):
                part_of = part_of or (None,)
                for at, q in list(enumerate(PAIRS[t]))[slice(*part_of)]:
                    act.wait_ge(turned, turned_base(t) + at + 1)
                    for k in range(2 * q, min(2 * q + 2, T_BLOCKS[t])):
                        g = gain(t, k)
                        ins = act.activation(h_hi[:, k, :], bank(4 + q)[:, (k % 2) * S:(k % 2 + 1) * S], ACT.Copy,
                                             scale=1.0 if g is None else g)
                    ins.then_inc(h_hi_ready, 1)

            def mix_hi(t, q, pv, b):
                act.wait_ge(pv, 4 * q + 4)
                act.activation(mix_part(t, q, h_hi, g_hi), bank(b), ACT.Copy).then_inc(h_hi_ready, 1)

            sums = [0]

            def squares(src, c, scale=1.0):
                if sums[0]:
                    act.wait_ge(ss_act, sums[0])
                sums[0] += 1
                act.activation(junk[:, 0:src.shape[-1]], src, ACT.Square, scale=scale,
                               accum_out=ssq[:, c:c + 1]).then_inc(ss_act, 1)

            def squares_x(jobs, x_at):
                for tb in range(TB):
                    act.wait_ge(x_ready, x_at + 2 * tb + 2)
                    squares(x[:, tb, :], JOBS[jobs[tb]][0])

            def row_out(n, b):
                act.wait_ge(row_spread, n + 1)
                act.activation(r_row[:, :], bank(b)[:, 0:S], ACT.Copy).then_inc(row_ready, 1)

            def rs(name, i=0):
                c = JOBS[name][0] + i
                return rstd[:, c:c + 1]

            load_vec(act, "ab_norm").then_inc(norm_loaded, 16)
            act.dma_start(gw_raw[:, :, :], w_in[:, :, 4 * A_W:4 * A_W + 16]).then_inc(gw_loaded, 16)
            act.wait_ge(vecs_turned, 1)
            act.activation(cols[:, 0:KB], bank(0)[:, 0:KB], ACT.Copy).then_inc(cols_ready, 1)
            act.wait_ge(cols_ready, 1)
            turn(T_AB)
            act.wait_ge(arrived[0], 16)
            for c in range(2):
                cs = slice(c * PIECE // 2, (c + 1) * PIECE // 2)
                act.activation(w_hi[:, 0, cs], raw[:, 0, cs], ACT.Copy).then_inc((hi_half, hi_ready)[c], 1)
            act.wait_ge(gw_loaded, 16)
            act.activation(gw_hi[:, :, :], gw_raw[:, :, :], ACT.Copy).then_inc(gw_hi_ready, 1)
            for tb in range(TB):
                act.wait_ge(x_loaded[tb], 16)
                squares(x[:, tb, :], JOBS["ab0"][0] + tb)
            hi(1)
            hi(2)
            act.wait_ge(vecs_turned, 2)
            act.activation(wsT[:, :, :], bank(1).rearrange("p (g t) -> p g t", g=B_G), ACT.Copy)
            act.activation(cols[:, KB:], bank(3)[:, KB:VECS], ACT.Copy).then_inc(cols_ready, 1)
            row_out(0, 6)
            act.wait_ge(gate_abs, 1)
            step(act.activation(g_exp[:, :, :], g_abs[:, :, :], ACT.Exp, scale=-1.0))
            act.activation(g_ln[:, :, :], g_exp[:, :, :], ACT.Ln, bias=1.0).then_inc(gate_ln, 1)

            def silu(j):
                act.wait_ge(conv_done, j + 1)
                b0 = 2 * QK_ORDER[j]
                act.activation(qkT[:, b0:b0 + 2, :], qk_conv[:, b0:b0 + 2, :], ACT.Silu)\
                    .then_inc(silu_done, 1)

            for j in range(4):
                hi(P_QK + j + RING)
            act.wait_ge(rstd_ready, JOB_AT["ab1"] + 1)
            hi(P_VA + RING)
            silu(0)
            act.wait_ge(piece_used, P_VA + 2)
            for tb in range(TB):
                act.activation(v_ext[:, tb, :, 0:A_D], bank(4 + tb).rearrange("p (h e) -> p h e", h=A_H), ACT.Copy,
                               scale=rs(f"ab{tb}"))\
                    .then_inc(evac_v, 1)
            hi(P_VA + 1 + RING)
            act.wait_ge(cols_turned, 1)
            tc = bank(6)[:, 0:32].rearrange("p (q t e) -> p q t e", q=2, t=TB)
            act.activation(a_col[:, :, :], tc[:, 0], ACT.Copy).then_inc(gcols_ready, 1)
            act.activation(e_col[:, :, :], tc[:, 1], ACT.Exp, scale=-1.0).then_inc(gcols_ready, 1)
            act.wait_ge(gcols_ready, 2)
            silu(1)
            silu(2)
            hi(P_VB + RING)
            silu(3)
            act.wait_ge(piece_used, P_VB + 2)
            for tb in range(TB):
                act.activation(vb[:, tb, :], bank(tb), ACT.Gelu_apprx_tanh, scale=rs(f"ab{tb}"))\
                    .then_inc(evac_vb, 1)

            def decay_of(u):
                h, back = u // 2, u % 2
                act.wait_ge(spread, u + 1)
                if u >= 2:
                    act.wait_ge(g_ready, u - 1)
                b = bank(u % 2)
                dst = decay[:, u % 2, :, :].rearrange("p b t -> p (b t)")
                at = back * A_H + h
                for s0, (c0, c1) in enumerate([((0, 256), (384, 512)), ((0, 128), (256, 512))][back]):
                    ins = act.activation(dst[:, c0:c1], b[:, c0:c1], ACT.Exp, bias=a_col[:, s0, at:at + 1])
                ins.then_inc(w_ready, 1)

            decay_of(0)
            decay_of(1)
            hi(P_VB + 1 + RING)
            decay_of(2)
            hi(P_U + RING)
            decay_of(3)
            decay_of(4)
            act.wait_ge(piece_used, P_U + 2)
            for tb in range(TB):
                act.activation(u_act[:, tb, :], bank(6 + tb), ACT.Gelu_apprx_tanh, scale=rs(f"ab{tb}"))\
                    .then_inc(evac_u, 1)
            decay_of(5)
            hi(P_U + 1 + RING)
            for u in range(6, 2 * A_H):
                decay_of(u)
            hi(P_OA + RING)
            act.wait_ge(piece_used, P_OA + 2)
            for tb in range(TB):
                act.activation(oa[:, tb, :], bank(6 + tb), ACT.Sigmoid, scale=rs(f"ab{tb}")).then_inc(evac_oa, 1)
            turn(T_AMIX, 0, 2)
            hi(P_OA + 1 + RING)
            hi(P_AOUT + RING)
            turn(T_AMIX, 2, 4)
            for j in range(1, 3):
                hi(P_AOUT + j + RING)
            act.wait_ge(trig_in, 1)
            act.activation(trig[:, :, :, :], ang2[:, :, :, :], ACT.Sin).then_inc(trig_ready, 1)

            def ffn(first, hb, t, jobs, x_at):
                turn(t)
                hi(first + RING - 1)
                squares_x(jobs, x_at)

                def hidden(c, r, n_w1):
                    act.wait_ge(piece_used, n_w1 + 1)
                    if not (isinstance(c, int) and c < 3):
                        act.wait_ge(g_lo_ready, hb + c - 2)
                    act.activation(g_act[:, r, :], bank(4 + r), ACT.Relu).then_inc(act_out, 1)
                    act.wait_ge(act_out, hb + c + 1)
                    act.activation(g_hi[:, r, :], g_act[:, r, :], ACT.Square).then_inc(g_hi_ready, 1)

                hidden(0, 0, first)
                hi(first + RING)

                def chunk(c, j, i):
                    n = first + 1 + 2 * j
                    hidden(c + 1, (j + 1) % 3, n + 6 * i)
                    if isinstance(i, int):
                        hi(n + 6 * i + RING)
                        hi(n + 6 * i + 1 + RING)
                    else:
                        hi_loop(n + RING, i)
                        hi_loop(n + 1 + RING, i)

                for j in range(3):
                    chunk(j, j, 0)
                with act.Fori(1, (FC - 1) // 3) as i:
                    for j in range(3):
                        chunk(3 * i + j, j, i)

            ffn(P_FFN0, 0, T_FFN0, ("ffn00", "ffn01"), X_AT["ffn0"])

            turn(T_C)
            hi(P_CIN + RING - 1)
            squares_x(("c0", "c1"), X_AT["c"])
            act.wait_ge(rstd_ready, JOB_AT["c1"] + 1)
            for j in range(2):
                hi(P_CIN + j + RING)
            for tb in range(TB):
                if tb == 0:
                    act.wait_ge(cin_half, 1)
                else:
                    act.wait_ge(piece_used, P_CIN + 3)
                for name, c0, w in (("cq", 0, Q_LORA), ("ckv", Q_LORA, KV_LORA)):
                    squares(bank(2 * tb, 2)[:, c0:c0 + w], JOBS[f"{name}{tb}"][0], rs(f"c{tb}"))
            turn(T_LAT)
            hi(P_CIN + 2 + RING)
            for j in range(3):
                act.wait_ge(piece_used, P_UQ + j + 1)
                for tb in range(TB):
                    ins = act.activation(q_tok[:, tb, j * 512:(j + 1) * 512], bank(2 * j + tb), ACT.Copy,
                                         scale=float(C_QK) ** -0.5)
                ins.then_inc(evac_q, 1)
                if j == 0:
                    act.wait_ge(krr_turned, 1)
                    act.activation(krT[C_NOPE:C_QK, :], psum[C_NOPE:C_QK, 7, 0:S], ACT.Copy).then_inc(krT_ready, 1)
                hi(P_UQ + j + RING)
            for j in range(2):
                act.wait_ge(piece_used, P_UKV + j + 1)
                act.activation(kfT[0:C_NOPE, 8 * j:8 * j + 8:2, :],
                               bank((6, 2)[j], 2)[0:C_NOPE, :].rearrange("p (h t) -> p h t", h=4), ACT.Copy)\
                    .then_inc(evac_k, 1)
            act.wait_ge(evac_q, 3)
            for half in range(TB):
                ins = act.activation(v_tok[:, half, 512:], bank(4 + half), ACT.Copy)
            ins.then_inc(evac_vc1, 1)
            for n in range(1, 8, 2):
                act.wait_ge(qf_turned, n + 1)
                act.activation(qfT[0:C_QK, 2 * n:2 * n + 2, :],
                               bank(QF_BANKS[n])[0:C_QK, :].rearrange("p (h t) -> p h t", h=2), ACT.Copy)\
                    .then_inc(qf_ready, 1)
            def exp_c(h):
                act.wait_ge(at_max[0], h + 1)
                if h >= 3:
                    act.wait_ge(at_pt[0], h - 2)
                for qb in range(2):
                    ins = act.activation(prob[:, h % 3, qb * S:(qb + 1) * S], bank(h % 2)[:, qb * S:(qb + 1) * S],
                                         ACT.Exp, bias=nmax[:, qb, h:h + 1], accum_out=psm[:, qb, h:h + 1])
                ins.then_inc(at_exp[0], 1)

            def copy_pc(h):
                act.wait_ge(at_pt[0], h + 1)
                if h >= 2:
                    act.wait_ge(at_pv[0], h - 1)
                act.activation(probT[:, h % 2, :], bank(2 + h % 2), ACT.Copy).then_inc(at_ptsb[0], 1)

            for i in range(C_H + 2):
                if i < C_H:
                    exp_c(i)
                if i >= 2:
                    copy_pc(i - 2)
                if 2 <= i < 10:
                    hi_quarter(P_COUT + 1 + (i - 2) // 4, (i - 2) % 4)
                if i % 4 == 3 and i >= 7:
                    mix_hi(T_CMIX, (i - 7) // 4, at_pv[0], 4 + (i - 7) // 4)
            mix_hi(T_CMIX, 3, at_pv[0], 7)
            for j in range(3):
                hi(P_COUT + j + RING)
            ffn(P_FFN1, FC, T_FFN1, ("ffn10", "ffn11"), X_AT["ffn1"])

            turn(T_2)
            hi(P_V2 + RING - 1)
            squares_x(("fin0", "fin1"), X_AT["fin"])
            hi(P_V2 + RING)
            squares_x(("pre0", "pre1"), X_AT["pre"])
            row_out(1, 5)
            for n in range(2):
                act.wait_ge(piece_used, P_V2 + 2 * n + 2)
                act.wait_ge(r_both_ready, 1)
                for tb in range(TB):
                    act.activation(v2[:, tb, n * 512:(n + 1) * 512], bank(2 * n + tb), ACT.Copy,
                                   scale=r_both[:, tb:tb + 1]).then_inc(evac_v2, 1)
                hi(P_V2 + 2 * n + 1 + RING)
                if n == 0:
                    hi(P_V2 + 2 + RING)

            def copy_pt(h):
                act.wait_ge(at_pt[1], h + 1)
                if h >= 2:
                    act.wait_ge(at_pv[1], h - 1)
                act.activation(probT2[:, h % 2, :], bank(4 + h % 2)[:, 0:3 * P], ACT.Copy).then_inc(at_ptsb[1], 1)

            def exp2(h):
                act.wait_ge(at_max[1], h + 1)
                if h >= 3:
                    act.wait_ge(at_pt[1], h - 2)
                for qb, (c0, c1) in enumerate(((0, P), (P, 3 * P))):
                    ins = act.activation(prob2[:, h % 3, c0:c1], s2[:, h % 2, c0:c1], ACT.Exp, scale=-1.0,
                                         bias=nmax2[:, qb, h:h + 1], accum_out=psm2[:, qb, h:h + 1])
                ins.then_inc(at_exp[1], 1)

            for j in range(8):
                for h in (2 * j - 4, 2 * j - 3):
                    if h >= 0:
                        exp2(h)
                    if h >= 2:
                        copy_pt(h - 2)
                if j in (5, 7):
                    mix_hi(T_2MIX, (j - 5) // 2, at_pv[1], OUT2[(j - 5) // 2])
                if j < 7:
                    hi(P_QK2 + j + RING)
            for h in range(12, H2 + 2):
                if h < H2:
                    exp2(h)
                copy_pt(h - 2)
                if h == 15:
                    mix_hi(T_2MIX, 2, at_pv[1], OUT2[2])
            mix_hi(T_2MIX, 3, at_pv[1], OUT2[3])
            for j in range(-1, 3):
                hi(P_O2 + j + RING)

            def squares_acc(stage, last, jobs, pre):
                for tb in range(TB):
                    if tb == 0:
                        act.wait_ge(acc_half, stage + 1)
                    else:
                        act.wait_ge(piece_used, last + 1)
                    squares(bank(2 * tb, 2), JOBS[jobs[tb]][0], pre[tb])

            squares_acc(4, P_O2 + 3, ("pm0", "pm1"), (1.0, 1.0))
            turn(T_GLU)
            hi(P_GLU + RING - 1)
            squares_x(("glu0", "glu1"), X_AT["glu"])
            row_out(2, 0)
            hb, first = 2 * FC, P_GLU

            def silu_glu(c, r):
                act.wait_ge(gate_scaled, c + 1)
                act.activation(g_act[:, r, :], g_act[:, r, :], ACT.Silu).then_inc(act_out, 1)

            def glu_hi(c, r):
                act.wait_ge(mul_out, hb + c + 1)
                act.activation(g_hi[:, r, :], g_mul[:, r, :], ACT.Copy).then_inc(g_hi_ready, 1)

            silu_glu(0, 0)
            hi(first + RING)
            glu_hi(0, 0)
            hi(first + 1 + RING)

            def glu_chunk(c, j, i):
                n = first + 2 + 3 * j
                silu_glu(c + 1, (j + 1) % 2)
                ahead = hi if isinstance(i, int) else hi_loop
                a = (lambda k: (n + 6 * i + k + RING,)) if isinstance(i, int) else (lambda k: (n + k + RING, i))
                ahead(*a(0))
                glu_hi(c + 1, (j + 1) % 2)
                ahead(*a(1))
                ahead(*a(2))

            for j in range(2):
                glu_chunk(j, j, 0)
            with act.Fori(1, (GC - 1) // 2 - 1) as i:
                for j in range(2):
                    glu_chunk(2 * i + j, j, i)
            i = (GC - 1) // 2 - 1
            for j in range(2):
                glu_chunk(2 * i + j, j, i)
            squares_acc(5, PIECES - 1, ("pf0", "pf1"), (rs("glu0"), rs("glu1")))

        @block.vector
        def _(dve):
            steps = [0]

            def step(ins):
                steps[0] += 1
                ins.then_inc(dve_step, 1)
                dve.wait_ge(dve_step, steps[0])

            def lo(n):
                if n >= PIECES:
                    return
                dve.wait_ge(hi_ready, n + 1)
                for dst, src, high in zip(views(n, w_lo, False), views(n, raw, True), views(n, w_hi, False)):
                    ins = dve.tensor_tensor(dst, src, high, ALU.subtract)
                ins.then_inc(lo_ready, 1)

            def lo_quarter(n, c):
                if c == 0:
                    dve.wait_ge(hi_ready, n + 1)
                cs = slice(c * PIECE // 4, (c + 1) * PIECE // 4)
                ins = dve.tensor_tensor(w_lo[:, n % RING, cs], raw[:, n % RING, cs], w_hi[:, n % RING, cs],
                                        ALU.subtract)
                if c == 3:
                    ins.then_inc(lo_ready, 1)

            def lo_loop(n0, i):
                slot = n0 % RING
                dve.wait_ge(hi_ready, n0 + 1 + 6 * i)
                dve.tensor_tensor(w_lo[:, slot, :], raw[:, slot, :], w_hi[:, slot, :], ALU.subtract)\
                    .then_inc(lo_ready, 1)

            def turn(t, *part_of):
                part_of = part_of or (None,)
                for at, q in list(enumerate(PAIRS[t]))[slice(*part_of)]:
                    dve.wait_ge(h_hi_ready, t_base(t) + at + 1)
                    for k in range(2 * q, min(2 * q + 2, T_BLOCKS[t])):
                        g = gain(t, k)
                        ins = dve.scalar_tensor_tensor(
                            out=h_lo[:, k, :], in0=bank(4 + q)[:, (k % 2) * S:(k % 2 + 1) * S],
                            scalar=1.0 if g is None else g, in1=h_hi[:, k, :], op0=ALU.mult, op1=ALU.subtract)
                    ins.then_inc(h_lo_ready, 1)

            def rs(name, i=0):
                c = JOBS[name][0] + i
                return rstd[:, c:c + 1]

            def rs_wait(name):
                dve.wait_ge(rstd_ready, JOB_AT[name] + 1)

            def acc_wait(stage, last, tb):
                if tb == 0:
                    dve.wait_ge(acc_half, stage + 1)
                else:
                    dve.wait_ge(piece_used, last + 1)

            def residual(stage, last, jobs=None):
                for tb in range(TB):
                    if jobs:
                        rs_wait(jobs[tb])
                    acc_wait(stage, last, tb)
                    for half in range(2):
                        xh = x[:, tb, half * 512:(half + 1) * 512]
                        dve.scalar_tensor_tensor(out=xh, in0=bank(2 * tb + half), scalar=rs(jobs[tb]) if jobs else 1.0,
                                                 in1=xh, op0=ALU.mult, op1=ALU.add).then_inc(x_ready, 1)

            def diagonal(cols_of_r):
                for tb in range(TB):
                    dve.tensor_scalar(diag[:, tb, :], ident[:, :], cols_of_r[tb], None, ALU.mult)\
                        .then_inc(diag_ready, 1)

            step(dve.memset(qk_pad[:, :, 0:PAD], 0.0))
            step(dve.memset(qk_pad[:, :, PAD + S:], 0.0))
            step(dve.memset(v_ext[:, :, :, A_D:A_D + 1], 1.0))
            step(dve.memset(ones_row[0:A_H, :], 1.0))
            dve.wait_ge(cols_ready, 1)
            turn(T_AB)
            for c in range(2):
                cs = slice(c * PIECE // 2, (c + 1) * PIECE // 2)
                dve.wait_ge((hi_half, hi_ready)[c], 1)
                dve.tensor_tensor(w_lo[:, 0, cs], raw[:, 0, cs], w_hi[:, 0, cs], ALU.subtract)\
                    .then_inc((lo_half, lo_ready)[c], 1)
            dve.wait_ge(gw_hi_ready, 1)
            dve.tensor_tensor(gw_lo[:, :, :], gw_raw[:, :, :], gw_hi[:, :, :], ALU.subtract).then_inc(gw_ready, 1)
            dve.wait_ge(ident_ready, 1)
            rs_wait("ab1")
            diagonal([rs("ab0"), rs("ab1")])
            lo(1)
            lo(2)
            dve.wait_ge(gates_done, 1)
            dve.wait_ge(ab_small, 16)
            for tb in range(TB):
                ins = dve.scalar_tensor_tensor(out=gates[:, 2 * tb:2 * tb + 2, :],
                                               in0=bank(7)[:, 16 * tb:16 * tb + 16].rearrange("p (a b) -> p a b", a=2),
                                               scalar=rs(f"ab{tb}"), in1=gb_row.rearrange("p (a b) -> p a b", a=2),
                                               op0=ALU.mult, op1=ALU.add)
            step(ins)
            fg = gates[:, :, A_H:2 * A_H]
            dve.scalar_tensor_tensor(out=g_abs[:, :, :], in0=fg, scalar=-1.0, in1=fg, op0=ALU.mult, op1=ALU.max)\
                .then_inc(gate_abs, 1)

            dve.wait_ge(cols_ready, 2)
            dve.tensor_tensor(gain2[:, :], cols[:, VEC["final_norm"]:VEC["final_norm"] + KB],
                              cols[:, VEC["g_pre_mix_2"]:VEC["g_pre_mix_2"] + KB], ALU.mult)
            step(dve.tensor_scalar(nsel[0:A_H, :, :],
                                   ident[0:A_H, 0:A_H].unsqueeze(2).to_broadcast([A_H, A_H, P]), -1.0, None, ALU.mult))
            dve.wait_ge(gate_ln, 1)
            dve.scalar_tensor_tensor(out=fg, in0=fg, scalar=0.0, in1=g_ln[:, :, :], op0=ALU.min, op1=ALU.subtract)\
                .then_inc(gates_ready, 1)
            dve.wait_ge(row_ready, 1)

            def qk_out(j):
                dve.wait_ge(piece_used, P_QK + j + 1)
                b0 = 2 * QK_ORDER[j]
                dve.tensor_tensor(qk_pad[:, b0:b0 + 2, PAD:PAD + S],
                                  bank(QK_ORDER[j]).rearrange("p (b t) -> p b t", b=2),
                                  r_row[:, :].unsqueeze(1).to_broadcast([P, 2, S]), ALU.mult).then_inc(evac_qk, 1)
                dve.wait_ge(evac_qk, j + 1)

            def conv(j):
                b0 = 2 * QK_ORDER[j]
                for t in range(TAPS):
                    for b in (b0, b0 + 1):
                        dst, src, w = qk_conv[:, b, :], qk_pad[:, b, t:t + S], col("ab_conv", 8 * t + b)
                        if t == 0:
                            ins = dve.tensor_scalar(dst, src, w, None, ALU.mult)
                        else:
                            ins = dve.scalar_tensor_tensor(out=dst, in0=src, scalar=w, in1=dst,
                                                           op0=ALU.mult, op1=ALU.add)
                        if t < TAPS - 1:
                            steps[0] += 1
                            ins.then_inc(dve_step, 1)
                            dve.wait_ge(dve_step, steps[0] - (b == b0))
                        elif b == b0:
                            step(ins)
                ins.then_inc(conv_done, 1)

            qk_out(0)
            lo(3)
            conv(0)
            qk_out(1)
            lo(4)
            dve.wait_ge(rows_turned, 1)
            rows = bank(6, 2)[0:A_H, :].rearrange("p (d q t) -> p d q t", d=2, q=2)
            one = ones_row[0:A_H, :]
            step(dve.tensor_tensor_scan(cumf[0:A_H, 0, :], one, rows[:, 0, 1, :], 0.0, ALU.mult, ALU.add))
            step(dve.tensor_tensor_scan(cumf[0:A_H, 1, ::-1], one, rows[:, 1, 1, ::-1], 0.0, ALU.mult, ALU.add))
            step(dve.tensor_tensor(a_row[0:A_H, :, :], rows[:, :, 0, :], cumf[0:A_H, :, :], ALU.subtract))
            step(dve.tensor_tensor_scan(m_row[0:A_H, 0, :], a_row[0:A_H, 0, :], a_row[0:A_H, 0, :], 0.0,
                                        ALU.max, ALU.max))
            step(dve.tensor_tensor_scan(m_row[0:A_H, 1, ::-1], a_row[0:A_H, 1, ::-1], a_row[0:A_H, 1, ::-1], 0.0,
                                        ALU.max, ALU.max))
            dve.tensor_tensor(mt_row[0:A_H, :, :], cumf[0:A_H, :, :], m_row[0:A_H, :, :], ALU.add)\
                .then_inc(rows_ready, 1)
            qk_out(2)
            lo(5)
            conv(1)
            qk_out(3)
            lo(6)
            conv(2)
            lo(7)
            lo(8)
            conv(3)
            lo(9)
            dve.wait_ge(evac_vb, 2)
            groups = vb[:, :, :].rearrange("p t (g c) -> p (t g) c", g=B_G)
            sq_g = sq_tmp[:, :, :].rearrange("p t (g c) -> p (t g) c", g=B_G)
            step(dve.tensor_tensor(sq_g, groups, groups, ALU.mult))
            c0 = JOBS["vb"][0]
            dve.tensor_reduce(ssq[:, c0:c0 + 8], sq_g, AX.X, ALU.add).then_inc(ss_dve, 1)

            def weigh(u):
                h, back = u // 2, u % 2
                dve.wait_ge(w_ready, u + 1)
                dve.wait_ge(s_ready, h + 1)
                src = bank(2 + h % 2)
                w = decay[:, u % 2, :, :].rearrange("p b t -> p (b t)")
                dst = score[:, u % 2, :, :].rearrange("p b t -> p (b t)")
                for c0, c1 in [((0, 256), (384, 512)), ((0, 128), (256, 512))][back]:
                    ins = dve.scalar_tensor_tensor(out=dst[:, c0:c1], in0=src[:, c0:c1], scalar=float(A_D) ** -0.5,
                                                   in1=w[:, c0:c1], op0=ALU.mult, op1=ALU.mult)
                ins.then_inc(g_ready, 1)

            def unit_out(u):
                h, back = u // 2, u % 2
                dve.wait_ge(o_ready, u + 1)
                o = bank(4 + u % 2)[:, 0:2 * (A_D + 1)].rearrange("p (t e) -> p t e", t=TB)
                at = back * A_H + h
                den = o[:, :, A_D]
                step(dve.tensor_tensor(dmax, den, e_col[:, :, at], ALU.max))
                step(dve.scalar_tensor_tensor(out=dmax, in0=den, scalar=-1.0, in1=dmax, op0=ALU.mult, op1=ALU.max))
                step(dve.reciprocal(dinv, dmax))
                for tb in range(TB):
                    dst = hsum[:, tb, h * A_D:(h + 1) * A_D]
                    if back:
                        ins = dve.scalar_tensor_tensor(out=dst, in0=o[:, tb, 0:A_D], scalar=dinv[:, tb:tb + 1],
                                                       in1=dst, op0=ALU.mult, op1=ALU.add)
                    else:
                        ins = dve.tensor_scalar(dst, o[:, tb, 0:A_D], dinv[:, tb:tb + 1], None, ALU.mult)
                    if tb == 0:
                        step(ins)
                ins.then_inc(unit_done, 1)
                dve.wait_ge(unit_done, u + 1)

            dve.wait_ge(gcols_ready, 2)
            for u in range(2 * A_H):
                weigh(u)
                if u == 1:
                    lo(P_VB + 1 + RING)
                if u == 2:
                    rs_wait("vb")
                    dve.wait_ge(vg_loaded, 16)
                    step(dve.tensor_tensor(groups, groups,
                                           rstd[:, c0:c0 + 8].unsqueeze(2).to_broadcast([P, 8, 128]), ALU.mult))
                    dve.tensor_tensor(vb[:, :, :], vb[:, :, :], vg_row.unsqueeze(1).to_broadcast([P, TB, B_W]),
                                      ALU.mult).then_inc(vbn_ready, 1)
                if u == 5:
                    dve.wait_ge(evac_u, 2)
                    for g in range(B_G):
                        dve.wait_ge(sgu_done, g // 2 + 1)
                        ins = dve.scalar_tensor_tensor(
                            out=xn[:, :, A_W + g * 128:A_W + (g + 1) * 128],
                            in0=bank(6, 2)[:, g * S:(g + 1) * S].rearrange("p (n c) -> p n c", n=TB),
                            scalar=col("ab_bs", g), in1=u_act[:, :, g * 128:(g + 1) * 128], op0=ALU.add, op1=ALU.mult)
                        if g % 2:
                            ins.then_inc(sgu_read, 1)
                if u >= 1:
                    unit_out(u - 1)
                if u == 2:
                    lo(P_U + RING)
                if u == 5:
                    lo(P_U + 1 + RING)
            lo(P_OA + RING)
            unit_out(2 * A_H - 1)
            heads = hsum[:, :, :].rearrange("p t (g c) -> p (t g) c", g=A_H)
            step(dve.tensor_tensor(sq_g, heads, heads, ALU.mult))
            c1 = JOBS["ha"][0]
            dve.tensor_reduce(ssq[:, c1:c1 + 8], sq_g, AX.X, ALU.add).then_inc(ss_dve, 1)
            turn(T_AMIX, 0, 2)
            rs_wait("ha")
            step(dve.tensor_tensor(heads, heads, rstd[:, c1:c1 + 8].unsqueeze(2).to_broadcast([P, 8, 128]), ALU.mult))
            dve.wait_ge(evac_oa, 2)
            for tb in range(TB):
                dve.tensor_tensor(xn[:, tb, 0:A_W], hsum[:, tb, :], oa[:, tb, :], ALU.mult).then_inc(xn_ready, 1)
            lo(P_OA + 1 + RING)
            lo(P_AOUT + RING)
            turn(T_AMIX, 2, 4)
            dve.wait_ge(rel_loaded, 16)
            n0 = P
            n1 = n0 + N_REL - 1
            step(dve.tensor_copy(rel_ext[:, 0:n0], rel_t[:, N_REL - 1:N_REL].to_broadcast([H2, n0])))
            step(dve.tensor_copy(rel_ext[:, n0:n1], rel_t[:, N_REL - 2::-1]))
            dve.tensor_copy(rel_ext[:, n1:EXT], rel_t[:, 0:1].to_broadcast([H2, EXT - n1])).then_inc(rel_built, 1)
            dve.wait_ge(pos_loaded, 16)
            dve.wait_ge(consts_ready, 3)
            step(dve.tensor_copy(pos_f[:, :], pos_i[:, :]))
            for tb in range(TB):
                step(dve.tensor_scalar(ang[:, tb, :], freq[:, :], pos_f[:, tb:tb + 1], None, ALU.mult))
            step(dve.tensor_scalar(turns[:, :, :], ang[:, :, :], 1.0 / TWO_PI, ROUND, ALU.mult, ALU.add))
            step(dve.tensor_scalar(turns[:, :, :], turns[:, :, :], -ROUND, None, ALU.add))
            for c in (PI_1, PI_2, PI_3):
                step(dve.scalar_tensor_tensor(out=ang[:, :, :], in0=turns[:, :, :], scalar=-c, in1=ang[:, :, :],
                                              op0=ALU.mult, op1=ALU.add))
            step(dve.tensor_scalar(ang2[:, 1, :, :], ang[:, :, :], PI_IN, -PI_IN, ALU.min, ALU.max))
            step(dve.tensor_scalar(ang[:, :, :], ang[:, :, :], math.pi / 2, None, ALU.add))
            step(dve.tensor_scalar(turns[:, :, :], ang[:, :, :], math.pi, -TWO_PI, ALU.is_gt, ALU.mult))
            step(dve.tensor_tensor(ang[:, :, :], ang[:, :, :], turns[:, :, :], ALU.add))
            dve.tensor_scalar(ang2[:, 0, :, :], ang[:, :, :], PI_IN, -PI_IN, ALU.min, ALU.max).then_inc(trig_in, 1)
            for j in range(1, 3):
                lo(P_AOUT + j + RING)
            residual(0, P_AOUT + 3)

            def ffn(first, hb, t, jobs, stage):
                turn(t)
                lo(first + RING - 1)

                def hidden(c, r):
                    dve.wait_ge(act_out, hb + c + 1)
                    dve.tensor_tensor(g_mul[:, r, :], g_act[:, r, :], g_act[:, r, :], ALU.mult).then_inc(mul_out, 1)
                    dve.wait_ge(mul_out, hb + c + 1)
                    dve.wait_ge(g_hi_ready, hb + c + 1)
                    dve.tensor_tensor(g_lo[:, r, :], g_mul[:, r, :], g_hi[:, r, :], ALU.subtract)\
                        .then_inc(g_lo_ready, 1)

                hidden(0, 0)
                lo(first + RING)

                def chunk(c, j, i):
                    n = first + 1 + 2 * j
                    hidden(c + 1, (j + 1) % 3)
                    if isinstance(i, int):
                        lo(n + 6 * i + RING)
                        lo(n + 6 * i + 1 + RING)
                    else:
                        lo_loop(n + RING, i)
                        lo_loop(n + 1 + RING, i)

                for j in range(3):
                    chunk(j, j, 0)
                with dve.Fori(1, (FC - 1) // 3) as i:
                    for j in range(3):
                        chunk(3 * i + j, j, i)
                residual(stage, first + 2 * FC - 1, jobs)

            ffn(P_FFN0, 0, T_FFN0, ("ffn00", "ffn01"), 1)

            dve.memset(krr[:, :, 0:C_NOPE], 0.0).then_inc(krr_zero, 1)
            turn(T_C)
            for j in range(-1, 2):
                lo(P_CIN + j + RING)

            def rope(first, second, out_lo, out_hi, cos, sin, t):
                dve.tensor_tensor(t[0], first, cos, ALU.mult)
                dve.tensor_tensor(t[1], second, sin, ALU.mult)
                dve.tensor_tensor(t[2], first, sin, ALU.mult)
                step(dve.tensor_tensor(t[3], second, cos, ALU.mult))
                dve.tensor_tensor(out_lo, t[0], t[1], ALU.subtract)
                return dve.tensor_tensor(out_hi, t[2], t[3], ALU.add)

            kr = psum[:, :, :].rearrange("p (t b) c -> p t (b c)", b=2)[:, 0:TB, Q_LORA + KV_LORA:C_IN]
            for tb in range(TB):
                rs_wait(f"ckv{tb}")
                for name, c0, w in (("cq", 0, Q_LORA), ("ckv", Q_LORA, KV_LORA)):
                    ins = dve.tensor_scalar(xn[:, tb, c0:c0 + w], bank(2 * tb, 2)[:, c0:c0 + w], rs(f"c{tb}"),
                                            rs(f"{name}{tb}"), ALU.mult, ALU.mult)
                ins.then_inc(xn_ready, 1)
                ins = dve.tensor_scalar(krs[:, tb, :], kr[:, tb, :], rs(f"c{tb}"), None, ALU.mult)
            step(ins)
            dve.wait_ge(trig_ready, 1)
            rope(krs[:, :, 0:HALF], krs[:, :, HALF:], krr[:, :, C_NOPE:C_NOPE + HALF], krr[:, :, C_NOPE + HALF:],
                 trig[:, 0], trig[:, 1], rk).then_inc(krr_ready, 1)
            turn(T_LAT)
            lo(P_CIN + 2 + RING)
            for j in range(2):
                lo(P_UQ + j + RING)
            dve.wait_ge(turned, turned_base(T_LAT) + 3)
            qv = q_tok[:, :, :].rearrange("p t (h e) -> p t h e", h=C_H)
            cs = [trig[:, i].unsqueeze(2).to_broadcast([P, TB, C_H, HALF]) for i in range(2)]
            dve.wait_ge(evac_q, 3)
            for tb in range(TB):
                rope(qv[:, tb, :, C_NOPE:C_NOPE + HALF], qv[:, tb, :, C_NOPE + HALF:],
                     qv[:, tb, :, C_NOPE:C_NOPE + HALF], qv[:, tb, :, C_NOPE + HALF:],
                     cs[0][:, tb], cs[1][:, tb], [t[:, tb] for t in rp]).then_inc(q_roped, 1)
            for j in range(2):
                if j == 0:
                    dve.wait_ge(piece_used, P_UKV + j + 1)
                    for half in range(TB):
                        ins = dve.tensor_copy(v_tok[:, half, j * 512:(j + 1) * 512], bank((0, 4)[j] + half))
                    ins.then_inc(evac_vc, 1)
                dve.wait_ge(evac_k, j + 1)
                dve.tensor_copy(kfT[0:C_NOPE, 8 * j + 1:8 * j + 8:2, :],
                                bank((6, 2)[j], 2)[C_NOPE:P, :].rearrange("p (h t) -> p h t", h=4)).then_inc(evac_k2, 1)
                if j == 0:
                    lo(P_UQ + 2 + RING)
            for n in range(0, 8, 2):
                dve.wait_ge(qf_turned, n + 1)
                dve.tensor_copy(qfT[0:C_QK, 2 * n:2 * n + 2, :],
                                bank(QF_BANKS[n])[0:C_QK, :].rearrange("p (h t) -> p h t", h=2))\
                    .then_inc(evac_k2, 1)

            def mix_lo(t, q, b):
                dve.wait_ge(h_hi_ready, t_base(t) + q + 1)
                dve.tensor_tensor(mix_part(t, q, h_lo, g_lo), bank(b), mix_part(t, q, h_hi, g_hi), ALU.subtract)\
                    .then_inc(h_lo_ready, 1)

            def head_max(h):
                dve.wait_ge(at_s[0], h + 1)
                dve.tensor_reduce(nmax[:, :, h], bank(h % 2).rearrange("p (q k) -> p q k", q=2), AX.X, ALU.max,
                                  negate=True).then_inc(at_max[0], 1)

            def normalise(h, layer, sums, inv, parts):
                dve.wait_ge(at_exp[layer], h + 1)
                step(dve.reciprocal(inv[:, :, h:h + 1], sums[:, :, h:h + 1]))
                for qb, part in enumerate(parts):
                    ins = dve.tensor_scalar(part, part, inv[:, qb, h:h + 1], None, ALU.mult)
                ins.then_inc(at_norm[layer], 1)

            for i in range(C_H + 1):
                if i < C_H:
                    head_max(i)
                if i >= 1:
                    h = i - 1
                    normalise(h, 0, psm, pinv, [prob[:, h % 3, qb * S:(qb + 1) * S] for qb in range(2)])
                if 7 <= i < 15:
                    lo_quarter(P_COUT + 1 + (i - 7) // 4, (i - 7) % 4)
                if i % 4 == 0 and i >= 8:
                    mix_lo(T_CMIX, (i - 8) // 4, 4 + (i - 8) // 4)
            mix_lo(T_CMIX, 3, 7)
            for j in range(3):
                lo(P_COUT + j + RING)
            residual(2, P_COUT + 3)
            ffn(P_FFN1, FC, T_FFN1, ("ffn10", "ffn11"), 3)

            turn(T_2)
            lo(P_V2 + RING - 1)
            dve.wait_ge(rows2_loaded, 48)
            for tb in range(TB):
                rs_wait(f"fin{tb}")
                for half in range(2):
                    cs = slice(half * 512, (half + 1) * 512)
                    dve.scalar_tensor_tensor(out=x[:, tb, cs], in0=x[:, tb, cs], scalar=rs(f"fin{tb}"),
                                             in1=fin_row[:, cs], op0=ALU.mult, op1=ALU.mult).then_inc(x_ready, 1)
            rs_wait("pre1")
            c0, c1 = JOBS["fin0"][0], JOBS["pre0"][0]
            dve.tensor_tensor(r_both[:, :], rstd[:, c0:c0 + TB], rstd[:, c1:c1 + TB], ALU.mult)\
                .then_inc(r_both_ready, 1)
            dve.wait_ge(r_both_ready, 1)
            diagonal([r_both[:, tb:tb + 1] for tb in range(TB)])
            for j in range(4):
                lo(P_V2 + j + RING)
            dve.wait_ge(bias_ready, 1)
            dve.wait_ge(row_ready, 2)

            def bias_max(h):
                dve.wait_ge(at_s[1], h + 1)
                if h >= 2:
                    dve.wait_ge(at_exp[1], h - 1)
                for qb, (c0, c1, k0) in enumerate(((0, P, P), (P, 3 * P, 0))):
                    ins = dve.tensor_tensor_reduce(s2[:, h % 2, c0:c1], bank(2 + h % 2)[:, c0:c1],
                                                   bias2[:, h, k0:S], -1.0, -NEG, ALU.add, ALU.min,
                                                   nmax2[:, qb, h:h + 1])
                ins.then_inc(at_max[1], 1)

            def normalise2(h):
                normalise(h, 1, psm2, pinv2, [prob2[:, h % 3, 0:P], prob2[:, h % 3, P:3 * P]])

            for j in range(8):
                if j >= 2:
                    bias_max(2 * j - 4)
                    if j > 2:
                        normalise2(2 * j - 5)
                dve.wait_ge(piece_used, P_QK2 + j + 1)
                dst = (kT2 if j % 2 else qT2)[:, 2 * (j // 2):2 * (j // 2) + 2, :]
                dve.scalar_tensor_tensor(out=dst, in0=bank(6 + j % 2).rearrange("p (b t) -> p b t", b=2),
                                         scalar=1.0 if j % 2 else float(HD2) ** -0.5,
                                         in1=r_row[:, :].unsqueeze(1).to_broadcast([P, 2, S]),
                                         op0=ALU.mult, op1=ALU.mult).then_inc(evac_qk2, 1)
                if j >= 2:
                    bias_max(2 * j - 3)
                    normalise2(2 * j - 4)
                if j in (5, 7):
                    mix_lo(T_2MIX, (j - 5) // 2, OUT2[(j - 5) // 2])
                if j < 7:
                    lo(P_QK2 + j + RING)
            for h in range(12, H2 + 1):
                if h < H2:
                    bias_max(h)
                normalise2(h - 1)
            mix_lo(T_2MIX, 2, OUT2[2])
            mix_lo(T_2MIX, 3, OUT2[3])
            for j in range(-1, 3):
                lo(P_O2 + j + RING)

            def post_norm(jobs, pre, row):
                for tb in range(TB):
                    dve.wait_ge(ss_act, SS_ACT.index(jobs[tb]) + 1)
                    step(dve.scalar_tensor_tensor(out=xn[:, tb, :], in0=bank(2 * tb, 2), scalar=pre[tb],
                                                  in1=row, op0=ALU.mult, op1=ALU.mult))
                    rs_wait(jobs[tb])
                    for half in range(2):
                        cs = slice(half * 512, (half + 1) * 512)
                        dve.scalar_tensor_tensor(out=x[:, tb, cs], in0=xn[:, tb, cs], scalar=rs(jobs[tb]),
                                                 in1=x[:, tb, cs], op0=ALU.mult, op1=ALU.add).then_inc(x_ready, 1)

            post_norm(("pm0", "pm1"), (1.0, 1.0), pm_row)
            turn(T_GLU)
            lo(P_GLU + RING - 1)
            rs_wait("glu1")
            diagonal([rs("glu0"), rs("glu1")])
            hb, first = 2 * FC, P_GLU

            def glu_scale(c, r, n_gate):
                dve.wait_ge(piece_used, n_gate + 1)
                dve.tensor_tensor(g_act[:, r, :].rearrange("p (f t) -> p f t", f=2),
                                  bank(4 + 2 * r).rearrange("p (f t) -> p f t", f=2),
                                  r_row[:, :].unsqueeze(1).to_broadcast([P, 2, S]), ALU.mult).then_inc(gate_scaled, 1)

            def glu_mul(c, r, n_up):
                dve.wait_ge(act_out, hb + c + 1)
                dve.wait_ge(piece_used, n_up + 1)
                dve.tensor_tensor(g_mul[:, r, :], g_act[:, r, :], bank(5 + 2 * r), ALU.mult).then_inc(mul_out, 1)

            def glu_lo(c, r):
                dve.wait_ge(g_hi_ready, hb + c + 1)
                dve.tensor_tensor(g_lo[:, r, :], g_mul[:, r, :], g_hi[:, r, :], ALU.subtract).then_inc(g_lo_ready, 1)

            dve.wait_ge(row_ready, 3)
            glu_scale(0, 0, first)
            lo(first + RING)
            glu_mul(0, 0, first + 1)
            glu_lo(0, 0)
            lo(first + 1 + RING)

            def glu_chunk(c, j, i):
                n = first + 2 + 3 * j
                r = (j + 1) % 2
                ahead = lo if isinstance(i, int) else lo_loop
                a = (lambda k: (n + 6 * i + k + RING,)) if isinstance(i, int) else (lambda k: (n + k + RING, i))
                glu_scale(c + 1, r, n + 6 * i)
                ahead(*a(0))
                glu_mul(c + 1, r, n + 1 + 6 * i)
                glu_lo(c + 1, r)
                ahead(*a(1))
                ahead(*a(2))

            for j in range(2):
                glu_chunk(j, j, 0)
            with dve.Fori(1, (GC - 1) // 2 - 1) as i:
                for j in range(2):
                    glu_chunk(2 * i + j, j, i)
            i = (GC - 1) // 2 - 1
            for j in range(2):
                glu_chunk(2 * i + j, j, i)
            post_norm(("pf0", "pf1"), (rs("glu0"), rs("glu1")), pf_row)

        @block.tensor
        def _(pe):
            def product(dst, stat, mov, first, last):
                pe.matmul(dst, stat[0], mov[0], start=first, stop=False)
                pe.matmul(dst, stat[0], mov[1], start=False, stop=False)
                return pe.matmul(dst, stat[1], mov[0], start=False, stop=last)

            def h_block(k, tb=None, t=None):
                if tb is None:
                    return h_hi[:, k, :], h_lo[:, k, :]
                if t == T_2MIX:
                    at = (k % 2) * S + tb * P
                    return [mix_part(t, k // 2, a, b)[:, at:at + P] for a, b in ((h_hi, g_hi), (h_lo, g_lo))]
                return h_hi[:, k, tb * P:(tb + 1) * P], h_lo[:, k, tb * P:(tb + 1) * P]

            def split(n):
                pe.wait_ge(lo_ready, n + 1)

            def turn(t, x_at=None, parts=None):
                n = T_BLOCKS[t]
                if x_at is not None:
                    parts = [(tb, 4 * g, 4 * g + 4, 2 * tb + g + 1) for tb in range(TB) for g in range(2)]
                elif parts is None:
                    parts = [(tb, 0, n, tb + 1) for tb in range(TB)]
                for tb, k0, k1, count in parts:
                    if t == T_AB:
                        pe.wait_ge(x_loaded[tb], 16)
                    elif x_at is not None:
                        pe.wait_ge(x_ready, x_at + count)
                    elif count is None:
                        pe.wait_ge(sgu_read, 2)
                    else:
                        pe.wait_ge(xn_ready, XN_AT[t] + count)
                    for k in range(k0, k1):
                        at = (k % 2) * S + tb * P
                        ins = pe.transpose(bank(4 + k // 2)[:, at:at + P],
                                           (x if x_at is not None else xn)[:, tb, k * P:(k + 1) * P], ident[:, :])
                        if tb == TB - 1 and (k % 2 or k == n - 1):
                            ins.then_inc(turned, 1)

            def h_wait(t, k):
                pe.wait_ge(h_lo_ready, t_base(t) + PAIRS[t].index(k // 2) + 1)

            def stationary_slice(slot, t, b, i, first_use=False):
                wh = w_hi[:, slot, :].rearrange("p (k c) -> p k c", k=KB)
                wl = w_lo[:, slot, :].rearrange("p (k c) -> p k c", k=KB)
                f = i // 2
                for k in range((i % 2) * KB // 2, (i % 2 + 1) * KB // 2):
                    if first_use and f == 0 and k % 2 == 0:
                        h_wait(t, k)
                    ins = product(bank(b)[:, f * S:(f + 1) * S],
                                  (wh[:, k, f * P:(f + 1) * P], wl[:, k, f * P:(f + 1) * P]),
                                  h_block(k), k == 0, k == KB - 1)
                if i == 3:
                    ins.then_inc(piece_used, 1)

            def stationary(slot, t, b, first_use=False):
                for i in range(4):
                    stationary_slice(slot, t, b, i, first_use)

            def moving_slice(first, j, banks, i, t=None):
                if i == 0:
                    split(first + j)
                wh, wl = part(w_hi, first + j, 4), part(w_lo, first + j, 4)
                tb = i // 2
                if t is not None and tb == 0:
                    h_wait(t, 4 * j + 2 * (i % 2))
                for k in (2 * (i % 2), 2 * (i % 2) + 1):
                    ins = product(bank(banks[tb]), h_block(4 * j + k, tb), (wh[:, k, :], wl[:, k, :]),
                                  j == 0 and k == 0, j == 1 and k == 3)
                if i == 3:
                    ins.then_inc(piece_used, 1)

            def moving(first, banks, t=None):
                for j in range(2):
                    for i in range(4):
                        moving_slice(first, j, banks, i, t)

            def out_piece(act_of, n_slot, first, last, between=None):
                wh = w_hi[:, n_slot, :].rearrange("p (k c) -> p k c", k=2)
                wl = w_lo[:, n_slot, :].rearrange("p (k c) -> p k c", k=2)
                for tb in range(TB):
                    for k in range(2):
                        for h in range(2):
                            ins = product(bank(2 * tb + h), act_of(k, tb),
                                          (wh[:, k, h * 512:(h + 1) * 512], wl[:, k, h * 512:(h + 1) * 512]),
                                          first and k == 0, last and k == 1)
                    if last and tb == 0:
                        ins.then_inc(acc_half, 1)
                    if between and tb == 0:
                        between()
                ins.then_inc(piece_used, 1)

            def out_product(first, t, js=range(4), between=None):
                for j in js:
                    k0 = 2 * PAIRS[t][j]
                    split(first + j)
                    h_wait(t, k0)
                    out_piece(lambda k, tb: h_block(k0 + k, tb, t), (first + j) % RING, j == 0, j == 3,
                              between if j == js[-1] else None)

            def spread_row(n, b):
                pe.wait_ge(diag_ready, 2 * n + 2)
                for tb in range(TB):
                    ins = pe.matmul(bank(b)[:, tb * P:(tb + 1) * P], ones[:, :], diag[:, tb, :], start=True, stop=True)
                ins.then_inc(row_spread, 1)

            pe.wait_ge(ident_ready, 1)
            pe.wait_ge(norm_loaded, 16)
            pe.transpose(bank(0)[:, 0:KB], vecs[0:KB, :], ident[0:KB, 0:KB]).then_inc(vecs_turned, 1)
            turn(T_AB, 0)
            pe.wait_ge(cols_ready, 1)
            for i in range(4):
                if i == 0:
                    pe.wait_ge(lo_half, 1)
                if i == 1:
                    split(P_QK)
                stationary_slice(P_QK % RING, T_AB, 0, i, True)
            pe.wait_ge(gw_ready, 1)
            for tb in range(TB):
                for k in range(KB):
                    ins = product(bank(7)[:, 16 * tb:16 * tb + 16], h_block(k, tb), (gw_hi[:, k, :], gw_lo[:, k, :]),
                                  k == 0, k == KB - 1)
            ins.then_inc(gates_done, 1)
            spread_row(0, 6)
            pe.wait_ge(ws_loaded, 16)
            for g in range(B_G):
                pe.transpose(bank(1)[:, g * P:(g + 1) * P], ws_raw[:, g, :], ident[:, :])
            pe.wait_ge(vecs_loaded, 16 * (len(VEC) - 1))
            pe.transpose(bank(3)[:, 0:VECS], vecs[:, :], ident[0:VECS, 0:VECS]).then_inc(vecs_turned, 1)
            split(P_QK + 1)
            stationary((P_QK + 1) % RING, T_AB, QK_ORDER[1])
            split(P_QK + 2)
            pe.wait_ge(cols_ready, 2)
            stationary((P_QK + 2) % RING, T_AB, QK_ORDER[2])
            pe.wait_ge(gates_ready, 1)
            pe.wait_ge(row_ready, 1)
            for dq in range(4):
                for tb in range(TB):
                    at = dq * S + tb * P
                    src = gates[:, 2 * tb + dq // 2, (dq % 2) * A_H:(dq % 2 + 1) * A_H]
                    ins = pe.transpose(bank(6, 2)[0:A_H, at:at + P], src, ident[:, :])
            ins.then_inc(rows_turned, 1)
            split(P_QK + 3)
            stationary((P_QK + 3) % RING, T_AB, QK_ORDER[3])
            moving(P_VA, (4, 5))
            pe.wait_ge(rows_ready, 1)
            for q, rows in enumerate((a_row, mt_row)):
                for tb in range(TB):
                    for back in range(2):
                        at = 16 * q + 8 * tb + A_H * back
                        ins = pe.transpose(bank(6)[:, at:at + A_H], rows[0:A_H, back, tb * P:(tb + 1) * P],
                                           ident[0:A_H, 0:A_H])
            ins.then_inc(cols_turned, 1)
            pe.wait_ge(evac_qk, 3)
            moving(P_VB, (0, 1))

            def spread_m(u):
                h, back = u // 2, u % 2
                if u == 0:
                    pe.wait_ge(evac_vb, 2)
                    pe.wait_ge(consts_ready, 3)
                if u >= 2:
                    pe.wait_ge(w_ready, u - 1)
                b = bank(u % 2)
                whole, half = (((0, 256), (384, 512)), ((256, 512), (0, 128)))[back]
                m = m_row[0:A_H, back, :]
                msk = mask[:, back, :]
                pe.matmul(b[:, whole[0]:whole[1]], nsel[0:A_H, h, :], m, start=True, stop=False)
                wd = whole[0] + (P if back else 0)
                pe.matmul(b[:, wd:wd + P], ident[:, :], msk, start=False, stop=True)
                pe.matmul(b[:, half[0]:half[1]], nsel[0:A_H, h, :], m[:, P:S] if not back else m[:, 0:P],
                          start=True, stop=False)
                pe.matmul(b[:, half[0]:half[1]], ident[:, :], msk, start=False, stop=True).then_inc(spread, 1)

            def head_scores(h):
                if h == 0:
                    pe.wait_ge(silu_done, 2)
                    pe.wait_ge(evac_qk, 4)
                if h == 2:
                    pe.wait_ge(silu_done, 4)
                if h >= 2:
                    pe.wait_ge(g_ready, 2 * h - 2)
                for s0 in range(2):
                    ins = pe.matmul(bank(2 + h % 2)[:, s0 * S:(s0 + 1) * S], qkT[:, 4 + h, s0 * P:(s0 + 1) * P],
                                    qkT[:, h, :], start=True, stop=True)
                ins.then_inc(s_ready, 1)

            def unit_pv(u):
                h, back = u // 2, u % 2
                if u == 0:
                    pe.wait_ge(evac_v, 2)
                pe.wait_ge(g_ready, u + 1)
                if u >= 2:
                    pe.wait_ge(unit_done, u - 1)
                for t0, sources in enumerate([((0,), (0, 1)), ((0, 1), (1,))][back]):
                    for s0 in sources:
                        ins = pe.matmul(bank(4 + u % 2)[:, t0 * (A_D + 1):(t0 + 1) * (A_D + 1)],
                                        score[:, u % 2, 2 * s0 + t0, :], v_ext[:, s0, h, :],
                                        start=s0 == sources[0], stop=s0 == sources[-1])
                ins.then_inc(o_ready, 1)

            def unit_step(u):
                if u + 2 < 2 * A_H:
                    spread_m(u + 2)
                if u % 2 == 1 and u // 2 + 1 < A_H:
                    head_scores(u // 2 + 1)
                unit_pv(u)

            def sgu_mix():
                pe.wait_ge(vbn_ready, 1)
                pe.wait_ge(evac_u, 2)
                for g in range(B_G):
                    ins = pe.matmul(bank(6, 2)[:, g * S:(g + 1) * S].rearrange("p (n c) -> p n c", n=TB),
                                    wsT[:, g, :], vb[:, :, g * 128:(g + 1) * 128], start=True, stop=True)
                    if g % 2:
                        ins.then_inc(sgu_done, 1)

            pe.wait_ge(gcols_ready, 2)
            for j in range(2):
                for i in range(4):
                    moving_slice(P_U, j, (6, 7), i)
                    if j == 0 and i == 0:
                        head_scores(0)
                    if j == 0 and i == 1:
                        spread_m(0)
                        spread_m(1)
                    if j == 0 and i >= 2:
                        unit_step(i - 2)
                    if j == 1 and i % 2:
                        unit_step(2 + i // 2)
            unit_step(4)
            sgu_mix()
            for j in range(2):
                for i in range(4):
                    if j == 0 and i % 2 == 0:
                        pe.wait_ge(sgu_read, i // 2 + 1)
                    moving_slice(P_OA, j, (6, 7), i)
                    if 2 * j + i // 2 < 3 and i % 2:
                        unit_step(5 + 2 * j + i // 2)
            pe.wait_ge(evac_oa, 2)
            turn(T_AMIX, parts=[(0, 4, 8, None), (1, 4, 8, None)])
            def turn_heads():
                pe.wait_ge(unit_done, 2 * A_H)
                turn(T_AMIX, parts=[(0, 0, 4, 1), (1, 0, 4, 2)])

            out_product(P_AOUT, T_AMIX, range(2), turn_heads)
            out_product(P_AOUT, T_AMIX, range(2, 4))

            def ffn(first, hb, t, x_at):
                turn(t, x_at)
                split(first)
                stationary(first % RING, t, 4, True)

                def chunk(c, j, i):
                    n = first + 1 + 2 * j
                    r1 = (j + 1) % 3
                    split(n + 6 * i)
                    if not (isinstance(c, int) and c < 2):
                        pe.wait_ge(act_out, hb + c - 1)
                    stationary(n % RING, t, 4 + r1)
                    split(n + 1 + 6 * i)
                    pe.wait_ge(g_lo_ready, hb + c + 1)
                    down(j % 3, (n + 1) % RING, isinstance(c, int) and c == 0, False)

                def down(r, slot, start, stop):
                    out_piece(lambda k, tb: (g_hi[:, r, k * S + tb * P:k * S + (tb + 1) * P],
                                             g_lo[:, r, k * S + tb * P:k * S + (tb + 1) * P]), slot, start, stop)

                for j in range(3):
                    chunk(j, j, 0)
                with pe.Fori(1, (FC - 1) // 3) as i:
                    for j in range(3):
                        chunk(3 * i + j, j, i)
                n = first + 2 * FC - 1
                split(n)
                pe.wait_ge(g_lo_ready, hb + FC)
                down((FC - 1) % 3, n % RING, False, True)

            ffn(P_FFN0, 0, T_FFN0, X_AT["ffn0"])

            turn(T_C, X_AT["c"])
            for j, (k0, k1) in enumerate(((0, 3), (3, 6), (6, 8))):
                n = P_CIN + j
                split(n)
                wh, wl = part(w_hi, n, k1 - k0), part(w_lo, n, k1 - k0)
                for tb in range(TB):
                    for k in range(k0, k1):
                        if tb == 0:
                            h_wait(T_C, k)
                        for c0, c1 in ((0, 512), (512, C_IN)):
                            ins = product(bank(2 * tb, 2)[:, c0:c1], h_block(k, tb),
                                          (wh[:, k - k0, c0:c1], wl[:, k - k0, c0:c1]), k == 0, k == KB - 1)
                    if j == 2 and tb == 0:
                        ins.then_inc(cin_half, 1)
                ins.then_inc(piece_used, 1)
            turn(T_LAT)
            for j in range(3):
                n = P_UQ + j
                split(n)
                wh, wl = part(w_hi, n, 3), part(w_lo, n, 3)
                for tb in range(TB):
                    for k in range(3):
                        if j == 0 and tb == 0:
                            h_wait(T_LAT, k)
                        ins = product(bank(2 * j + tb), h_block(k, tb), (wh[:, k, :], wl[:, k, :]), k == 0, k == 2)
                ins.then_inc(piece_used, 1)
                if j == 0:
                    pe.wait_ge(krr_ready, 1)
                    pe.wait_ge(krr_zero, 1)
                    for tb in range(TB):
                        ins = pe.transpose(psum[0:C_QK, 7, tb * P:(tb + 1) * P], krr[:, tb, :], ident[:, :])
                    ins.then_inc(krr_turned, 1)
            h_wait(T_LAT, 4)
            pe.wait_ge(krT_ready, 1)
            for j in range(2):
                n = P_UKV + j
                split(n)
                wh, wl = part(w_hi, n, 2), part(w_lo, n, 2)
                pe.wait_ge(evac_q, j + 1)
                for pair in range(4):
                    hs = slice(pair * P, (pair + 1) * P)
                    for k in range(2):
                        product(bank((6, 2)[j], 2)[:, pair * S:(pair + 1) * S],
                                (wh[:, k, hs], wl[:, k, hs]), h_block(3 + k), k == 0, k == 1)
                if j == 1:
                    pe.wait_ge(evac_q, 3)
                for tb in range(TB):
                    for k in range(2):
                        ins = product(bank((0, 4)[j] + tb), h_block(3 + k, tb), (wh[:, k, 512:], wl[:, k, 512:]),
                                      k == 0, k == 1)
                ins.then_inc(piece_used, 1)
            pe.wait_ge(q_roped, 2)
            pe.wait_ge(evac_k2, 1)
            pe.wait_ge(evac_vc, 1)

            def qf_wait(n):
                if n % 2:
                    pe.wait_ge(qf_ready, n // 2 + 1)
                else:
                    pe.wait_ge(evac_k2, 2 + n // 2 + 1)

            for n in range(8):
                if n in (4, 5):
                    qf_wait(n - 4)
                if n == 6:
                    pe.wait_ge(evac_k2, 2)
                for i in range(2):
                    h = 2 * n + i
                    for tb in range(TB):
                        at = i * S + tb * P
                        ins = pe.transpose(bank(QF_BANKS[n])[0:C_QK, at:at + P],
                                           q_tok[:, tb, h * C_QK:(h + 1) * C_QK], ident[:, :])
                ins.then_inc(qf_turned, 1)
            pe.wait_ge(kfT_rope, 1)

            def c_scores(h):
                if h < 2:
                    qf_wait(2 + h)
                if h % 2 == 0:
                    qf_wait(h // 2)
                if h >= 2:
                    pe.wait_ge(at_exp[0], h - 1)
                for qb in range(2):
                    ins = pe.matmul(bank(h % 2)[:, qb * S:(qb + 1) * S], qfT[0:C_QK, h, qb * P:(qb + 1) * P],
                                    kfT[0:C_QK, h, :], start=True, stop=True)
                ins.then_inc(at_s[0], 1)

            def c_turn(h):
                pe.wait_ge(at_norm[0], h + 1)
                if h == 0:
                    qf_wait(6)
                    qf_wait(7)
                if h >= 2:
                    pe.wait_ge(at_ptsb[0], h - 1)
                for kb in range(2):
                    for qb in range(2):
                        at = kb * S + qb * P
                        ins = pe.transpose(bank(2 + h % 2)[:, at:at + P],
                                           prob[:, h % 3, qb * S + kb * P:qb * S + (kb + 1) * P], ident[:, :])
                ins.then_inc(at_pt[0], 1)

            def c_pv(h):
                pe.wait_ge(at_ptsb[0], h + 1)
                if h == 0:
                    pe.wait_ge(evac_vc1, 1)
                rows, c0 = slice(C_V * (h % 2), C_V * (h % 2 + 1)), (h // 2 % 2) * S
                for kb in range(2):
                    ins = pe.matmul(psum[rows, 4 + h // 4, c0:c0 + S], v_tok[:, kb, h * C_V:(h + 1) * C_V],
                                    probT[:, h % 2, kb * S:(kb + 1) * S], start=kb == 0, stop=kb == 1)
                ins.then_inc(at_pv[0], 1)

            def pipeline(n, *stages):
                for i in range(n + len(stages) - 1):
                    for lag, stage in enumerate(stages):
                        if stage and 0 <= i - lag < n:
                            stage(i - lag)

            pipeline(C_H, c_scores, None, c_turn, c_pv)
            out_product(P_COUT, T_CMIX)
            ffn(P_FFN1, FC, T_FFN1, X_AT["ffn1"])

            turn(T_2, X_AT["fin"])
            moving(P_V2, (0, 1), T_2)
            moving_slice(P_V2 + 2, 0, (2, 3), 0)
            spread_row(1, 5)
            for i in range(1, 4):
                moving_slice(P_V2 + 2, 0, (2, 3), i)
            for i in range(4):
                moving_slice(P_V2 + 2, 1, (2, 3), i)

            def scores2(h):
                if h % 4 == 0:
                    pe.wait_ge(evac_qk2, h // 2 + 2)
                if h == 0:
                    pe.wait_ge(evac_v2, 4)
                if h >= 2:
                    pe.wait_ge(at_max[1], h - 1)
                rows = slice(HD2 * (h % 2), HD2 * (h % 2 + 1))
                for qb, (c0, c1) in enumerate(((0, P), (P, 3 * P))):
                    ins = pe.matmul(bank(2 + h % 2)[:, c0:c1], qT2[rows, h // 2, qb * P:(qb + 1) * P],
                                    kT2[rows, h // 2, 0:c1 - c0], start=True, stop=True)
                ins.then_inc(at_s[1], 1)

            def turn2(h):
                pe.wait_ge(at_norm[1], h + 1)
                if h >= 2:
                    pe.wait_ge(at_ptsb[1], h - 1)
                for b in range(3):
                    ins = pe.transpose(bank(4 + h % 2)[:, b * P:(b + 1) * P], prob2[:, h % 3, b * P:(b + 1) * P],
                                       ident[:, :])
                ins.then_inc(at_pt[1], 1)

            def pv2(h):
                pe.wait_ge(at_ptsb[1], h + 1)
                if h >= 8 and h % 4 == 0:
                    pe.wait_ge(evac_qk2, 7 + (h - 8) // 4)
                rows, c0 = slice(HD2 * (h % 2), HD2 * (h % 2 + 1)), (h // 2 % 2) * S
                out_h = psum[rows, OUT2[h // 4], c0:c0 + S]
                pe.matmul(out_h, v2[:, 0, h * HD2:(h + 1) * HD2], probT2[:, h % 2, 0:S], start=True, stop=False)
                pe.matmul(out_h[:, P:S], v2[:, 1, h * HD2:(h + 1) * HD2], probT2[:, h % 2, S:3 * P],
                          start=False, stop=True).then_inc(at_pv[1], 1)

            def step2(i):
                if i < H2:
                    scores2(i)
                if 0 <= i - 2 < H2:
                    turn2(i - 2)
                if 0 <= i - 3 < H2:
                    pv2(i - 3)

            for j in range(8):
                split(P_QK2 + j)
                if j >= 2:
                    pe.wait_ge(evac_qk2, j - 1)
                for i in range(4):
                    stationary_slice((P_QK2 + j) % RING, T_2, 6 + j % 2, i)
                    if j >= 2 and i % 2:
                        step2(2 * (j - 2) + i // 2)
            for i in range(12, H2 + 3):
                step2(i)
            out_product(P_O2, T_2MIX)

            turn(T_GLU, X_AT["glu"])
            hb, first = 2 * FC, P_GLU

            def gate_up(c, r, n0, i):
                split(n0 + 6 * i)
                if not (isinstance(c, int) and c < 2):
                    pe.wait_ge(gate_scaled, c - 1)
                stationary(n0 % RING, T_GLU, 4 + 2 * r, isinstance(c, int) and c == 0)
                split(n0 + 1 + 6 * i)
                if isinstance(c, int) and c == 0:
                    stationary_slice((n0 + 1) % RING, T_GLU, 5, 0)
                    spread_row(2, 0)
                    for q in range(1, 4):
                        stationary_slice((n0 + 1) % RING, T_GLU, 5, q)
                    return
                if not (isinstance(c, int) and c < 2):
                    pe.wait_ge(mul_out, hb + c - 1)
                stationary((n0 + 1) % RING, T_GLU, 5 + 2 * r)

            def glu_down(c, r, n0, i, start, stop):
                split(n0 + 6 * i)
                pe.wait_ge(g_lo_ready, hb + c + 1)
                out_piece(lambda k, tb: (g_hi[:, r, k * S + tb * P:k * S + (tb + 1) * P],
                                         g_lo[:, r, k * S + tb * P:k * S + (tb + 1) * P]), n0 % RING, start, stop)

            gate_up(0, 0, first, 0)

            def glu_chunk(c, j, i):
                n = first + 2 + 3 * j
                gate_up(c + 1, (j + 1) % 2, n, i)
                glu_down(c, j % 2, n + 2, i, isinstance(c, int) and c == 0, False)

            for j in range(2):
                glu_chunk(j, j, 0)
            with pe.Fori(1, (GC - 1) // 2) as i:
                for j in range(2):
                    glu_chunk(2 * i + j, j, i)
            glu_down(GC - 1, (GC - 1) % 2, PIECES - 1, 0, False, True)


_INS = ["x", "positions", "ab_norm", "ab_w_in", "ab_conv", "ab_gate_b", "ab_head_g", "ab_v_g", "ab_ws", "ab_bs",
        "ab_w_out", "c_norm", "c_w_in", "c_q_g", "c_kv_g", "c_w_uq", "c_w_ukv", "c_w_out", "ffn_norm", "ffn_w1",
        "ffn_w2", "final_norm", "g_pre_mix_2", "g_post_mix_2", "w_qkv_2", "w_o_2", "rel_bias_2", "g_pre_ffn_2",
        "g_post_ffn_2", "w_gate_2", "w_up_2", "w_down_2"]


def kernel(**inputs):
    import numpy as _np
    import concourse.bacc as _bacc
    from concourse import mybir as _mybir
    from concourse.bass_utils import run_bass_kernel_spmd as _run

    nc = _bacc.Bacc("TRN2", target_bir_lowering=False, num_devices=1)
    arrays, d = {}, {}
    for name in _INS:
        a = _np.ascontiguousarray(inputs[name])
        arrays[f"in_{name}"] = a
        d[name] = nc.dram_tensor(f"in_{name}", a.shape, _mybir.dt.from_np(a.dtype), kind="ExternalInput").ap()
    out = nc.dram_tensor("out", (1, S, D), _mybir.dt.float32, kind="ExternalOutput").ap()
    build(nc, d, out)
    r = _run(nc, [arrays], core_ids=[0])
    return r.results[0]["out"]
```
